# Optimizing a Trainium2 kernel written in Bass

```python
import math
import jax, jax.numpy as jnp
from jax import lax
import numpy as np

D_MODEL = 1024
BATCH = 1
SEQ = 256
DEPTH = 2

GRID_W = 64
CTX_LEN = 256
N_MIXERS = 2
N_ATTN_LAYERS = (DEPTH + 1) // 2
N_HGRN_LAYERS = DEPTH // 2
EPS = 1e-6

HEAD_DIM = 64
N_HEADS = D_MODEL // HEAD_DIM
N_KV_HEADS = 4
GROUP = N_HEADS // N_KV_HEADS
WINDOW = 128
BLOCK = 128
ROPE_THETA = 10000.0
ATTN_IN_W = (N_HEADS + 2 * N_KV_HEADS) * HEAD_DIM

HG_EXPAND = 128
HG_HEADS = D_MODEL // HG_EXPAND
HG_DK = HG_EXPAND
HG_DV = D_MODEL // HG_HEADS
HG_DF = HG_HEADS * HG_DK
HG_CHUNK = 32
HG_SPLITS = [HG_DF, 2 * HG_DF, 3 * HG_DF, 3 * HG_DF + D_MODEL]
HG_IN_W = 3 * HG_DF + 2 * D_MODEL

D_FF = 2816
CONV_W = 3


def rms_norm(x, gain):
    xf = x.astype(jnp.float32)
    y = xf * lax.rsqrt(jnp.mean(xf * xf, axis=-1, keepdims=True) + EPS)
    return (y * gain.astype(jnp.float32)).astype(x.dtype)

def axial_angles(rows):
    row = jnp.repeat(jnp.arange(rows, dtype=jnp.float32), GRID_W)
    col = jnp.tile(jnp.arange(GRID_W, dtype=jnp.float32), rows)
    n_pairs = HEAD_DIM // 4
    inv = ROPE_THETA ** (-jnp.arange(n_pairs, dtype=jnp.float32) / n_pairs)
    return row[:, None] * inv, col[:, None] * inv

def rope_rotate(x, ang):
    x1, x2 = jnp.split(x, 2, axis=-1)
    cos = jnp.cos(ang)[None, :, None, :].astype(x.dtype)
    sin = jnp.sin(ang)[None, :, None, :].astype(x.dtype)
    return jnp.concatenate([x1 * cos - x2 * sin, x1 * sin + x2 * cos], axis=-1)

def apply_axial_rope(x, ang_r, ang_c):
    xr, xc = jnp.split(x, 2, axis=-1)
    return jnp.concatenate([rope_rotate(xr, ang_r), rope_rotate(xc, ang_c)], axis=-1)

def sink_softmax(scores, sink_g):
    s_sink = jnp.broadcast_to(sink_g[None, :, :, None, None].astype(jnp.float32), scores.shape[:-1] + (1,))
    p = jax.nn.softmax(jnp.concatenate([scores, s_sink], axis=-1), axis=-1)
    return p[..., :-1]

def attn_project(h, w_in, q_gain, k_gain):
    b, t, _ = h.shape
    q, k, v = jnp.split(h @ w_in, [N_HEADS * HEAD_DIM, (N_HEADS + N_KV_HEADS) * HEAD_DIM], axis=-1)
    q = rms_norm(q.reshape(b, t, N_HEADS, HEAD_DIM), q_gain)
    k = rms_norm(k.reshape(b, t, N_KV_HEADS, HEAD_DIM), k_gain)
    v = v.reshape(b, t, N_KV_HEADS, HEAD_DIM)
    return q, k, v

def windowed_gqa(hx, hc, w_in, w_out, q_gain, k_gain, sink, ang_r, ang_c, need_ctx_out):
    B, L, _ = hx.shape
    nb = L // BLOCK
    scale = HEAD_DIM ** -0.5
    qx, kx, vx = attn_project(hx, w_in, q_gain, k_gain)
    qc, kc, vc = attn_project(hc, w_in, q_gain, k_gain)
    qx = apply_axial_rope(qx, ang_r, ang_c)
    kx = apply_axial_rope(kx, ang_r, ang_c)
    kc_t = kc.transpose(0, 2, 1, 3)
    vc_t = vc.transpose(0, 2, 1, 3)
    pad = ((0, 0), (0, 0), (BLOCK, BLOCK), (0, 0))
    kx_p = jnp.pad(kx.transpose(0, 2, 1, 3), pad)
    vx_p = jnp.pad(vx.transpose(0, 2, 1, 3), pad)
    q_blocks = qx.reshape(B, nb, BLOCK, N_KV_HEADS, GROUP, HEAD_DIM).transpose(1, 0, 3, 4, 2, 5)
    sink_g = sink.reshape(N_KV_HEADS, GROUP)
    q_off = jnp.arange(BLOCK, dtype=jnp.int32)
    k_off = jnp.arange(3 * BLOCK, dtype=jnp.int32) - BLOCK

    def block(args):
        n, qb = args
        start = n * BLOCK
        kb = lax.dynamic_slice_in_dim(kx_p, start, 3 * BLOCK, axis=2)
        vb = lax.dynamic_slice_in_dim(vx_p, start, 3 * BLOCK, axis=2)
        qi = start + q_off
        kj = start + k_off
        valid = ((kj >= 0) & (kj < L))[None, :] & (jnp.abs(qi[:, None] - kj[None, :]) <= WINDOW)
        s_win = jnp.einsum('bkgqd,bkjd->bkgqj', qb, kb).astype(jnp.float32) * scale
        s_win = jnp.where(valid, s_win, -jnp.inf)
        s_ctx = jnp.einsum('bkgqd,bkcd->bkgqc', qb, kc_t).astype(jnp.float32) * scale
        p = sink_softmax(jnp.concatenate([s_win, s_ctx], axis=-1), sink_g).astype(vb.dtype)
        return (jnp.einsum('bkgqj,bkjd->bkgqd', p[..., :3 * BLOCK], vb)
                + jnp.einsum('bkgqc,bkcd->bkgqd', p[..., 3 * BLOCK:], vc_t))

    o = lax.map(block, (jnp.arange(nb, dtype=jnp.int32), q_blocks))
    ox = o.transpose(1, 0, 4, 2, 3, 5).reshape(B, L, N_HEADS * HEAD_DIM)
    yc = None
    if need_ctx_out:
        C = hc.shape[1]
        qcg = qc.reshape(B, C, N_KV_HEADS, GROUP, HEAD_DIM).transpose(0, 2, 3, 1, 4)
        s = jnp.einsum('bkgqd,bkcd->bkgqc', qcg, kc_t).astype(jnp.float32) * scale
        p = sink_softmax(s, sink_g).astype(vc.dtype)
        oc = jnp.einsum('bkgqc,bkcd->bkgqd', p, vc_t).transpose(0, 3, 1, 2, 4).reshape(B, C, N_HEADS * HEAD_DIM)
        yc = oc @ w_out
    return ox @ w_out, yc

def chunk_scan(q, k, g, v, s0, need_out):
    B, T, H, dk = q.shape
    dv = v.shape[-1]
    n = T // HG_CHUNK

    def to_chunks(a):
        return a.reshape(B, n, HG_CHUNK, H, a.shape[-1]).transpose(1, 0, 3, 2, 4).astype(jnp.float32)

    tri = jnp.tril(jnp.ones((HG_CHUNK, HG_CHUNK), dtype=bool))

    def step(S, inp):
        qc, kc, gc, vc = inp
        b = jnp.cumsum(gc, axis=2)
        b_last = b[:, :, -1:, :]
        k_dec = kc * jnp.exp(b_last - b)
        S_new = jnp.exp(b_last[:, :, 0, :])[..., None] * S + jnp.einsum('bhck,bhcv->bhkv', k_dec, vc)
        if not need_out:
            return S_new, None
        o_inter = jnp.einsum('bhck,bhkv->bhcv', qc * jnp.exp(b), S)
        diff = jnp.where(tri[:, :, None], b[:, :, :, None, :] - b[:, :, None, :, :], -jnp.inf)
        a = jnp.einsum('bhtk,bhsk,bhtsk->bhts', qc, kc, jnp.exp(diff))
        return S_new, o_inter + jnp.einsum('bhts,bhsv->bhtv', a, vc)

    S_fin, o = lax.scan(step, s0, (to_chunks(q), to_chunks(k), to_chunks(g), to_chunks(v)))
    if need_out:
        o = o.transpose(1, 0, 3, 2, 4).reshape(B, T, H, dv)
    return o, S_fin

def hgrn2_bidir(hx, hc, w_in, w_out, o_gain, lb, need_ctx_out):
    def project(h):
        b, t, _ = h.shape
        q, f_fw, f_bw, inp, gate = jnp.split(h @ w_in, HG_SPLITS, axis=-1)
        q = jax.nn.silu(q).reshape(b, t, HG_HEADS, HG_DK)
        inp = inp.reshape(b, t, HG_HEADS, HG_DV)

        def forget(fl):
            f = lb + (1.0 - lb) * jax.nn.sigmoid(fl.astype(jnp.float32))
            return (1.0 - f).reshape(b, t, HG_HEADS, HG_DK), jnp.log(f).reshape(b, t, HG_HEADS, HG_DK)

        return q, forget(f_fw), forget(f_bw), inp, gate

    flip = lambda a: jnp.flip(a, axis=1)
    qx, (kxf, gxf), (kxb, gxb), vx, gx = project(hx)
    qc, (kcf, gcf), (kcb, gcb), vc, gc = project(hc)
    s0 = jnp.zeros((hc.shape[0], HG_HEADS, HG_DK, HG_DV), jnp.float32)
    oc_f, sc_f = chunk_scan(qc, kcf, gcf, vc, s0, need_ctx_out)
    oc_b, sc_b = chunk_scan(flip(qc), flip(kcb), flip(gcb), flip(vc), s0, need_ctx_out)
    ox_f, _ = chunk_scan(qx, kxf, gxf, vx, sc_f, True)
    ox_b, _ = chunk_scan(flip(qx), flip(kxb), flip(gxb), flip(vx), sc_b, True)

    def readout(o, gate, h):
        o = rms_norm(o, o_gain).astype(h.dtype) * jax.nn.silu(gate).reshape(o.shape)
        return o.reshape(h.shape[0], h.shape[1], D_MODEL) @ w_out

    yx = readout(ox_f + flip(ox_b), gx, hx)
    yc = readout(oc_f + flip(oc_b), gc, hc) if need_ctx_out else None
    return yx, yc

def dwconv3(u, w, b):
    up = jnp.pad(u, ((0, 0), (1, 1), (0, 0)))
    return up[:, :-2] * w[0] + up[:, 1:-1] * w[1] + up[:, 2:] * w[2] + b

def conv_glu(h, w_up, conv_w, conv_b, w_down):
    gate, val = jnp.split(h @ w_up, 2, axis=-1)
    return (jax.nn.silu(dwconv3(gate, conv_w, conv_b)) * val) @ w_down

def first_inputs(seed: int = 0) -> dict:
    key = jax.random.key(seed)
    ks = jax.random.split(key, 21)
    D = D_MODEL

    def nrm(k, shape, scale):
        return jax.random.normal(k, shape, jnp.float32) * scale

    def gain(k, shape):
        return 1.0 + 0.05 * jax.random.normal(k, shape, jnp.float32)

    return {
        'x': nrm(ks[0], (BATCH, SEQ, D), 1.0),
        'c': nrm(ks[1], (BATCH, D), 1.0),
        'ctx': nrm(ks[2], (BATCH, CTX_LEN, D), 1.0),
        'c_ctx': nrm(ks[3], (D,), 1.0),
        'ada_w': nrm(ks[4], (DEPTH, D, 6 * D), 0.5 * D ** -0.5),
        'ada_b': nrm(ks[5], (DEPTH, 6 * D), 0.02),
        'norm1_g': gain(ks[6], (DEPTH, D)),
        'norm2_g': gain(ks[7], (DEPTH, D)),
        'attn_w_in': nrm(ks[8], (N_ATTN_LAYERS, D, ATTN_IN_W), D ** -0.5),
        'attn_w_out': nrm(ks[9], (N_ATTN_LAYERS, N_HEADS * HEAD_DIM, D), (N_HEADS * HEAD_DIM) ** -0.5),
        'attn_q_gain': gain(ks[10], (N_ATTN_LAYERS, HEAD_DIM)),
        'attn_k_gain': gain(ks[11], (N_ATTN_LAYERS, HEAD_DIM)),
        'attn_sink': nrm(ks[12], (N_ATTN_LAYERS, N_HEADS), 0.5),
        'hgrn_w_in': nrm(ks[13], (N_HGRN_LAYERS, D, HG_IN_W), D ** -0.5),
        'hgrn_w_out': nrm(ks[14], (N_HGRN_LAYERS, D, D), D ** -0.5),
        'hgrn_o_gain': gain(ks[15], (N_HGRN_LAYERS, HG_DV)),
        'hgrn_lb_logits': nrm(ks[16], (DEPTH, HG_DF), 0.5),
        'ffn_w_up': nrm(ks[17], (DEPTH, D, 2 * D_FF), D ** -0.5),
        'ffn_conv_w': nrm(ks[18], (DEPTH, CONV_W, D_FF), CONV_W ** -0.5),
        'ffn_conv_b': nrm(ks[19], (DEPTH, D_FF), 0.02),
        'ffn_w_down': nrm(ks[20], (DEPTH, D_FF, D), D_FF ** -0.5),
    }

def first_block(x, c, ctx, c_ctx, ada_w, ada_b, norm1_g, norm2_g, attn_w_in, attn_w_out, attn_q_gain,
              attn_k_gain, attn_sink, hgrn_w_in, hgrn_w_out, hgrn_o_gain, hgrn_lb_logits, ffn_w_up,
              ffn_conv_w, ffn_conv_b, ffn_w_down):
    L = x.shape[1]
    rows = L // GRID_W
    ang_r, ang_c = axial_angles(rows)
    lb_prob = jax.nn.softmax(hgrn_lb_logits.astype(jnp.float32), axis=0)
    lb_sched = jnp.cumsum(lb_prob, axis=0) - lb_prob[0]
    for layer in range(DEPTH):
        last = layer == DEPTH - 1
        j = layer // N_MIXERS
        mod = jax.nn.silu(c) @ ada_w[layer] + ada_b[layer]
        mod_c = jax.nn.silu(c_ctx) @ ada_w[layer] + ada_b[layer]
        sh1, sc1, g1, sh2, sc2, g2 = jnp.split(mod[:, None, :], 6, axis=-1)
        csh1, csc1, cg1, csh2, csc2, cg2 = jnp.split(mod_c, 6)
        hx = rms_norm(x, norm1_g[layer]) * (1.0 + sc1) + sh1
        hc = rms_norm(ctx, norm1_g[layer]) * (1.0 + csc1) + csh1
        if layer % N_MIXERS == 0:
            yx, yc = windowed_gqa(hx, hc, attn_w_in[j], attn_w_out[j], attn_q_gain[j], attn_k_gain[j],
                                  attn_sink[j], ang_r, ang_c, not last)
        else:
            yx, yc = hgrn2_bidir(hx, hc, hgrn_w_in[j], hgrn_w_out[j], hgrn_o_gain[j], lb_sched[layer], not last)
        x = x + g1 * yx
        hx2 = rms_norm(x, norm2_g[layer]) * (1.0 + sc2) + sh2
        x = x + g2 * conv_glu(hx2, ffn_w_up[layer], ffn_conv_w[layer], ffn_conv_b[layer], ffn_w_down[layer])
        if not last:
            ctx = ctx + cg1 * yc
            hc2 = rms_norm(ctx, norm2_g[layer]) * (1.0 + csc2) + csh2
            ctx = ctx + cg2 * conv_glu(hc2, ffn_w_up[layer], ffn_conv_w[layer], ffn_conv_b[layer], ffn_w_down[layer])
    return x


SWA_HEADS = 8
SWA_KV_HEADS = 2
SWA_HEAD_DIM = 64
SWA_WINDOW = 128
SWA_BLOCK = 128
GLA_HEADS = 4
GLA_DK = D_MODEL // 2 // GLA_HEADS
GLA_DV = D_MODEL // GLA_HEADS
GLA_GATE_RANK = 16
GLA_TAU = 16.0
GLA_CHUNK = 64

SWA_Q_W = SWA_HEADS * SWA_HEAD_DIM
SWA_KV_W = SWA_KV_HEADS * SWA_HEAD_DIM
GLA_K_W = GLA_HEADS * GLA_DK
GLA_V_W = GLA_HEADS * GLA_DV
IN_SPLITS = (SWA_Q_W, SWA_KV_W, SWA_KV_W, GLA_K_W, GLA_K_W, GLA_V_W, GLA_V_W, GLA_GATE_RANK, D_MODEL, D_MODEL)
IN_COLS = sum(IN_SPLITS)


def rmsnorm(x, g):
    xf = x.astype(jnp.float32)
    y = xf * lax.rsqrt(jnp.mean(xf * xf, axis=-1, keepdims=True) + EPS)
    return (y * g.astype(jnp.float32)).astype(x.dtype)

def swiglu(h, w_gate, w_up, w_down):
    return (jax.nn.silu(h @ w_gate) * (h @ w_up)) @ w_down

def split_cols(z, sizes):
    idx = np.cumsum(np.array(sizes))[:-1].tolist()
    return jnp.split(z, idx, axis=-1)

def rope_tables(T):
    inv_freq = ROPE_THETA ** (-jnp.arange(0, SWA_HEAD_DIM, 2, dtype=jnp.float32) / SWA_HEAD_DIM)
    ang = jnp.arange(T, dtype=jnp.float32)[:, None] * inv_freq[None, :]
    return jnp.cos(ang), jnp.sin(ang)

def apply_rope(x, cos, sin):
    x1, x2 = jnp.split(x, 2, axis=-1)
    c = cos[None, :, None, :]
    s = sin[None, :, None, :]
    return jnp.concatenate([x1 * c - x2 * s, x2 * c + x1 * s], axis=-1)

def swa_attention(q, k, v, q_gain, k_gain, sinks, cos, sin):
    B, T = q.shape[0], q.shape[1]
    G = SWA_HEADS // SWA_KV_HEADS
    nb = T // SWA_BLOCK
    q = apply_rope(rmsnorm(q, q_gain).astype(jnp.float32), cos, sin)
    k = apply_rope(rmsnorm(k, k_gain).astype(jnp.float32), cos, sin)
    v = v.astype(jnp.float32)
    q = q.reshape(B, nb, SWA_BLOCK, SWA_KV_HEADS, G, SWA_HEAD_DIM)
    k = k.reshape(B, nb, SWA_BLOCK, SWA_KV_HEADS, SWA_HEAD_DIM)
    v = v.reshape(B, nb, SWA_BLOCK, SWA_KV_HEADS, SWA_HEAD_DIM)

    def band(t):
        prev = jnp.pad(t[:, :-1], ((0, 0), (1, 0), (0, 0), (0, 0), (0, 0)))
        return jnp.concatenate([prev, t], axis=2)

    kb, vb = band(k), band(v)
    s = jnp.einsum('bnqhgd,bnkhd->bnhgqk', q, kb) * (SWA_HEAD_DIM ** -0.5)
    i = jnp.arange(SWA_BLOCK)[:, None]
    j = jnp.arange(2 * SWA_BLOCK)[None, :]
    rel = i + SWA_BLOCK - j
    blk = jnp.arange(nb)[:, None, None]
    valid = (rel >= 0) & (rel < SWA_WINDOW) & ((blk > 0) | (j >= SWA_BLOCK))
    s = jnp.where(valid[None, :, None, None], s, -jnp.inf)
    sink = sinks.astype(jnp.float32).reshape(1, 1, SWA_KV_HEADS, G, 1, 1)
    m = jnp.maximum(jnp.max(s, axis=-1, keepdims=True), sink)
    p = jnp.exp(s - m)
    denom = jnp.sum(p, axis=-1, keepdims=True) + jnp.exp(sink - m)
    o = jnp.einsum('bnhgqk,bnkhd->bnqhgd', p / denom, vb)
    return o.reshape(B, T, SWA_Q_W)

def gla_attention(q, k, v, log_a):
    B, T = q.shape[0], q.shape[1]
    nc = T // GLA_CHUNK

    def chunks(t, d):
        return t.astype(jnp.float32).reshape(B, nc, GLA_CHUNK, GLA_HEADS, d).transpose(1, 0, 3, 2, 4)

    qc = chunks(q, GLA_DK) * (GLA_DK ** -0.5)
    kc = chunks(k, GLA_DK)
    vc = chunks(v, GLA_DV)
    gc = chunks(log_a, GLA_DK)
    causal = jnp.tril(jnp.ones((GLA_CHUNK, GLA_CHUNK), dtype=bool))[:, :, None]

    def step(S, inp):
        qi, ki, vi, gi = inp
        b = jnp.cumsum(gi, axis=-2)
        b_last = b[:, :, -1:, :]
        o_inter = jnp.einsum('bhtc,bhcv->bhtv', qi * jnp.exp(b), S)
        diff = b[:, :, :, None, :] - b[:, :, None, :, :]
        decay = jnp.exp(jnp.where(causal, diff, -jnp.inf))
        attn = jnp.einsum('bhtsc,bhsc->bhts', qi[:, :, :, None, :] * decay, ki)
        o_intra = jnp.einsum('bhts,bhsv->bhtv', attn, vi)
        S = jnp.exp(b_last[:, :, 0, :])[..., None] * S + jnp.einsum('bhsc,bhsv->bhcv', ki * jnp.exp(b_last - b), vi)
        return S, o_inter + o_intra

    S0 = jnp.zeros((B, GLA_HEADS, GLA_DK, GLA_DV), jnp.float32)
    _, o = lax.scan(step, S0, (qc, kc, vc, gc))
    return o.transpose(1, 0, 3, 2, 4).reshape(B, T, GLA_HEADS, GLA_DV)

def second_inputs(seed: int = 0) -> dict:
    key = jax.random.key(seed)
    ks = jax.random.split(key, 24)
    L, D = DEPTH, D_MODEL

    def w(k, shape, fan_in):
        return jax.random.normal(k, shape, jnp.float32) * (fan_in ** -0.5)

    def gain(k, shape):
        return 1.0 + 0.02 * jax.random.normal(k, shape, jnp.float32)

    return {
        "x": jax.random.normal(ks[0], (BATCH, SEQ, D), jnp.float32),
        "ffn1_norm": gain(ks[1], (L, D)),
        "ffn1_w_gate": w(ks[2], (L, D, D_FF), D),
        "ffn1_w_up": w(ks[3], (L, D, D_FF), D),
        "ffn1_w_down": w(ks[4], (L, D_FF, D), D_FF),
        "mix_norm": gain(ks[5], (L, D)),
        "w_in": w(ks[6], (L, D, IN_COLS), D),
        "swa_q_norm": gain(ks[7], (L, SWA_HEAD_DIM)),
        "swa_k_norm": gain(ks[8], (L, SWA_HEAD_DIM)),
        "swa_sinks": 0.5 * jax.random.normal(ks[9], (L, SWA_HEADS), jnp.float32),
        "gla_w_gate": w(ks[10], (L, GLA_GATE_RANK, GLA_K_W), GLA_GATE_RANK),
        "gla_gate_bias": 0.1 * jax.random.normal(ks[11], (L, GLA_K_W), jnp.float32),
        "gla_out_norm": gain(ks[12], (L, GLA_V_W)),
        "w_proj_a": w(ks[13], (L, SWA_Q_W, D), SWA_Q_W),
        "w_proj_b": w(ks[14], (L, GLA_V_W, D), GLA_V_W),
        "w_out": w(ks[15], (L, D, D), D),
        "ffn2_norm": gain(ks[16], (L, D)),
        "ffn2_w_gate": w(ks[17], (L, D, D_FF), D),
        "ffn2_w_up": w(ks[18], (L, D, D_FF), D),
        "ffn2_w_down": w(ks[19], (L, D_FF, D), D_FF),
    }

def second_block(x, ffn1_norm, ffn1_w_gate, ffn1_w_up, ffn1_w_down, mix_norm, w_in,
              swa_q_norm, swa_k_norm, swa_sinks, gla_w_gate, gla_gate_bias, gla_out_norm,
              w_proj_a, w_proj_b, w_out, ffn2_norm, ffn2_w_gate, ffn2_w_up, ffn2_w_down):
    B, T = x.shape[0], x.shape[1]
    cos, sin = rope_tables(T)
    for l in range(DEPTH):
        h = rmsnorm(x, ffn1_norm[l])
        x = x + 0.5 * swiglu(h, ffn1_w_gate[l], ffn1_w_up[l], ffn1_w_down[l])

        h = rmsnorm(x, mix_norm[l])
        z = h @ w_in[l]
        q_a, k_a, v_a, q_b, k_b, v_b, r_b, g_lr, gate_a, gate_b = split_cols(z, IN_SPLITS)

        o_a = swa_attention(q_a.reshape(B, T, SWA_HEADS, SWA_HEAD_DIM),
                            k_a.reshape(B, T, SWA_KV_HEADS, SWA_HEAD_DIM),
                            v_a.reshape(B, T, SWA_KV_HEADS, SWA_HEAD_DIM),
                            swa_q_norm[l], swa_k_norm[l], swa_sinks[l], cos, sin).astype(x.dtype)

        log_a = jax.nn.log_sigmoid((g_lr @ gla_w_gate[l] + gla_gate_bias[l]).astype(jnp.float32)) / GLA_TAU
        o_b = gla_attention(q_b.reshape(B, T, GLA_HEADS, GLA_DK),
                            k_b.reshape(B, T, GLA_HEADS, GLA_DK),
                            v_b.reshape(B, T, GLA_HEADS, GLA_DV),
                            log_a.reshape(B, T, GLA_HEADS, GLA_DK))
        o_b = rmsnorm(o_b, gla_out_norm[l].reshape(GLA_HEADS, GLA_DV)).reshape(B, T, GLA_V_W).astype(x.dtype)
        o_b = o_b * jax.nn.silu(r_b)

        y_a = o_a @ w_proj_a[l]
        y_b = o_b @ w_proj_b[l]
        merged = jax.nn.sigmoid(gate_a) * y_a + jax.nn.sigmoid(gate_b) * y_b
        x = x + merged @ w_out[l]

        h = rmsnorm(x, ffn2_norm[l])
        x = x + 0.5 * swiglu(h, ffn2_w_gate[l], ffn2_w_up[l], ffn2_w_down[l])
    return x


def setup_inputs(seed=0):
    out = dict(first_inputs(seed))
    for name, value in second_inputs(seed + 1).items():
        if name != "x":
            out[name + "_2"] = value
    return out


def reference(
    x, c, ctx, c_ctx, ada_w, ada_b, norm1_g, norm2_g, attn_w_in, attn_w_out, attn_q_gain,
    attn_k_gain, attn_sink, hgrn_w_in, hgrn_w_out, hgrn_o_gain, hgrn_lb_logits, ffn_w_up,
    ffn_conv_w, ffn_conv_b, ffn_w_down, ffn1_norm_2, ffn1_w_gate_2, ffn1_w_up_2, ffn1_w_down_2,
    mix_norm_2, w_in_2, swa_q_norm_2, swa_k_norm_2, swa_sinks_2, gla_w_gate_2, gla_gate_bias_2,
    gla_out_norm_2, w_proj_a_2, w_proj_b_2, w_out_2, ffn2_norm_2, ffn2_w_gate_2, ffn2_w_up_2,
    ffn2_w_down_2,
):
    x = first_block(
        x, c, ctx, c_ctx, ada_w, ada_b, norm1_g, norm2_g, attn_w_in, attn_w_out, attn_q_gain,
        attn_k_gain, attn_sink, hgrn_w_in, hgrn_w_out, hgrn_o_gain, hgrn_lb_logits, ffn_w_up,
        ffn_conv_w, ffn_conv_b, ffn_w_down,
    )
    return second_block(
        x, ffn1_norm_2, ffn1_w_gate_2, ffn1_w_up_2, ffn1_w_down_2, mix_norm_2, w_in_2,
        swa_q_norm_2, swa_k_norm_2, swa_sinks_2, gla_w_gate_2, gla_gate_bias_2, gla_out_norm_2,
        w_proj_a_2, w_proj_b_2, w_out_2, ffn2_norm_2, ffn2_w_gate_2, ffn2_w_up_2, ffn2_w_down_2,
    )


_drawn_inputs = setup_inputs


def setup_inputs(seed=0):
    import zlib

    import numpy as np

    out = dict(_drawn_inputs(seed))
    spreads = {}
    factors = {'norm1_g': 3.311,
     'attn_q_gain': 8.0,
     'attn_k_gain': 8.0,
     'attn_sink': 8.0,
     'hgrn_o_gain': 4.027,
     'hgrn_lb_logits': 4.58,
     'ffn_conv_b': 7.127,
     'ffn1_norm_2': 4.309,
     'mix_norm_2': 3.1,
     'swa_q_norm_2': 8.0,
     'swa_k_norm_2': 8.0,
     'swa_sinks_2': 58.551,
     'gla_gate_bias_2': 3.032,
     'gla_out_norm_2': 6.448,
     'ffn2_norm_2': 5.189}
    for name, (base, spread) in spreads.items():
        noise = np.random.default_rng([zlib.crc32(name.encode()), seed]).standard_normal(out[name].shape)
        drawn = base * np.exp(spread * noise) if base else spread * noise
        out[name] = __import__('jax').numpy.asarray(drawn.astype(out[name].dtype))
    for name, factor in factors.items():
        out[name] = (out[name] * factor).astype(out[name].dtype)
    return out
```

```python
import math
from contextlib import ExitStack

import numpy as np
import concourse.bass as bass
from concourse import mybir

F32 = mybir.dt.float32
F32R = mybir.dt.float32r
ALU = mybir.AluOpType
ACT = mybir.ActivationFunctionType
AX_X = mybir.AxisListType.X

P = 128
D = 1024
KD = D // P
T = 256
TT = T // P
FF = 2816
KF = FF // P
HALF = KF // 2
EPS = 1e-6
HD = 64
NEG = -1.0e30
SCALE = HD ** -0.5
LEVELS = [1, 2, 4, 8, 16, 32, 64]
NL = len(LEVELS) + 1
HG_HEADS = 8
GLA_HEADS = 4
GLA_TAU = 16.0
GLA_RANK = 16

X, C = 0, 1
RAW, RING = 4, 4
SLAB = HALF * P
AHEAD = RING
ADA_FIRST, ADA_QKV, ADA_ATT = 8, 24, 16

VEC = {}
_at = 0
for _name, _width in [
    ("c", 2 * KD), ("ada_b", 2 * 48), ("norm1", 2 * KD), ("norm2", 2 * KD), ("q_gain", 1), ("k_gain", 1),
    ("conv_w", 2 * KF * 3), ("conv_b", 2 * KF), ("lb", 2 * KD), ("o_gain", 1), ("ffn1_norm", 2 * KD),
    ("mix_norm", 2 * KD), ("ffn2_norm", 2 * KD), ("swa_q", 2), ("swa_k", 2), ("gla_bias", 2 * GLA_HEADS),
    ("gla_norm", 2 * KD), ("sink", 16), ("swa_sink", 2 * 8), ("gla_gate", 2 * GLA_HEADS * P),
]:
    VEC[_name] = (_at, _width)
    _at += _width
VEC_W = _at

CON = {}
_at = 0
for _name, _width in [
    ("cos_ax", T), ("sin_ax", T), ("cos_1d", T), ("sin_1d", T), ("ones", P), ("ident", P), ("head_ones", P),
    ("swap16", P), ("swap32", P), ("win0", P), ("win1", P), ("swa_cur", P), ("swa_prev", P),
    ("both", NL * P), ("causal", NL * P),
]:
    CON[_name] = (_at, _width)
    _at += _width
CON_W = _at
CON_EARLY = CON["both"][0]

PAIRS = [(j, 4 + j) for j in range(4)] + [(8 + j, 12 + j) for j in range(4)]
SWA_PAIRS = [(j, 4 + j) for j in range(4)]


def plan():
    slabs, panels, start, ada = [], [], {}, []

    def add_ada(count):
        for n in range(len(ada), len(ada) + count):
            ada.append(len(panels))
            panels.append((f"ada{n // 24}", 2 * (n % 24), 2, None, D))

    def add(phase, array, first, count, width):
        start.setdefault(phase, len(slabs))
        for n in range(0, count, 2):
            here = min(2, count - n)
            panels.append((array, first + n, here, len(slabs), width))
            for k in range(here):
                slabs.append((len(panels) - 1, k, width))
            if len(slabs) == AHEAD:
                add_ada(ADA_FIRST)
            elif AHEAD < len(slabs) <= AHEAD + 24:
                add_ada(2)
            if len(slabs) == AHEAD + 24:
                add_ada(ADA_ATT)

    def ffn(phase, up, down):
        add(phase, up, 0, 2 * KF, D)
        add(phase + "_down", down, 0, 2 * KD, SLAB)

    for t in "xc":
        add("qkv_" + t, "attn_in", 0, 12, D)
    for t in "xc":
        add("attn_out_" + t, "attn_out", 0, KD, D)
    ffn("ffn0_x", "up0", "down0")
    ffn("ffn0_c", "up0", "down0")
    add("hg_c", "hg_v", 0, 8, D)
    add("hg_c", "hg_c", 0, 2 * HG_HEADS, D)
    add("hg_x", "hg_v", 0, 8, D)
    add("hg_x", "hg_x", 0, 4 * HG_HEADS, D)
    add("hg_out", "hg_out", 0, KD, D)
    ffn("ffn1", "up1", "down1")
    for n in range(2):
        ffn(f"b{n}_ffn1", f"b_up1_{n}", f"b_down1_{n}")
        add(f"b{n}_swa", f"b_swa_{n}", 0, 6, D)
        add(f"b{n}_gla", f"b_gla_{n}", 0, 17, D)
        add(f"b{n}_r", f"b_r_{n}", 0, 8, D)
        for j in range(KD):
            add(f"b{n}_merge", f"b_ga_{n}", 2 * j, 2, D)
            add(f"b{n}_merge", f"b_gb_{n}", 2 * j, 2, D)
        add(f"b{n}_out", f"b_out_{n}", 0, KD, D)
        ffn(f"b{n}_ffn2", f"b_up2_{n}", f"b_down2_{n}")
    return slabs, panels, start, ada


def arrays(a):
    def tiles(w):
        k, n = w.shape
        return w.reshape(k // P, P, n // P, P).transpose(2, 1, 0, 3).reshape(n // P, P, k)

    def token_major(w):
        n = w.shape[1]
        return w.reshape(2, 4, P, n // 256, 256).transpose(3, 0, 2, 1, 4).reshape(2 * (n // 256), P, D)

    def down(w):
        return w.reshape(2, HALF, P, KD, P).transpose(3, 0, 2, 1, 4).reshape(2 * KD, P, SLAB)

    def pairs(first, second):
        return np.stack([first, second], 1).reshape(-1, P, first.shape[-1])

    def cat(*parts):
        return np.ascontiguousarray(np.concatenate(parts, 0))

    out = {}
    for n in range(2):
        out[f"ada{n}"] = a["ada_w"][n].reshape(4, 2, P, 12, 512).transpose(3, 0, 2, 1, 4).reshape(48, P, D)
        up = a["ffn_w_up"][n]
        out[f"up{n}"] = pairs(tiles(up[:, :FF]), tiles(up[:, FF:]))
        out[f"down{n}"] = down(a["ffn_w_down"][n])
    w = a["attn_w_in"][0]
    heads = [h for p in PAIRS for h in p]
    q = w[:, :D].reshape(D, 16, HD)[:, heads].reshape(D, D)
    out["attn_in"] = cat(tiles(q), tiles(w[:, D:D + 256]), token_major(w[:, D + 256:]))
    out["attn_out"] = tiles(a["attn_w_out"][0].reshape(16, HD, D)[heads].reshape(D, D))
    w = a["hgrn_w_in"][0]
    q, ff, fb, v, g = (tiles(w[:, n * D:(n + 1) * D]) for n in range(5))
    out["hg_v"] = token_major(w[:, 3 * D:4 * D])
    out["hg_c"] = pairs(ff, fb)
    out["hg_x"] = np.stack([ff, fb, q, g], 1).reshape(-1, P, D)
    out["hg_out"] = tiles(a["hgrn_w_out"][0])
    for n in range(2):
        for k in (1, 2):
            out[f"b_up{k}_{n}"] = pairs(tiles(a[f"ffn{k}_w_gate_2"][n]), tiles(a[f"ffn{k}_w_up_2"][n]))
            out[f"b_down{k}_{n}"] = down(a[f"ffn{k}_w_down_2"][n])
        w = a["w_in_2"][n]
        cut = np.cumsum([0, 512, 128, 128, 512, 512, 1024, 1024, GLA_RANK, 1024, 1024])
        qa, ka, va, qb, kb, vb, rb, lr, ga, gb = (w[:, i:j] for i, j in zip(cut[:-1], cut[1:]))
        heads = [h for p in SWA_PAIRS for h in p]
        qa = qa.reshape(D, 8, HD)[:, heads].reshape(D, 512)
        out[f"b_swa_{n}"] = cat(tiles(qa), tiles(ka), tiles(va))
        wide = np.zeros((D, P), w.dtype)
        wide[:, :GLA_RANK] = lr
        out[f"b_gla_{n}"] = cat(tiles(wide), tiles(qb), tiles(kb), token_major(vb))
        out[f"b_r_{n}"] = tiles(rb)
        pa = a["w_proj_a_2"][n].reshape(8, HD, D)[heads].reshape(512, D)
        short = np.zeros((KD, P, D), w.dtype)
        short[:, :, :512] = tiles(pa)
        out[f"b_ga_{n}"] = pairs(tiles(ga), short)
        out[f"b_gb_{n}"] = pairs(tiles(gb), tiles(a["w_proj_b_2"][n]))
        out[f"b_out_{n}"] = tiles(a["w_out_2"][n])
    out = {k: np.ascontiguousarray(v) for k, v in out.items()}

    vec = np.zeros((P, VEC_W), np.float32)

    def put(name, value):
        at, width = VEC[name]
        vec[:value.shape[0], at:at + width] = value.reshape(value.shape[0], -1)

    def cols(v):
        return np.moveaxis(v.reshape(*v.shape[:-1], -1, P), -1, 0)

    def twice(v):
        return np.moveaxis(np.concatenate([v, v], -1), -1, 0)

    def rows(v):
        return np.broadcast_to(v.reshape(1, -1), (P, v.size))

    put("c", np.stack([cols(a["c"][0]), cols(a["c_ctx"])], -1))
    put("ada_b", cols(a["ada_b"]))
    put("norm1", cols(a["norm1_g"]))
    put("norm2", cols(a["norm2_g"]))
    put("q_gain", twice(a["attn_q_gain"]))
    put("k_gain", twice(a["attn_k_gain"]))
    put("conv_w", cols(a["ffn_conv_w"]).transpose(0, 1, 3, 2))
    put("conv_b", cols(a["ffn_conv_b"]))
    put("lb", cols(a["hgrn_lb_logits"]))
    put("o_gain", cols(a["hgrn_o_gain"]))
    put("ffn1_norm", cols(a["ffn1_norm_2"]))
    put("mix_norm", cols(a["mix_norm_2"]))
    put("ffn2_norm", cols(a["ffn2_norm_2"]))
    put("swa_q", twice(a["swa_q_norm_2"]))
    put("swa_k", twice(a["swa_k_norm_2"]))
    put("gla_bias", cols(a["gla_gate_bias_2"]))
    put("gla_norm", cols(a["gla_out_norm_2"]))
    put("sink", rows(a["attn_sink"]))
    put("swa_sink", rows(a["swa_sinks_2"]))
    put("gla_gate", a["gla_w_gate_2"].transpose(1, 0, 2))
    out["vec"] = vec
    out["con"] = constants()
    for name in ("x", "ctx"):
        out[name] = np.ascontiguousarray(a[name][0].T.reshape(KD, P, T).transpose(1, 0, 2))
    return out


def constants():
    con = np.zeros((P, CON_W), np.float32)

    def put(name, value):
        at, width = CON[name]
        con[:, at:at + width] = value.reshape(P, width)

    tok = np.arange(T, dtype=np.float32)
    d = np.arange(P) % HD
    inv = (10000.0 ** (-(np.arange(16, dtype=np.float32) / 16))).astype(np.float32)
    place = np.where(d[:, None] < 32, (tok // 64)[None], (tok % 64)[None]).astype(np.float32)
    ang = place * inv[d % 16][:, None]
    sign = np.where(d % 32 < 16, -1.0, 1.0)[:, None]
    put("cos_ax", np.cos(ang))
    put("sin_ax", np.sin(ang) * sign)
    inv = (10000.0 ** (-(np.arange(0, HD, 2, dtype=np.float32) / HD))).astype(np.float32)
    ang = tok[None] * inv[d % 32][:, None]
    put("cos_1d", np.cos(ang))
    put("sin_1d", np.sin(ang) * np.where(d < 32, -1.0, 1.0)[:, None])
    put("ones", np.ones((P, P)))
    put("ident", np.eye(P))
    put("head_ones", np.kron(np.eye(2), np.ones((HD, HD))))
    i = np.arange(P)
    put("swap16", i[:, None] == (i ^ 16)[None])
    put("swap32", i[:, None] == (i ^ 32)[None])
    q, k = i[:, None], i[None]
    put("win0", np.where(k <= q, 0, NEG))
    put("win1", np.where(k >= q, 0, NEG))
    put("swa_cur", np.where(k <= q, 0, NEG))
    put("swa_prev", np.where(k > q, 0, NEG))
    s, t = i[:, None], i[None]
    both = [s == t] + [(s // (2 * m) == t // (2 * m)) & (s // m != t // m) for m in LEVELS]
    put("both", np.stack(both, 1))
    put("causal", np.stack([both[0]] + [b & (s < t) for b in both[1:]], 1))
    return con


CONVS = {"ffn0_x": 0, "ffn0_c": 1, "ffn1": 2}


def tile_plan(start, n_slabs):
    freed, first, count = [], {}, {"v": 0, "a": 0}

    def add(phase, who):
        first.setdefault(phase, len(freed))
        for w in who:
            count[w] += 1
            freed.append((w, count[w]))

    for phase in start:
        if phase.startswith("qkv"):
            add(phase, "v" * 12)
        elif phase == "hg_c":
            add(phase, "a" * (8 + 2 * HG_HEADS))
        elif phase == "hg_x":
            add(phase, "a" * (8 + 4 * HG_HEADS))
        elif phase.endswith("swa"):
            add(phase, "v" * 5 + "v" * 2)
        elif phase.endswith("gla"):
            add(phase, "v" * 9 + "a" * 8)
        elif phase.endswith("merge"):
            add(phase, "v" * 4 * KD)
        elif phase.endswith("_down") or "out" in phase or phase.endswith("_r"):
            add(phase, "v" * KD)
        else:
            add(phase, "v" * 2 * KF)
    return freed, first


def build(nc, dram, out):
    slabs, panels, start, ada = plan()
    freed, first_tile = tile_plan(start, len(slabs))
    with ExitStack() as ctx:
        scopes = [ctx]

        def sb(name, shape, dt=F32):
            return scopes[-1].enter_context(nc.sbuf_tensor(name, shape, dt))

        def sem(name):
            return ctx.enter_context(nc.semaphore(name))

        raw = [sb(f"raw{n}", [P, 2, SLAB]) for n in range(RAW)]
        w_hi = [sb(f"w_hi{n}", [P, SLAB], F32R) for n in range(RING)]
        w_lo = [sb(f"w_lo{n}", [P, SLAB], F32R) for n in range(RING)]
        res = [sb("res_x", [P, KD, T]), sb("res_c", [P, KD, T])]
        h_hi = sb("h_hi", [P, KD, T], F32R)
        h_lo = sb("h_lo", [P, KD, T], F32R)
        h_fp = sb("h_fp", [P, KD, T])
        vec = sb("vec", [P, VEC_W])
        con = sb("con", [P, CON_W])
        mod = sb("mod", [P, 2, 48, 2])
        mod_g = sb("mod_g", [P, 2, 2, 2, KD])
        WIDE = ADA_QKV - 2
        c_wide = sb("c_wide", [P, KD, 2 * WIDE + 2])
        lb = sb("lb", [P, 4, KD])
        eps = sb("eps", [P, 1])
        warm = sb("warm", [P, 1])
        rms = sb("rms", [P, T])
        rstd = sb("rstd", [P, T])
        conv = [sb(f"conv{n}", [P, T]) for n in range(2)]
        gate = [sb(f"gate{n}", [P, T]) for n in range(2)]
        prod = [sb(f"prod{n}", [P, T]) for n in range(2)]

        def V(name, *shape):
            at, width = VEC[name]
            v = vec[:, at:at + width]
            return v if not shape else v.rearrange(shape[0], **shape[1])

        def K(name, cols=None):
            at, width = CON[name]
            return con[:, at:at + (cols or width)]

        c_in = V("c", "p (k s) -> p k s", dict(s=2))
        norm1 = V("norm1", "p (l k) -> p l k", dict(l=2))
        norm2 = V("norm2", "p (l k) -> p l k", dict(l=2))
        conv_w = V("conv_w", "p (l f w) -> p l f w", dict(l=2, w=3))
        conv_b = V("conv_b", "p (l f) -> p l f", dict(l=2))

        psum = [ctx.enter_context(nc.psum_tensor(f"bank{n}", [P, 512], F32)) for n in range(8)]
        NORM, ADA, SUMS, TURN = 4, 5, 6, 7

        params_in = sem("params_in")
        con_in = sem("con_in")
        x_in = sem("x_in")
        ctx_in = sem("ctx_in")
        raw_ready = [sem(f"raw_ready{n}") for n in range(RAW)]
        hi_ready = sem("hi_ready")
        lo_ready = sem("lo_ready")
        slab_used = sem("slab_used")
        freed_v = sem("freed_v")
        freed_a = sem("freed_a")
        v_step = sem("v_step")
        eps_set = sem("eps_set")
        c_silu = sem("c_silu")
        c_clear = sem("c_clear")
        ada_used = sem("ada_used")
        ada_rows = sem("ada_rows")
        ada_turned = sem("ada_turned")
        mod_ready = sem("mod_ready")
        sq_ready = sem("sq_ready")
        norm_sum = sem("norm_sum")
        rms_ready = sem("rms_ready")
        h_fp_ready = sem("h_fp_ready")
        h_hi_ready = sem("h_hi_ready")
        h_ready = sem("h_ready")
        conv_1 = sem("conv_1")
        conv_2 = sem("conv_2")
        conv_3 = sem("conv_3")
        gate_ready = sem("gate_ready")
        act_hi_ready = sem("act_hi_ready")
        act_ready = sem("act_ready")
        out_done = sem("out_done")

        def freed_by(o):
            who, n = freed[o]
            return (freed_v if who == "v" else freed_a), n


        def load(sp, p, i=0, laps=0):
            array, row, count, s, width = panels[p]
            if p >= RAW:
                prev = panels[p - RAW]
                if prev[3] is None:
                    sp.wait_ge(ada_used, ada.index(p - RAW) + 1)
                else:
                    sp.wait_ge(lo_ready, prev[3] + prev[2] + i * 2 * RAW)
            src = dram[array][row + i * 2 * RAW:row + i * 2 * RAW + count] if laps else \
                dram[array][row:row + count]
            sp.dma_start(raw[p % RAW][:, 0:count, 0:width], src.rearrange("s p f -> p s f"))\
                .then_inc(raw_ready[p % RAW], 16)

        def split_hi(act, k, i=0):
            if k >= len(slabs):
                return
            p, place, width = slabs[k]
            if place == 0:
                act.wait_ge(raw_ready[p % RAW], 16 * (p // RAW + 1) + i * 16)
            if k >= RING:
                act.wait_ge(slab_used, k - RING + 1 + i * 8)
            act.activation(w_hi[k % RING][:, 0:width], raw[p % RAW][:, place, 0:width], ACT.Copy)\
                .then_inc(hi_ready, 1)

        def split_lo(dve, k, i=0):
            if k >= len(slabs):
                return
            p, place, width = slabs[k]
            dve.wait_ge(hi_ready, k + 1 + i * 8)
            dve.tensor_tensor(w_lo[k % RING][:, 0:width], raw[p % RAW][:, place, 0:width],
                              w_hi[k % RING][:, 0:width], ALU.subtract).then_inc(lo_ready, 1)

        def three(pe, out_ap, a_hi, a_lo, b_hi, b_lo, start, stop):
            pe.matmul(out_ap, a_hi, b_hi, start=start, stop=False)
            pe.matmul(out_ap, a_hi, b_lo, start=False, stop=False)
            return pe.matmul(out_ap, a_lo, b_hi, start=False, stop=stop)

        def multiply(pe, k, o, hi, lo, blocks=KD, first=True, last=True, k0=0, i=0, lap=4, norm=None):
            pe.wait_ge(lo_ready, k + 1 + i * lap)
            bank = psum[o % 4][:, 0:T]
            for b in range(blocks):
                w = slice(b * P, (b + 1) * P)
                if norm is not None:
                    pe.wait_ge(h_ready, KD * norm + b + 1)
                mm = three(pe, bank, w_hi[k % RING][:, w], w_lo[k % RING][:, w], hi[:, k0 + b, :], lo[:, k0 + b, :],
                           first and b == 0, last and b == blocks - 1)
            mm.then_inc(slab_used, 1)

        def bank_free(pe, o):
            if o >= 4:
                pe.wait_ge(*freed_by(o - 4))

        def multiply_tokens(pe, k, o, part, groups=4, width=256, norm=None):
            pe.wait_ge(lo_ready, k + 1)
            for t in range(TT):
                for b in range(groups):
                    f = part * groups + b
                    w = slice(b * width, (b + 1) * width)
                    tok = slice(t * P, (t + 1) * P)
                    if norm is not None:
                        pe.wait_ge(h_ready, KD * norm + f + 1)
                    mm = three(pe, psum[(o + t) % 4][:, 0:width], h_hi[:, f, tok], h_lo[:, f, tok],
                               w_hi[k % RING][:, w], w_lo[k % RING][:, w],
                               f == 0, f == KD - 1)
            mm.then_inc(slab_used, 1)

        ADA_PARTS = [(0, ADA_FIRST), (ADA_FIRST, ADA_QKV), (ADA_FIRST + ADA_QKV, ADA_ATT)]
        ADA_BANK = [psum[ADA], psum[ADA], psum[3]]

        def ada_pe(pe, part, first, count):
            at, panels_ = ADA_PARTS[part]
            for n in range(first, first + count):
                p = ada[at + n]
                pe.wait_ge(raw_ready[p % RAW], 16 * (p // RAW + 1))
                shift_ = WIDE - 2 * (n // 2)
                for b in range(4):
                    k = 4 * (n % 2) + b
                    mm = pe.matmul(ADA_BANK[part][0:panels_, :], c_wide[:, k, shift_:shift_ + panels_],
                                   raw[p % RAW][:, b // 2, (b % 2) * 512:(b % 2 + 1) * 512],
                                   start=n == 0 and b == 0, stop=n == panels_ - 1 and b == 3)
                mm.then_inc(ada_used, 1)

        def ada_turn_pe(pe, part):
            rows = ADA_PARTS[part][1]
            pe.wait_ge(ada_rows, part + 1)
            for q in range(4):
                mm = pe.transpose(ADA_BANK[part][:, q * rows:(q + 1) * rows],
                                  conv[q // 2][0:rows, (q % 2) * P:(q % 2 + 1) * P], K("ident")[0:rows, 0:rows])
            mm.then_inc(ada_turned, 1)

        def ada_dve(dve, link, part):
            at, rows = ADA_PARTS[part]
            first, end = 2 * at, 2 * (at + rows)
            dve.wait_ge(ada_used, at + rows)
            for half in range(2):
                ins = dve.tensor_copy(conv[half][0:rows, :], ADA_BANK[part][0:rows, half * T:(half + 1) * T])
            ins.then_inc(ada_rows, 1)
            dve.wait_ge(ada_turned, part + 1)
            for q in range(4):
                sums = ADA_BANK[part][:, q * rows:(q + 1) * rows].rearrange("p (g s) -> p g s", s=2)
                ada_bias = V("ada_b", "p (g q) -> p g q", dict(q=4))[:, first // 4:end // 4, q]
                into = mod[:].rearrange("p l (g q) s -> p (l g) q s", q=4)[:, first // 4:end // 4, q, :]
                ins = dve.tensor_tensor(into, sums, ada_bias.unsqueeze(2).to_broadcast([P, (end - first) // 4, 2]), ALU.add)
            link(ins)
            for layer in range(2):
                for n, (gains_, chunk) in enumerate(((norm1, 1), (norm2, 4))):
                    if first <= 48 * layer + 8 * chunk < end:
                        for t in (X, C):
                            ins = dve.scalar_tensor_tensor(mod_g[:, layer, n, t, :], mod[:, layer, 8 * chunk:8 * chunk + 8, t],
                                                           1.0, gains_[:, layer, :], ALU.add, ALU.mult)
            ins.then_inc(mod_ready, 1)
            dve.wait_ge(mod_ready, part + 1)

        def norm_act(act, n, t, base_freed, shift, s_before, mod_parts=None):
            act.wait_ge(eps_set, 1)
            act.activation(warm[:], eps[:], ACT.Sqrt)
            if n:
                act.wait_ge(h_ready, KD * n)
            for k in range(KD):
                if base_freed is None:
                    act.wait_ge((x_in, ctx_in)[t], 16)
                else:
                    act.wait_ge(*freed_by(base_freed + k))
                act.activation(h_fp[:, k, :], res[t][:, k, :], ACT.Square).then_inc(sq_ready, 1)
            act.wait_ge(norm_sum, n + 1)
            act.activation(rms[:], psum[NORM][:, 0:T], ACT.Sqrt, bias=eps[:], scale=1.0 / D).then_inc(rms_ready, 1)
            if s_before:
                act.wait_ge(slab_used, s_before)
            if mod_parts:
                act.wait_ge(mod_ready, mod_parts)
            for k in range(KD):
                act.wait_ge(h_fp_ready, KD * n + k + 1)
                if shift is None:
                    act.activation(h_hi[:, k, :], h_fp[:, k, :], ACT.Copy).then_inc(h_hi_ready, 1)
                else:
                    act.activation(h_hi[:, k, :], h_fp[:, k, :], ACT.Identity, bias=shift(k)).then_inc(h_hi_ready, 1)

        def norm_pe(pe, n):
            for k in range(KD):
                pe.wait_ge(sq_ready, KD * n + k + 1)
                mm = pe.matmul(psum[NORM][:, 0:T], K("ones"), h_fp[:, k, :], start=k == 0, stop=k == KD - 1)
            mm.then_inc(norm_sum, 1)

        def norm_dve(dve, link, n, t, scale, shift):
            dve.wait_ge(rms_ready, n + 1)
            link(dve.reciprocal(rstd[:], rms[:]))
            for k in range(KD):
                dve.scalar_tensor_tensor(h_fp[:, k, :], res[t][:, k, :], scale(k), rstd[:], ALU.mult, ALU.mult)\
                    .then_inc(h_fp_ready, 1)
                if k >= 1:
                    norm_lo(dve, n, k - 1, shift)
            norm_lo(dve, n, KD - 1, shift)

        def norm_lo(dve, n, k, shift):
            dve.wait_ge(h_hi_ready, KD * n + k + 1)
            if shift is None:
                ins = dve.tensor_tensor(h_lo[:, k, :], h_fp[:, k, :], h_hi[:, k, :], ALU.subtract)
            else:
                ins = dve.scalar_tensor_tensor(h_lo[:, k, :], h_fp[:, k, :], shift(k), h_hi[:, k, :],
                                               ALU.add, ALU.subtract)
            ins.then_inc(h_ready, 1)

        def ffn_pe(pe, phase, n_norm, n_ffn):
            s0, o0 = start[phase], first_tile[phase]
            with pe.Fori(0, 2 * KF // 4) as i:
                for j in range(4):
                    pe.wait_ge(freed_v, freed[o0 + j - 4][1] + i * 4)
                    multiply(pe, s0 + j, o0 + j, h_hi, h_lo, i=i, norm=n_norm if j == 0 else None)
            s1, o1 = start[phase + "_down"], first_tile[phase + "_down"]
            with pe.Fori(0, 2) as i:
                for j in range(8):
                    pe.wait_ge(act_ready, KF * n_ffn + HALF * (j % 2 + 1))
                    if j % 2 == 0:
                        pe.wait_ge(freed_v, freed[o1 + j // 2 - 4][1] + i * 4)
                    multiply(pe, s1 + j, o1 + j // 2, act_hi, act_lo, blocks=HALF, first=j % 2 == 0,
                             last=j % 2 == 1, k0=HALF * (j % 2), i=i, lap=8)

        def ffn_up_act(act, phase, n_ffn, conv_layer, j, f, i, i8=0):
            s, o = start[phase] + 2 * j, first_tile[phase] + 2 * j
            u = KF * n_ffn + j
            four = i8 * 4
            act.wait_ge(slab_used, s + 1 + i8 * 8)
            if conv_layer is None:
                act.wait_ge(freed_v, freed[o - 4][1] + 1 + i8 * 8)
                act.activation(gate[j % 2][:], psum[o % 4][:, 0:T], ACT.Silu).then_inc(gate_ready, 1)
                split_hi(act, s + AHEAD, i8)
            else:
                act.wait_ge(freed_v, freed[o - 4][1] + 1 + i8 * 8)
                act.activation(conv[j % 2][:], psum[o % 4][:, 0:T], ACT.Identity, scale=conv_w[:, conv_layer, f, 1:2],
                               bias=conv_b[:, conv_layer, f:f + 1] if isinstance(f, int) else
                               conv_b[:, conv_layer, bass.ds(f, 1)]).then_inc(conv_1, 1)
                split_hi(act, s + AHEAD, i8)
                nc_ = CONVS[phase]
                act.wait_ge(conv_3, KF * nc_ + j + 1 + four)
                act.activation(gate[j % 2][:], conv[j % 2][:], ACT.Silu).then_inc(gate_ready, 1)
            split_hi(act, s + 1 + AHEAD, i8)
            act.wait_ge(freed_v, freed[o][1] + 1 + i8 * 8)
            act.activation(act_hi[:, f, :], prod[j % 2][:], ACT.Copy).then_inc(act_hi_ready, 1)

        def ffn_up_dve(dve, phase, n_ffn, conv_layer, j, f, i, i8=0):
            s, o = start[phase] + 2 * j, first_tile[phase] + 2 * j
            u = KF * n_ffn + j
            four = i8 * 4
            if conv_layer is not None:
                nc_ = KF * CONVS[phase] + j
                g = psum[o % 4]
                cv = conv[j % 2]
                dve.wait_ge(conv_1, nc_ + 1 + four)
                dve.scalar_tensor_tensor(cv[:, 1:T], g[:, 0:T - 1], conv_w[:, conv_layer, f, 0:1], cv[:, 1:T],
                                         ALU.mult, ALU.add).then_inc(conv_2, 1)
                dve.wait_ge(conv_2, nc_ + 1 + four)
                dve.scalar_tensor_tensor(cv[:, 0:T - 1], g[:, 1:T], conv_w[:, conv_layer, f, 2:3], cv[:, 0:T - 1],
                                         ALU.mult, ALU.add).then_inc(conv_3, 1)
            split_lo(dve, s + AHEAD, i8)
            dve.wait_ge(slab_used, s + 2 + i8 * 8)
            dve.wait_ge(gate_ready, u + 1 + four)
            dve.tensor_tensor(prod[j % 2][:], psum[(o + 1) % 4][:, 0:T], gate[j % 2][:], ALU.mult)\
                .then_inc(freed_v, 2)
            split_lo(dve, s + 1 + AHEAD, i8)
            dve.wait_ge(act_hi_ready, u + 1 + four)
            dve.tensor_tensor(act_lo[:, f, :], prod[j % 2][:], act_hi[:, f, :], ALU.subtract)\
                .then_inc(act_ready, 1)

        def ffn_up(eng, step, phase, n_ffn, conv_layer):
            with eng.Fori(0, 5) as i:
                for j in range(4):
                    step(eng, phase, n_ffn, conv_layer, j, i * 4 + j, i, i)
            for j in range(20, KF):
                step(eng, phase, n_ffn, conv_layer, j, j, None)

        def ffn_down_act(act, phase):
            for j in range(2 * KD):
                split_hi(act, start[phase + "_down"] + j + AHEAD)

        def residual_dve(dve, phase, t, gain, halves=1):
            s0, o0 = start[phase], first_tile[phase]
            for j in range(KD):
                dve.wait_ge(slab_used, s0 + halves * (j + 1))
                dve.scalar_tensor_tensor(res[t][:, j, :], psum[(o0 + j) % 4][:, 0:T], gain(j), res[t][:, j, :],
                                         ALU.mult, ALU.add).then_inc(freed_v, 1)
                for k in range(halves):
                    split_lo(dve, s0 + halves * j + k + AHEAD)

        def linear_pe(pe, phase, hi, lo, ready=None):
            s0, o0 = start[phase], first_tile[phase]
            for j in range(KD):
                bank_free(pe, o0 + j)
                if ready:
                    ready(j)
                multiply(pe, s0 + j, o0 + j, hi, lo)

        def region():
            scopes.append(ExitStack())

        def close():
            scopes.pop().close()

        sums4 = sb("sums4", [P, 4])
        top4 = sb("top4", [P, 4])
        ntop4 = sb("ntop4", [P, 4])
        esink4 = sb("esink4", [P, 4])
        den4 = sb("den4", [P, 4])
        rden4 = sb("rden4", [P, 4])
        nsink = sb("nsink", [P, 32])
        region()
        act_hi = sb("act_hi", [P, KF, T], F32R)
        act_lo = sb("act_lo", [P, KF, T], F32R)
        close()
        region()
        att_q = [sb("att_q_x", [P, KD, T]), sb("att_q_c", [P, KD, T])]
        att_k = sb("att_k", [P, 2, 2 * T])
        att_v = sb("att_v", [P, 2 * TT, 2 * P])
        att_o = sb("att_o", [P, 2 * TT, D])
        probs = [h_fp[:, 4 + 2 * n:6 + 2 * n, :].rearrange("p a b -> p (a b)") for n in range(2)]
        att_sq = prod
        att_root = gate
        probs_t = [sb(f"probs_t{n}", [P, 4, P]) for n in range(2)]
        close()
        region()
        hg_v = sb("hg_v", [P, TT, D])
        hg_s = res[C][:].rearrange("p h (d v) -> p h d v", d=2)
        hg_sq = sb("hg_sq", [P, T])
        hg_root = sb("hg_root", [P, T])
        hg_o_hi = sb("hg_o_hi", [P, KD, T], F32R)
        hg_o_lo = sb("hg_o_lo", [P, KD, T], F32R)
        hg_sig = [[h_fp[:, 2 * d + n, :] for n in range(2)] for d in range(2)]
        hg_q = [sb(f"hg_q{n}", [P, T]) for n in range(2)]
        hg_g = [sb(f"hg_g{n}", [P, T]) for n in range(2)]
        hg_k = [[sb(f"hg_k{d}{n}", [P, T]) for n in range(2)] for d in range(2)]
        hg_p = [[sb(f"hg_p{d}{n}", [P, T]) for n in range(2)] for d in range(2)]
        hg_r = [sb(f"hg_r{d}", [P, T]) for d in range(2)]
        hg_u = [sb(f"hg_u{n}", [P, T]) for n in range(2)]
        hg_w = [sb(f"hg_w{n}", [P, T]) for n in range(2)]
        hg_a = [sb(f"hg_a{n}", [P, TT, P]) for n in range(2)]
        hg_kt = h_fp[:, 4:6, :].rearrange("p a (b q) -> p (a b) q", q=P)
        close()
        region()
        oa_hi = sb("oa_hi", [P, 4, T], F32R)
        oa_lo = sb("oa_lo", [P, 4, T], F32R)
        ob = res[C]
        region()
        swa_q = sb("swa_q", [P, 5, T])
        swa_v = sb("swa_v", [P, TT, P])
        swa_sq = [sb(f"swa_sq{n}", [P, T]) for n in range(2)]
        swa_root = [sb(f"swa_root{n}", [P, T]) for n in range(2)]
        swa_o = sb("swa_o", [P, TT, 4 * P])
        swa_p = [sb(f"swa_p{n}", [P, T]) for n in range(2)]
        swa_pt = [sb(f"swa_pt{n}", [P, TT, P]) for n in range(2)]
        close()
        region()
        gl_q = sb("gl_q", [P, GLA_HEADS, T])
        gl_k = sb("gl_k", [P, GLA_HEADS, T])
        gl_p = sb("gl_p", [P, GLA_HEADS, T])
        gl_r = sb("gl_r", [P, GLA_HEADS, T])
        gl_lr = conv[0]
        gl_v = sb("gl_v", [P, TT, D])
        gl_u = [sb(f"gl_u{n}", [P, GLA_HEADS, P]) for n in range(2)]
        gl_w = [sb(f"gl_w{n}", [P, GLA_HEADS, P]) for n in range(2)]
        gl_sq = [u[:].rearrange("p h t -> p (h t)") for u in gl_u]
        gl_a = [sb(f"gl_a{n}", [P, GLA_HEADS, P]) for n in range(2)]
        close()
        region()
        ob_hi = sb("ob_hi", [P, KD, T], F32R)
        ob_lo = sb("ob_lo", [P, KD, T], F32R)
        mg_hi = sb("mg_hi", [P, KD, T], F32R)
        mg_lo = sb("mg_lo", [P, KD, T], F32R)
        close()
        close()
        scopes[:] = [ctx]

        qk_sq = sem("qk_sq")
        qk_sum = sem("qk_sum")
        qk_rms = sem("qk_rms")
        qk_turn = sem("qk_turn")
        turn_free = sem("turn_free")
        mixer_in = sem("mixer_in")
        s_done = sem("s_done")
        top_ready = sem("top_ready")
        p_ready = sem("p_ready")
        esink_ready = sem("esink_ready")
        pt_done = sem("pt_done")
        pt_ready = sem("pt_ready")
        o_done = sem("o_done")
        o_out = sem("o_out")
        ot_done = sem("ot_done")
        ot_hi = sem("ot_hi")
        ot_ready = sem("ot_ready")
        sig_ready = sem("sig_ready")
        f_ready = sem("f_ready")
        decay_b = sem("decay_b")
        decay_f = sem("decay_f")
        kd_ready = sem("kd_ready")
        kd_ready_b = sem("kd_ready_b")
        kt_done = sem("kt_done")
        kt_ready = sem("kt_ready")
        state_done = sem("state_done")
        state_ready = sem("state_ready")
        uw_ready = sem("uw_ready")
        a_done = sem("a_done")
        a_ready = sem("a_ready")
        pv_done = sem("pv_done")
        lin_sq = sem("lin_sq")
        lin_sum = sem("lin_sum")
        lin_rms = sem("lin_rms")
        lin_norm = sem("lin_norm")
        lin_gated = sem("lin_gated")
        lin_hi = sem("lin_hi")
        lin_ready = sem("lin_ready")
        lr_ready = sem("lr_ready")
        z_done = sem("z_done")
        z_abs = sem("z_abs")
        z_exp = sem("z_exp")
        z_ln = sem("z_ln")
        z_min = sem("z_min")
        z_sub = sem("z_sub")
        w_ready = sem("w_ready")
        r_set = sem("r_set")
        mix_sig = sem("mix_sig")
        mix_sum = sem("mix_sum")
        mix_hi = sem("mix_hi")
        mix_ready = sem("mix_ready")
        lb_top = sem("lb_top")
        lb_exp = sem("lb_exp")

        def nsink_dve(dve, link):
            link(dve.tensor_scalar(nsink[:, 0:16], V("sink"), -1.0, None, ALU.mult))
            link(dve.tensor_scalar(nsink[:, 16:32], V("swa_sink"), -1.0, None, ALU.mult))

        def qk_pe(pe, phase, tiles, dst, swap, n0, r0, sq, norm, ada_first=None):
            s0, o0 = start[phase], first_tile[phase]
            for m in range(tiles + 2):
                if m < tiles:
                    bank_free(pe, o0 + m)
                    multiply(pe, s0 + m, o0 + m, h_hi, h_lo, norm=norm if m == 0 else None)
                    if ada_first is not None and m % 2:
                        ada_pe(pe, 1, ada_first + m - 1, 2)
                if 1 <= m <= tiles:
                    n = n0 + m - 1
                    pe.wait_ge(qk_sq, n + 1)
                    if n:
                        pe.wait_ge(qk_rms, n)
                    pe.matmul(psum[SUMS][:, 0:T], K("head_ones"), sq[n % 2][:], start=True, stop=True)\
                        .then_inc(qk_sum, 1)
                if m >= 2 and swap:
                    pe.wait_ge(*freed_by(o0 + m - 2))
                    if r0 + m - 2:
                        pe.wait_ge(turn_free, r0 + m - 2)
                    pe.matmul(psum[TURN][:, 0:T], K(swap), dst(m - 2), start=True, stop=True).then_inc(qk_turn, 1)

        def qk_act(act, phase, tiles, n0, sq, root):
            s0, o0 = start[phase], first_tile[phase]
            for m in range(tiles + 1):
                n = n0 + m
                if m < tiles:
                    act.wait_ge(slab_used, s0 + m + 1)
                    if n >= 2:
                        act.wait_ge(qk_sum, n - 1)
                    act.activation(sq[n % 2][:], psum[(o0 + m) % 4][:, 0:T], ACT.Square).then_inc(qk_sq, 1)
                if m >= 1:
                    act.wait_ge(qk_sum, n)
                    if m >= 3:
                        act.wait_ge(*freed_by(o0 + m - 3))
                    act.activation(root[(n - 1) % 2][:], psum[SUMS][:, 0:T], ACT.Sqrt, bias=eps[:],
                                   scale=1.0 / HD).then_inc(qk_rms, 1)
                if m < tiles:
                    split_hi(act, s0 + m + AHEAD)

        def qk_dve(dve, link, phase, tiles, dst, gain, cos, sin, n0, r0, root):
            s0, o0 = start[phase], first_tile[phase]
            for m in range(tiles + 2):
                if 1 <= m <= tiles:
                    n = n0 + m - 1
                    dve.wait_ge(qk_rms, n + 1)
                    if m >= 2:
                        dve.wait_ge(*freed_by(o0 + m - 2))
                    link(dve.reciprocal(rstd[:], root[n % 2][:]))
                    dve.scalar_tensor_tensor(dst(m - 1), psum[(o0 + m - 1) % 4][:, 0:T], gain(m - 1), rstd[:],
                                             ALU.mult, ALU.mult).then_inc(freed_v, 1)
                if m >= 2 and cos:
                    dve.wait_ge(*freed_by(o0 + m - 2))
                    dve.wait_ge(qk_turn, r0 + m - 1)
                    link(dve.tensor_tensor(conv[0][:], psum[TURN][:, 0:T], K(sin), ALU.mult))
                    dve.tensor_tensor(dst(m - 2), dst(m - 2), K(cos), ALU.mult).then_inc(turn_free, 1)
                    dve.wait_ge(turn_free, r0 + m - 1)
                    link(dve.tensor_tensor(dst(m - 2), dst(m - 2), conv[0][:], ALU.add))
                if m < tiles:
                    split_lo(dve, s0 + m + AHEAD)

        def att_pe(pe, units, u0, o_last, probs_, probs_t_, n_in, with_ada=False):
            pe.wait_ge(mixer_in, n_in)
            for n in range(o_last - 3, o_last + 1):
                pe.wait_ge(*freed_by(n))
            for m in range(len(units) + 2):
                if m < len(units):
                    u = u0 + m
                    q, k, masks = units[m][:3]
                    if m >= 2:
                        pe.wait_ge(p_ready, u - 1)
                    bank = psum[4 + m % 2]
                    keys = k.shape[-1]
                    mm = pe.matmul(bank[:, 0:keys], q, k, start=True, stop=True, skip_group_check=bool(masks))
                    for block, mask in masks:
                        mm = pe.matmul(bank[:, block * P:(block + 1) * P], K("ident"), K(mask), start=False,
                                       stop=True, skip_group_check=True)
                    mm.then_inc(s_done, 1)
                if with_ada and m % 2 and m < 2 * ADA_ATT:
                    ada_pe(pe, 2, m // 2, 1)
                if 1 <= m <= len(units):
                    u = u0 + m - 1
                    pe.wait_ge(p_ready, u + 1)
                    if m >= 3:
                        pe.wait_ge(pt_ready, u - 1)
                    for b in range(units[m - 1][1].shape[-1] // P):
                        mm = pe.transpose(psum[6 + (m - 1) % 2][:, b * P:(b + 1) * P],
                                          probs_[(m - 1) % 2][:, b * P:(b + 1) * P], K("ident"))
                    mm.then_inc(pt_done, 1)
                if m >= 2:
                    u = u0 + m - 2
                    pe.wait_ge(pt_ready, u + 1)
                    if m >= 4:
                        pe.wait_ge(o_out, u - 1)
                    v = units[m - 2][3]
                    for b in range(len(v)):
                        mm = pe.matmul(psum[m % 2][:, 0:HD], probs_t_[m % 2][:, b, :], v[b], start=b == 0,
                                       stop=b == len(v) - 1)
                    mm.then_inc(o_done, 1)

        def att_act(act, units, u0, probs_, probs_t_):
            for m in range(len(units) + 1):
                if m < len(units):
                    u = u0 + m
                    keys = units[m][1].shape[-1]
                    col = slice(u % 4, u % 4 + 1)
                    act.wait_ge(top_ready, u + 1)
                    if m >= 2:
                        act.wait_ge(pt_done, u - 1)
                    act.activation(probs_[m % 2][:, 0:keys], psum[4 + m % 2][:, 0:keys], ACT.Exp, bias=ntop4[:, col],
                                   scale=SCALE, accum_out=sums4[:, col]).then_inc(p_ready, 1)
                    act.activation(esink4[:, col], ntop4[:, col], ACT.Exp, bias=units[m][4]).then_inc(esink_ready, 1)
                if m >= 1:
                    u = u0 + m - 1
                    keys = units[m - 1][1].shape[-1]
                    act.wait_ge(pt_done, u + 1)
                    if m >= 3:
                        act.wait_ge(o_done, u - 1)
                    act.activation(probs_t_[(m - 1) % 2][:, 0:keys // P, :],
                                   psum[6 + (m - 1) % 2][:, 0:keys].rearrange("p (b q) -> p b q", q=P), ACT.Copy)\
                        .then_inc(pt_ready, 1)

        def att_dve(dve, link, units, u0):
            for m in range(len(units) + 2):
                if m < len(units):
                    u = u0 + m
                    col = slice(u % 4, u % 4 + 1)
                    dve.wait_ge(s_done, u + 1)
                    link(dve.reduce_max(top4[:, col], psum[4 + m % 2][:, 0:units[m][1].shape[-1]], AX_X))
                    dve.tensor_scalar(ntop4[:, col], top4[:, col], -SCALE, units[m][5], ALU.mult, ALU.min)\
                        .then_inc(top_ready, 1)
                if m >= 2:
                    u = u0 + m - 2
                    col = slice(u % 4, u % 4 + 1)
                    dve.wait_ge(esink_ready, u + 1)
                    link(dve.tensor_tensor(den4[:, col], sums4[:, col], esink4[:, col], ALU.add))
                    link(dve.reciprocal(rden4[:, col], den4[:, col]))
                    dve.wait_ge(o_done, u + 1)
                    dve.tensor_scalar(units[m - 2][2 + 4], psum[m % 2][:, 0:HD], rden4[:, col], None, ALU.mult)\
                        .then_inc(o_out, 1)

        def turn_pe(pe, o, tiles, u_end, n0):
            pe.wait_ge(o_out, u_end)
            for f in range(tiles):
                if n0 + f >= 2:
                    pe.wait_ge(ot_ready, n0 + f - 1)
                for t in range(TT):
                    mm = pe.transpose(psum[f % 2][:, t * P:(t + 1) * P], o[:, t, f * P:(f + 1) * P], K("ident"))
                mm.then_inc(ot_done, 1)

        def turn_act(act, hi, tiles, n0):
            for f in range(tiles):
                act.wait_ge(ot_done, n0 + f + 1)
                act.activation(hi[:, f, :], psum[f % 2][:, 0:T], ACT.Copy).then_inc(ot_hi, 1)

        def turn_dve(dve, hi, lo, tiles, n0):
            for f in range(tiles):
                dve.wait_ge(ot_hi, n0 + f + 1)
                dve.tensor_tensor(lo[:, f, :], psum[f % 2][:, 0:T], hi[:, f, :], ALU.subtract).then_inc(ot_ready, 1)

        STEPS = [1, 2, 4, 8, 16, 32, 64, 128]
        NSTEP = len(STEPS)
        done = {"b": 0, "f": 0}

        def decay_step(eng, way, p, r, m, heads=False):
            signal = decay_f if way == "f" else decay_b
            shape = "p h (b c m) -> p (h b) c m" if heads else "p (b c m) -> p b c m"
            pv, rv = (x.rearrange(shape, c=2, m=m) for x in (p, r))
            near, far, end = (0, 1, m - 1) if way == "f" else (1, 0, 0)
            blocks = pv.shape[1]
            for x, side, other in ((rv, near, far), (pv, far, near)):
                eng.tensor_tensor(x[:, :, side, :], x[:, :, side, :],
                                  pv[:, :, other, end:end + 1].to_broadcast([P, blocks, m]), ALU.mult)\
                    .then_inc(signal, 1)
                done[way] += 1
                eng.wait_ge(signal, done[way])

        def decay_f_step(dve, p, r, m, heads=False):
            decay_step(dve, "f", p, r, m, heads)

        def decay_b_step(pool, p, r, m):
            decay_step(pool, "b", p, r, m)


        def values_pe(pe, phase, first_slab, groups, o, norm=None):
            s0 = start[phase] + first_slab
            for g in range(groups):
                bank_free(pe, o + 2 * g)
                bank_free(pe, o + 2 * g + 1)
                for part in range(2):
                    multiply_tokens(pe, s0 + 2 * g + part, o + 2 * g, part, norm=norm if g == 0 else None)

        def values_act(act, phase, first_slab, groups, o, dst):
            s0 = start[phase] + first_slab
            for g in range(groups):
                act.wait_ge(slab_used, s0 + 2 * g + 2)
                for t in range(TT):
                    act.activation(dst[:, t, g * 256:(g + 1) * 256], psum[(o + 2 * g + t) % 4][:, 0:256], ACT.Copy)\
                        .then_inc(freed_a, 1)
                for part in range(2):
                    split_hi(act, s0 + 2 * g + part + AHEAD)

        def hg_forget_act(act, s, o, n, d):
            act.wait_ge(slab_used, s + 1)
            if n >= 2:
                act.wait_ge(f_ready, n - 1)
            act.activation(hg_sig[d][n % 2], psum[o % 4][:, 0:T], ACT.Sigmoid).then_inc(freed_a, 1)

        def hgc_pe(pe):
            phase = "hg_c"
            s0, o0 = start[phase], first_tile[phase]
            values_pe(pe, phase, 0, 4, o0, norm=4)
            for h in range(HG_HEADS + 1):
                if h < HG_HEADS:
                    for d in range(2):
                        k = 8 + 2 * h + d
                        bank_free(pe, o0 + k)
                        multiply(pe, s0 + k, o0 + k, h_hi, h_lo)
                if h >= 1:
                    g = h - 1
                    pe.wait_ge(kd_ready, g + 1)
                    pe.wait_ge(kd_ready_b, g + 1)
                    if g:
                        pe.wait_ge(kt_ready, g)
                    for d in range(2):
                        for t in range(TT):
                            mm = pe.transpose(psum[TURN][:, (2 * d + t) * P:(2 * d + t + 1) * P],
                                              hg_r[d][:, t * P:(t + 1) * P], K("ident"))
                    mm.then_inc(kt_done, 1)
                    pe.wait_ge(kt_ready, g + 1)
                    if g:
                        pe.wait_ge(state_ready, g)
                    for d in range(2):
                        for t in range(TT):
                            mm = pe.matmul(psum[SUMS][:, d * P:(d + 1) * P], hg_kt[:, 2 * d + t, :],
                                           hg_v[:, t, g * P:(g + 1) * P], start=t == 0, stop=t == TT - 1)
                    mm.then_inc(state_done, 1)

        def hgc_act(act):
            phase = "hg_c"
            s0, o0 = start[phase], first_tile[phase]
            values_act(act, phase, 0, 4, o0, hg_v)
            for h in range(HG_HEADS + 1):
                if h < HG_HEADS:
                    for d in range(2):
                        k = 8 + 2 * h + d
                        hg_forget_act(act, s0 + k, o0 + k, h, d)
                        split_hi(act, s0 + k + AHEAD)
                if h >= 1:
                    g = h - 1
                    act.wait_ge(kt_done, g + 1)
                    if g:
                        act.wait_ge(state_done, g)
                    act.activation(hg_kt, psum[TURN][:].rearrange("p (b q) -> p b q", q=P), ACT.Copy)\
                        .then_inc(kt_ready, 1)
                    act.wait_ge(state_done, g + 1)
                    act.activation(hg_s[:, g, :, :], psum[SUMS][:, 0:2 * P].rearrange("p (d v) -> p d v", v=P), ACT.Copy)\
                        .then_inc(state_ready, 1)

        def hg_start_head(dve, link, h, n, o_f, o_b):
            if 2 <= n < HG_HEADS + 2:
                dve.wait_ge(kd_ready_b, min(n - 1, HG_HEADS))
            for d, o in ((0, o_f), (1, o_b)):
                dve.wait_ge(*freed_by(o))
                link(dve.tensor_scalar(hg_p[d][n % 2][:], hg_sig[d][n % 2], lb[:, 3, h:h + 1], lb[:, 2, h:h + 1],
                                       ALU.mult, ALU.add))
                ins = dve.tensor_scalar(hg_k[d][n % 2][:], hg_p[d][n % 2][:], -1.0, 1.0, ALU.mult, ALU.add)
            ins.then_inc(f_ready, 1)

        def hgc_dve(dve, link):
            phase = "hg_c"
            s0, o0 = start[phase], first_tile[phase]
            for k in range(8):
                split_lo(dve, s0 + k + AHEAD)
            for h in range(HG_HEADS):
                k = 8 + 2 * h
                hg_start_head(dve, link, h, h, o0 + k, o0 + k + 1)
                dve.wait_ge(f_ready, h + 1)
                if h:
                    dve.wait_ge(kt_done, h)
                link(dve.memset(hg_r[0][:], 1.0))
                for m in STEPS[:4]:
                    decay_f_step(dve, hg_p[0][h % 2][:], hg_r[0][:], m)
                split_lo(dve, s0 + k + AHEAD)
                for m in STEPS[4:]:
                    decay_f_step(dve, hg_p[0][h % 2][:], hg_r[0][:], m)
                dve.tensor_tensor(hg_r[0][:], hg_r[0][:], hg_k[0][h % 2][:], ALU.mult).then_inc(kd_ready, 1)
                split_lo(dve, s0 + k + 1 + AHEAD)

        def hgc_pool(pool):
            for h in range(HG_HEADS):
                pool.wait_ge(f_ready, h + 1)
                if h:
                    pool.wait_ge(kt_done, h)
                pool.memset(hg_r[1][:], 1.0).then_inc(r_set, 1)
                pool.wait_ge(r_set, h + 1)
                for m in STEPS:
                    decay_b_step(pool, hg_p[1][h % 2][:], hg_r[1][:], m)
                pool.tensor_tensor(hg_r[1][:], hg_r[1][:], hg_k[1][h % 2][:], ALU.mult).then_inc(kd_ready_b, 1)

        PARTS = [(0, 1), (2, 3), (4, 5, 6), (7, 8, 9)]
        LV = 9

        def hgx_unit_pe(pe, h, l):
            n = HG_HEADS + h
            q = hg_q[n % 2]
            if l < LV:
                a = LV * h + l
                pe.wait_ge(uw_ready, 10 * h + l + 1)
                if l >= 2 or h:
                    pe.wait_ge(a_ready, a - 1)
                for c in range(TT):
                    other = 1 - c if l == 8 else c
                    u = (q if l == 0 else hg_u[l % 2])[:, other * P:(other + 1) * P]
                    mm = pe.matmul(psum[4 + a % 2][:, c * P:(c + 1) * P], hg_w[l % 2][:, c * P:(c + 1) * P], u,
                                   start=True, stop=True)
                mm.then_inc(a_done, 1)
            if 1 <= l:
                a = LV * h + l - 1
                pe.wait_ge(a_ready, a + 1)
                if l == 1 and h:
                    pe.wait_ge(lin_norm, h)
                for c in range(TT):
                    to = 1 - c if l - 1 == 8 else c
                    mm = pe.matmul(psum[SUMS][:, to * P:(to + 1) * P], hg_v[:, c, h * P:(h + 1) * P],
                                   hg_a[a % 2][:, c, :], start=l == 1 and c == 0, stop=False, skip_group_check=True)
                mm.then_inc(pv_done, 1)
            if l == LV:
                pe.wait_ge(uw_ready, 10 * h + 10)
                for d in range(2):
                    mm = pe.matmul(psum[SUMS][:, 0:T], hg_s[:, h, d, :], hg_u[d][:], start=False, stop=d == 1,
                                   skip_group_check=True)
                mm.then_inc(pv_done, 1)

        def hgx_sum_pe(pe, h):
            pe.wait_ge(lin_sq, h + 1)
            if h:
                pe.wait_ge(lin_rms, h)
            pe.matmul(psum[TURN][:, 0:T], K("ones"), hg_sq[:], start=True, stop=True).then_inc(lin_sum, 1)

        def hgx_pe(pe):
            phase = "hg_x"
            s0, o0 = start[phase], first_tile[phase]
            values_pe(pe, phase, 0, 4, o0, norm=5)
            for h in range(HG_HEADS + 1):
                for part in range(4):
                    if h < HG_HEADS:
                        k = 8 + 4 * h + part
                        bank_free(pe, o0 + k)
                        multiply(pe, s0 + k, o0 + k, h_hi, h_lo)
                    if h >= 2 and part == 0:
                        hgx_sum_pe(pe, h - 2)
                    if h >= 1:
                        if h == 1 and part == 0:
                            pe.wait_ge(*freed_by(o0 + 7))
                            pe.wait_ge(state_ready, HG_HEADS)
                        for l in PARTS[part]:
                            hgx_unit_pe(pe, h - 1, l)
            hgx_sum_pe(pe, HG_HEADS - 1)

        def hgx_unit_dve(dve, link, h, l):
            n = HG_HEADS + h
            q, kf, kb = hg_q[n % 2], hg_k[0][n % 2], hg_k[1][n % 2]
            pf, pb, rf, rb = hg_p[0][n % 2], hg_p[1][n % 2], hg_r[0], hg_r[1]
            if l == 0:
                dve.wait_ge(*freed_by(first_tile["hg_x"] + 8 + 4 * h + 3))
                if h == 0:
                    dve.wait_ge(kt_done, HG_HEADS)
                if h:
                    dve.wait_ge(pv_done, 10 * h)
                link(dve.memset(rf[:], 1.0))
                dve.tensor_tensor(hg_w[0][:], kf[:], kb[:], ALU.add).then_inc(uw_ready, 1)
            else:
                if l >= 2:
                    decay_f_step(dve, pf[:], rf[:], STEPS[l - 2])
                    dve.wait_ge(decay_b, 2 * (NSTEP * (HG_HEADS + h) + l - 1))
                if l == 1:
                    dve.wait_ge(r_set, HG_HEADS + h + 1)
                if l >= 2:
                    dve.wait_ge(a_done, LV * h + l - 1)
                if l == LV:
                    dve.wait_ge(a_done, LV * h + LV)
                    dve.tensor_tensor(hg_u[0][:], q[:], pf[:], ALU.mult)
                    dve.tensor_tensor(hg_u[1][:], q[:], pb[:], ALU.mult).then_inc(uw_ready, 1)
                else:
                    m = STEPS[l - 1]

                    def half(x, c):
                        return x[:].rearrange("p (b c m) -> p b c m", c=2, m=m)[:, :, c, :]

                    u, w = hg_u[l % 2], hg_w[l % 2]
                    dve.tensor_tensor(half(u, 1), half(q, 1), half(pf, 1), ALU.mult)
                    dve.tensor_tensor(half(u, 0), half(q, 0), half(pb, 0), ALU.mult)
                    dve.tensor_tensor(half(w, 0), half(kf, 0), half(rf, 0), ALU.mult)
                    dve.tensor_tensor(half(w, 1), half(kb, 1), half(rb, 1), ALU.mult).then_inc(uw_ready, 1)
            if l >= 1:
                a = LV * h + l - 1
                dve.wait_ge(a_done, a + 1)
                if a >= 2:
                    dve.wait_ge(pv_done, 10 * ((a - 2) // LV) + (a - 2) % LV + 1)
                at = psum[4 + a % 2][:, 0:T].rearrange("p (c t) -> p c t", t=P)
                if l - 1 == 8:
                    ins = dve.tensor_copy(hg_a[a % 2][:], at)
                else:
                    mask = K("both")[:, (l - 1) * P:l * P].unsqueeze(1).to_broadcast([P, TT, P])
                    ins = dve.tensor_tensor(hg_a[a % 2][:], at, mask, ALU.mult)
                ins.then_inc(a_ready, 1)

        def hgx_out_dve(dve, link, h):
            n = HG_HEADS + h
            dve.wait_ge(lin_rms, h + 1)
            link(dve.reciprocal(rstd[:], hg_root[:]))
            dve.scalar_tensor_tensor(conv[0][:], psum[SUMS][:, 0:T], V("o_gain"), rstd[:], ALU.mult, ALU.mult)\
                .then_inc(lin_norm, 1)
            dve.wait_ge(lin_norm, h + 1)
            dve.tensor_tensor(prod[0][:], conv[0][:], hg_g[n % 2][:], ALU.mult).then_inc(lin_gated, 1)
            dve.wait_ge(lin_hi, h + 1)
            dve.tensor_tensor(hg_o_lo[:, h, :], prod[0][:], hg_o_hi[:, h, :], ALU.subtract).then_inc(lin_ready, 1)

        def hgx_dve(dve, link):
            phase = "hg_x"
            s0, o0 = start[phase], first_tile[phase]
            dve.wait_ge(con_in, 32)
            for k in range(8):
                split_lo(dve, s0 + k + AHEAD)
            for h in range(HG_HEADS + 1):
                n = HG_HEADS + h
                for part in range(4):
                    if h >= 1:
                        if part == 0 and h >= 2:
                            hgx_out_dve(dve, link, h - 2)
                        for l in PARTS[part]:
                            hgx_unit_dve(dve, link, h - 1, l)
                    if h < HG_HEADS:
                        k = 8 + 4 * h + part
                        split_lo(dve, s0 + k + AHEAD)
                        if part == 3:
                            hg_start_head(dve, link, h, n, o0 + k - 3, o0 + k - 2)
            hgx_out_dve(dve, link, HG_HEADS - 1)

        def hgx_act(act):
            phase = "hg_x"
            s0, o0 = start[phase], first_tile[phase]
            act.wait_ge(state_done, HG_HEADS)
            values_act(act, phase, 0, 4, o0, hg_v)
            for h in range(HG_HEADS + 1):
                n = HG_HEADS + h
                if h < HG_HEADS:
                    for part in range(4):
                        k = 8 + 4 * h + part
                        if part < 2:
                            hg_forget_act(act, s0 + k, o0 + k, n, part)
                        else:
                            act.wait_ge(slab_used, s0 + k + 1)
                            if h >= 2:
                                act.wait_ge(pv_done, 10 * (h - 1))
                                act.wait_ge(lin_gated, h - 1)
                            dst = hg_q if part == 2 else hg_g
                            act.activation(dst[n % 2][:], psum[(o0 + k) % 4][:, 0:T], ACT.Silu).then_inc(freed_a, 1)
                        if h >= 2 and part == 0:
                            hgx_out_act(act, h - 2)
                        split_hi(act, s0 + k + AHEAD)
                if h == HG_HEADS:
                    hgx_out_act(act, h - 2)
                    hgx_out_act(act, h - 1)

        def hgx_out_act(act, h):
            act.wait_ge(pv_done, 10 * h + 10)
            act.activation(hg_sq[:], psum[SUMS][:, 0:T], ACT.Square).then_inc(lin_sq, 1)
            act.wait_ge(lin_sum, h + 1)
            act.activation(hg_root[:], psum[TURN][:, 0:T], ACT.Sqrt, bias=eps[:], scale=1.0 / P).then_inc(lin_rms, 1)
            act.wait_ge(lin_gated, h + 1)
            act.activation(hg_o_hi[:, h, :], prod[0][:], ACT.Copy).then_inc(lin_hi, 1)

        def hgx_pool(pool):
            for h in range(HG_HEADS):
                n = HG_HEADS + h
                pool.wait_ge(f_ready, n + 1)
                if h == 0:
                    pool.wait_ge(kt_done, HG_HEADS)
                else:
                    pool.wait_ge(pv_done, 10 * h)
                pool.memset(hg_r[1][:], 1.0).then_inc(r_set, 1)
                pool.wait_ge(r_set, n + 1)
                for l in range(2, 10):
                    pool.wait_ge(uw_ready, 10 * h + l)
                    decay_b_step(pool, hg_p[1][n % 2][:], hg_r[1][:], STEPS[l - 2])

        UG = 17
        DG = 15
        UNITS_G = [(l, c) for l in range(8) for c in range(TT)] + [(8, 0)]

        def gla_pe(pe, n):
            phase = f"b{n}_gla"
            s0, o0 = start[phase], first_tile[phase]
            for m in range(9):
                bank_free(pe, o0 + m)
                multiply(pe, s0 + m, o0 + m, h_hi, h_lo)
                if m == 1:
                    pe.wait_ge(*freed_by(o0))
                    for h in range(GLA_HEADS):
                        w = V("gla_gate")[0:GLA_RANK, (GLA_HEADS * n + h) * P:(GLA_HEADS * n + h + 1) * P]
                        mm = pe.matmul(psum[4 + h // 2][:, (h % 2) * T:(h % 2 + 1) * T], w, gl_lr[0:GLA_RANK, :],
                                       start=True, stop=True)
                    mm.then_inc(z_done, 1)
            values_pe(pe, phase, 9, 4, o0 + 9)
            for o in range(o0 + 13, o0 + 17):
                pe.wait_ge(*freed_by(o))
            for j in range(UG + 1):
                if j < UG:
                    l, c = UNITS_G[j]
                    a = UG * n + j
                    to = 1 if l == 8 else c
                    if l:
                        pe.wait_ge(uw_ready, 10 * HG_HEADS + DG * n + j - 1)
                        pe.wait_ge(w_ready, DG * n + j - 1)
                    else:
                        pe.wait_ge(*freed_by(o0 + 8))
                        pe.wait_ge(z_min, GLA_HEADS * (n + 1))
                    if j >= 2:
                        pe.wait_ge(a_ready, LV * HG_HEADS + a - 1)
                    for h in range(GLA_HEADS):
                        if l == 0:
                            w, u = gl_k[:, h, c * P:(c + 1) * P], gl_q[:, h, c * P:(c + 1) * P]
                        else:
                            w, u = gl_w[j % 2][:, h, :], gl_u[j % 2][:, h, :]
                        mm = pe.matmul(psum[4 + j % 2][:, h * P:(h + 1) * P], w, u, start=True, stop=True)
                    mm.then_inc(a_done, 1)
                if j >= 1:
                    l, c = UNITS_G[j - 1]
                    a = UG * n + j - 1
                    to = 1 if l == 8 else c
                    pe.wait_ge(a_ready, LV * HG_HEADS + a + 1)
                    for f in range(2 * GLA_HEADS):
                        mm = pe.matmul(psum[f // 2][:, (f % 2) * T + to * P:(f % 2) * T + (to + 1) * P],
                                       gl_v[:, c, f * P:(f + 1) * P], gl_a[(j - 1) % 2][:, f // 2, :],
                                       start=j == 1 and f % 2 == 0, stop=j == UG, skip_group_check=True)
                    mm.then_inc(pv_done, 1)
            for h in range(GLA_HEADS):
                v = HG_HEADS + GLA_HEADS * n + h
                pe.wait_ge(lin_sq, v + 1)
                pe.wait_ge(lin_rms, v)
                for d in range(2):
                    mm = pe.matmul(psum[SUMS][:, 0:T], K("ones"), gl_sq[h % 2][:, d * T:(d + 1) * T], start=d == 0,
                                   stop=d == 1)
                mm.then_inc(lin_sum, 1)
            pe.wait_ge(lin_norm, HG_HEADS + 2 * GLA_HEADS * (n + 1))

        def gla_act(act, n):
            phase = f"b{n}_gla"
            s0, o0 = start[phase], first_tile[phase]
            for m in range(9):
                split_hi(act, s0 + m + AHEAD)
                if m == 2:
                    act.wait_ge(z_done, n + 1)
                    for h in range(GLA_HEADS):
                        act.activation(gl_r[:, h, :], psum[4 + h // 2][:, (h % 2) * T:(h % 2 + 1) * T], ACT.Abs,
                                       bias=V("gla_bias")[:, GLA_HEADS * n + h:GLA_HEADS * n + h + 1]).then_inc(z_abs, 1)
                    act.wait_ge(z_abs, GLA_HEADS * (n + 1))
                    act.activation(gl_r[:], gl_r[:], ACT.Exp, scale=-1.0).then_inc(z_exp, 1)
                    act.wait_ge(z_exp, 2 * n + 1)
                    act.activation(gl_r[:], gl_r[:], ACT.Ln, bias=1.0).then_inc(z_ln, 1)
                    act.wait_ge(z_sub, n + 1)
                    act.activation(gl_p[:], gl_p[:], ACT.Exp, scale=1.0 / GLA_TAU).then_inc(z_exp, 1)
            values_act(act, phase, 9, 4, o0 + 9, gl_v)
            for h in range(GLA_HEADS):
                v = HG_HEADS + GLA_HEADS * n + h
                act.wait_ge(pv_done, 10 * HG_HEADS + UG * (n + 1))
                if h >= 2:
                    act.wait_ge(lin_sum, v - 1)
                act.activation(gl_sq[h % 2], psum[h][:], ACT.Square).then_inc(lin_sq, 1)
                if h >= 1:
                    gla_root(act, n, h - 1)
            gla_root(act, n, GLA_HEADS - 1)

        def gla_root(act, n, h):
            v = HG_HEADS + GLA_HEADS * n + h
            act.wait_ge(lin_sum, v + 1)
            if h >= 2:
                act.wait_ge(lin_norm, HG_HEADS + 2 * GLA_HEADS * n + 2 * (h - 1))
            act.activation(gate[h % 2][:], psum[SUMS][:, 0:T], ACT.Sqrt, bias=eps[:], scale=1.0 / (2 * P))\
                .then_inc(lin_rms, 1)

        def gla_dve(dve, link, n):
            phase = f"b{n}_gla"
            s0, o0 = start[phase], first_tile[phase]
            for m in range(9):
                dve.wait_ge(slab_used, s0 + m + 1)
                bank = psum[(o0 + m) % 4][:, 0:T]
                if m == 0:
                    ins = dve.tensor_copy(gl_lr[:], bank)
                elif m <= GLA_HEADS:
                    ins = dve.tensor_scalar(gl_q[:, m - 1, :], bank, P ** -0.5, None, ALU.mult)
                else:
                    ins = dve.tensor_copy(gl_k[:, m - 1 - GLA_HEADS, :], bank)
                ins.then_inc(freed_v, 1)
                split_lo(dve, s0 + m + AHEAD)
                if m == 2:
                    dve.wait_ge(z_done, n + 1)
                    dve.wait_ge(z_abs, GLA_HEADS * (n + 1))
                    for h in range(GLA_HEADS):
                        dve.tensor_scalar(gl_p[:, h, :], psum[4 + h // 2][:, (h % 2) * T:(h % 2 + 1) * T],
                                          V("gla_bias")[:, GLA_HEADS * n + h:GLA_HEADS * n + h + 1], 0.0, ALU.add, ALU.min)\
                            .then_inc(z_min, 1)
                    dve.wait_ge(z_min, GLA_HEADS * (n + 1))
                    dve.wait_ge(z_ln, n + 1)
                    dve.tensor_tensor(gl_p[:], gl_p[:], gl_r[:], ALU.subtract).then_inc(z_sub, 1)
            for k in range(8):
                split_lo(dve, s0 + 9 + k + AHEAD)
            for j in range(UG + 1):
                if j < UG:
                    l, c = UNITS_G[j]
                    a = UG * n + j
                    if j == 0:
                        dve.wait_ge(z_exp, 2 * n + 2)
                        dve.wait_ge(freed_v, freed[o0 + 8][1])
                        link(dve.memset(gl_r[:], 1.0))
                    if l >= 2 and c == 0:
                        dve.wait_ge(w_ready, DG * n + j - 2)
                        decay_f_step(dve, gl_p, gl_r, STEPS[l - 2], heads=True)
                    if l:
                        if j >= 4:
                            dve.wait_ge(a_done, LV * HG_HEADS + a - 1)
                        to = 1 if l == 8 else c
                        dve.tensor_tensor(gl_u[j % 2][:], gl_q[:, :, to * P:(to + 1) * P],
                                          gl_p[:, :, to * P:(to + 1) * P], ALU.mult).then_inc(uw_ready, 1)
                if j >= 1:
                    l, c = UNITS_G[j - 1]
                    a = UG * n + j - 1
                    dve.wait_ge(a_done, LV * HG_HEADS + a + 1)
                    if j >= 3:
                        dve.wait_ge(pv_done, 10 * HG_HEADS + a - 1)
                    at = psum[4 + (j - 1) % 2][:].rearrange("p (h t) -> p h t", t=P)
                    if l == 8:
                        ins = dve.tensor_copy(gl_a[(j - 1) % 2][:], at)
                    else:
                        mask = K("causal")[:, l * P:(l + 1) * P].unsqueeze(1).to_broadcast([P, GLA_HEADS, P])
                        ins = dve.tensor_tensor(gl_a[(j - 1) % 2][:], at, mask, ALU.mult)
                    ins.then_inc(a_ready, 1)
            for h in range(GLA_HEADS):
                v = HG_HEADS + GLA_HEADS * n + h
                dve.wait_ge(lin_rms, v + 1)
                if h:
                    dve.wait_ge(lin_norm, HG_HEADS + 2 * GLA_HEADS * n + 2 * h)
                link(dve.reciprocal(rstd[:], gate[h % 2][:]))
                for d in range(2):
                    f = 2 * h + d
                    g = V("gla_norm")[:, KD * n + f:KD * n + f + 1]
                    dve.scalar_tensor_tensor(ob[:, f, :], psum[h][:, d * T:(d + 1) * T], g, rstd[:], ALU.mult,
                                             ALU.mult).then_inc(lin_norm, 1)

        def gla_pool(pool, n):
            for j in range(TT, UG):
                l, c = UNITS_G[j]
                a = UG * n + j
                pool.wait_ge(uw_ready, 10 * HG_HEADS + DG * n + j - 1)
                if j >= 4:
                    pool.wait_ge(a_done, LV * HG_HEADS + a - 1)
                pool.tensor_tensor(gl_w[j % 2][:], gl_k[:, :, c * P:(c + 1) * P], gl_r[:, :, c * P:(c + 1) * P],
                                   ALU.mult).then_inc(w_ready, 1)

        def r_act(act, n):
            phase = f"b{n}_r"
            s0, o0 = start[phase], first_tile[phase]
            for j in range(KD):
                act.wait_ge(slab_used, s0 + j + 1)
                act.activation(gate[j % 2][:], psum[(o0 + j) % 4][:, 0:T], ACT.Silu).then_inc(mix_sig, 1)
                split_hi(act, s0 + j + AHEAD)
                act.wait_ge(*freed_by(o0 + j))
                act.activation(ob_hi[:, j, :], prod[j % 2][:], ACT.Copy).then_inc(mix_hi, 1)

        def r_dve(dve, link, n):
            phase = f"b{n}_r"
            s0, o0 = start[phase], first_tile[phase]
            for j in range(KD):
                u = 3 * KD * n + j
                dve.wait_ge(mix_sig, u + 1)
                dve.tensor_tensor(prod[j % 2][:], ob[:, j, :], gate[j % 2][:], ALU.mult).then_inc(freed_v, 1)
                split_lo(dve, s0 + j + AHEAD)
                dve.wait_ge(mix_hi, 2 * KD * n + j + 1)
                dve.tensor_tensor(ob_lo[:, j, :], prod[j % 2][:], ob_hi[:, j, :], ALU.subtract).then_inc(mix_ready, 1)

        def merge_pe(pe, n, ot_end):
            phase = f"b{n}_merge"
            s0, o0 = start[phase], first_tile[phase]
            pe.wait_ge(ot_ready, ot_end)
            for j in range(KD):
                for m, (hi, lo, blocks) in enumerate(((h_hi, h_lo, KD), (oa_hi, oa_lo, 4), (h_hi, h_lo, KD),
                                                      (ob_hi, ob_lo, KD))):
                    k = 4 * j + m
                    if j == 0 and m == 3:
                        pe.wait_ge(mix_ready, 2 * KD * n + KD)
                    bank_free(pe, o0 + k)
                    multiply(pe, s0 + k, o0 + k, hi, lo, blocks=blocks)

        def merge_act(act, n):
            phase = f"b{n}_merge"
            s0, o0 = start[phase], first_tile[phase]
            for j in range(KD):
                for m in range(2):
                    k = 4 * j + 2 * m
                    act.wait_ge(slab_used, s0 + k + 1)
                    if k >= 4:
                        act.wait_ge(*freed_by(o0 + k - 3))
                    act.activation(gate[m][:], psum[(o0 + k) % 4][:, 0:T], ACT.Sigmoid).then_inc(mix_sig, 1)
                    split_hi(act, s0 + k + AHEAD)
                    split_hi(act, s0 + k + 1 + AHEAD)
                act.wait_ge(mix_sum, KD * n + j + 1)
                act.activation(mg_hi[:, j, :], conv[j % 2][:], ACT.Copy).then_inc(mix_hi, 1)

        def merge_dve(dve, link, n):
            phase = f"b{n}_merge"
            s0, o0 = start[phase], first_tile[phase]
            for j in range(KD):
                for m in range(2):
                    k = 4 * j + 2 * m
                    dve.wait_ge(mix_sig, 3 * KD * n + KD + 2 * j + m + 1)
                    dve.wait_ge(slab_used, s0 + k + 2)
                    dve.tensor_tensor(prod[m][:], psum[(o0 + k + 1) % 4][:, 0:T], gate[m][:], ALU.mult)\
                        .then_inc(freed_v, 2)
                    split_lo(dve, s0 + k + AHEAD)
                    split_lo(dve, s0 + k + 1 + AHEAD)
                dve.wait_ge(*freed_by(o0 + 4 * j + 3))
                dve.tensor_tensor(conv[j % 2][:], prod[0][:], prod[1][:], ALU.add).then_inc(mix_sum, 1)
                dve.wait_ge(mix_hi, 2 * KD * n + KD + j + 1)
                dve.tensor_tensor(mg_lo[:, j, :], conv[j % 2][:], mg_hi[:, j, :], ALU.subtract).then_inc(mix_ready, 1)

        def att_units(t_set):
            units = []
            for j, pair in enumerate(PAIRS):
                for part, head in enumerate(pair):
                    rows = slice(part * HD, (part + 1) * HD)
                    kv = head // 4
                    keys = slice(0, 2 * T) if t_set == X else slice(T, 2 * T)
                    first = 0 if t_set == X else TT
                    for t in range(TT):
                        masks = [] if t_set == C else [(1 - t, f"win{t}")]
                        v = [att_v[:, b, kv * HD:(kv + 1) * HD] for b in range(first, 2 * TT)]
                        units.append((att_q[t_set][rows, j, t * P:(t + 1) * P], att_k[rows, j // 4, keys], masks, v,
                                      V("sink")[:, head:head + 1], nsink[:, head:head + 1],
                                      att_o[:, TT * t_set + t, j * P + part * HD:j * P + (part + 1) * HD]))
            return units

        def swa_units(n):
            units = []
            for j, pair in enumerate(SWA_PAIRS):
                for part, head in enumerate(pair):
                    rows = slice(part * HD, (part + 1) * HD)
                    col = 8 * n + head
                    for t in range(TT):
                        masks = [(0, "swa_cur")] if t == 0 else [(0, "swa_prev"), (1, "swa_cur")]
                        v = [swa_v[:, b, part * HD:(part + 1) * HD] for b in range(t + 1)]
                        units.append((swa_q[rows, j, t * P:(t + 1) * P], swa_q[rows, 4, 0:(t + 1) * P], masks, v,
                                      V("swa_sink")[:, col:col + 1], nsink[:, 16 + col:17 + col],
                                      swa_o[:, t, j * P + part * HD:j * P + (part + 1) * HD]))
            return units

        ATT = [att_units(X), att_units(C)]
        SWA = [swa_units(0), swa_units(1)]
        N_ATT, N_SWA = len(ATT[0]), len(SWA[0])

        def att_dst(t):
            return lambda m: att_q[t][:, m, :] if m < KD else att_k[:, m - KD, t * T:(t + 1) * T]

        def swa_dst(m):
            return swa_q[:, m, :]

        def shift(layer, norm, t):
            return lambda k: mod[:, layer, 8 * (3 * norm) + k, t:t + 1]

        def scale(layer, norm, t):
            return lambda k: mod_g[:, layer, norm, t, k:k + 1]

        def branch(layer, norm, t):
            return lambda k: mod[:, layer, 8 * (3 * norm + 2) + k, t:t + 1]

        def gains(name, n):
            return lambda k: V(name)[:, KD * n + k:KD * n + k + 1]

        last = {p: first_tile[p] for p in first_tile}

        block = ctx.enter_context(nc.Block())

        @block.sync
        def _(sp):
            sp.dma_start(vec[:], dram["vec"]).then_inc(params_in, 16)
            for p in range(RAW):
                load(sp, p)
            sp.dma_start(res[X][:], dram["x"]).then_inc(x_in, 16)
            for p in range(RAW, len(panels)):
                load(sp, p)
                if p == 2 * RAW - 1:
                    sp.dma_start(con[:, 0:CON_EARLY], dram["con"][:, 0:CON_EARLY]).then_inc(con_in, 16)
                if p == 3 * RAW:
                    sp.dma_start(con[:, CON_EARLY:], dram["con"][:, CON_EARLY:]).then_inc(con_in, 16)
                    sp.dma_start(res[C][:], dram["ctx"]).then_inc(ctx_in, 16)
            for j in range(KD):
                sp.wait_ge(*freed_by(first_tile["b1_ffn2_down"] + j))
                sp.dma_start(out[:, j, :], res[X][:, j, :]).then_inc(out_done, 16)
            sp.wait_ge(out_done, 16 * KD)

        @block.gpsimd
        def _(pool):
            hgc_pool(pool)
            hgx_pool(pool)
            for n in range(2):
                gla_pool(pool, n)

        @block.tensor
        def _(pe):
            pe.wait_ge(c_silu, 1)
            ada_pe(pe, 0, 0, ADA_FIRST)
            pe.wait_ge(con_in, 16)
            ada_turn_pe(pe, 0)
            for t in (X, C):
                norm_pe(pe, t)
                phase = "qkv_" + "xc"[t]
                qk_pe(pe, phase, 10, att_dst(t), "swap16" if t == X else None, 10 * t, 0, att_sq, t,
                      ada_first=12 * t)
                values_pe(pe, phase, 10, 1, first_tile[phase] + 10)
                ada_pe(pe, 1, 12 * t + 10, 2)
            ada_turn_pe(pe, 1)
            for t in (X, C):
                att_pe(pe, ATT[t], N_ATT * t, first_tile["qkv_c"] + 11, probs, probs_t, 1,
                       with_ada=t == X)
                if t == X:
                    ada_turn_pe(pe, 2)
                turn_pe(pe, att_o[:, TT * t:TT * t + TT, :], KD, N_ATT * (t + 1), KD * t)
                pe.wait_ge(ot_ready, KD * (t + 1))
                pe.wait_ge(mod_ready, 3)
                linear_pe(pe, "attn_out_" + "xc"[t], h_hi, h_lo)
            for t in (X, C):
                norm_pe(pe, 2 + t)
                ffn_pe(pe, "ffn0_" + "xc"[t], 2 + t, t)
            norm_pe(pe, 4)
            hgc_pe(pe)
            norm_pe(pe, 5)
            hgx_pe(pe)
            pe.wait_ge(lin_ready, HG_HEADS)
            linear_pe(pe, "hg_out", hg_o_hi, hg_o_lo)
            norm_pe(pe, 6)
            ffn_pe(pe, "ffn1", 6, 2)
            for n in range(2):
                norm_pe(pe, 7 + 3 * n)
                ffn_pe(pe, f"b{n}_ffn1", 7 + 3 * n, 3 + 2 * n)
                norm_pe(pe, 8 + 3 * n)
                phase = f"b{n}_swa"
                qk_pe(pe, phase, 5, swa_dst, "swap32", 20 + 5 * n, 10 + 5 * n, swa_sq, 8 + 3 * n)
                o = first_tile[phase] + 5
                bank_free(pe, o)
                bank_free(pe, o + 1)
                multiply_tokens(pe, start[phase] + 5, o, 0, groups=KD, width=P)
                att_pe(pe, SWA[n], 2 * N_ATT + N_SWA * n, o + 1, swa_p, swa_pt, 2 + n)
                turn_pe(pe, swa_o, 4, 2 * N_ATT + N_SWA * (n + 1), 2 * KD + 4 * n)
                pe.wait_ge(ot_ready, 2 * KD + 4 * (n + 1))
                gla_pe(pe, n)
                linear_pe(pe, f"b{n}_r", h_hi, h_lo)
                merge_pe(pe, n, 2 * KD + 4 * (n + 1))
                pe.wait_ge(mix_ready, 2 * KD * (n + 1))
                linear_pe(pe, f"b{n}_out", mg_hi, mg_lo)
                norm_pe(pe, 9 + 3 * n)
                ffn_pe(pe, f"b{n}_ffn2", 9 + 3 * n, 4 + 2 * n)

        @block.scalar
        def _(act):
            act.wait_ge(params_in, 16)
            act.wait_ge(c_clear, 1)
            act.activation(c_wide[:, :, WIDE:WIDE + 2], c_in, ACT.Silu).then_inc(c_silu, 1)
            act.wait_ge(lb_top, 1)
            act.activation(lb[:, 0:2, :], lb[:, 0:2, :], ACT.Exp).then_inc(lb_exp, 1)
            for k in range(AHEAD):
                split_hi(act, k)
            for t in (X, C):
                phase = "qkv_" + "xc"[t]
                norm_act(act, t, t, None, shift(0, 0, t), start[phase], mod_parts=1)
                qk_act(act, phase, 10, 10 * t, att_sq, att_root)
                for k in (10, 11):
                    split_hi(act, start[phase] + k + AHEAD)
            for t in (X, C):
                att_act(act, ATT[t], N_ATT * t, probs, probs_t)
                turn_act(act, h_hi, KD, KD * t)
                for k in range(KD):
                    split_hi(act, start["attn_out_" + "xc"[t]] + k + AHEAD)
            for t in (X, C):
                phase = "ffn0_" + "xc"[t]
                norm_act(act, 2 + t, t, first_tile["attn_out_" + "xc"[t]], shift(0, 1, t), start[phase])
                ffn_up(act, ffn_up_act, phase, t, 0)
                ffn_down_act(act, phase)
            norm_act(act, 4, C, first_tile["ffn0_c_down"], shift(1, 0, C), start["hg_c"])
            hgc_act(act)
            act.wait_ge(f_ready, HG_HEADS)
            norm_act(act, 5, X, first_tile["ffn0_x_down"], shift(1, 0, X), start["hg_x"])
            hgx_act(act)
            for k in range(KD):
                split_hi(act, start["hg_out"] + k + AHEAD)
            norm_act(act, 6, X, first_tile["hg_out"], shift(1, 1, X), start["ffn1"])
            ffn_up(act, ffn_up_act, "ffn1", 2, 1)
            ffn_down_act(act, "ffn1")
            before = "ffn1_down"
            for n in range(2):
                norm_act(act, 7 + 3 * n, X, first_tile[before], None, start[f"b{n}_ffn1"])
                ffn_up(act, ffn_up_act, f"b{n}_ffn1", 3 + 2 * n, None)
                ffn_down_act(act, f"b{n}_ffn1")
                norm_act(act, 8 + 3 * n, X, first_tile[f"b{n}_ffn1_down"], None, start[f"b{n}_swa"])
                qk_act(act, f"b{n}_swa", 5, 20 + 5 * n, swa_sq, swa_root)
                split_hi(act, start[f"b{n}_swa"] + 5 + AHEAD)
                att_act(act, SWA[n], 2 * N_ATT + N_SWA * n, swa_p, swa_pt)
                turn_act(act, oa_hi, 4, 2 * KD + 4 * n)
                gla_act(act, n)
                r_act(act, n)
                merge_act(act, n)
                for k in range(KD):
                    split_hi(act, start[f"b{n}_out"] + k + AHEAD)
                norm_act(act, 9 + 3 * n, X, first_tile[f"b{n}_out"], None, start[f"b{n}_ffn2"])
                ffn_up(act, ffn_up_act, f"b{n}_ffn2", 4 + 2 * n, None)
                ffn_down_act(act, f"b{n}_ffn2")
                before = f"b{n}_ffn2_down"

        @block.vector
        def _(dve):
            steps = [0]

            def link(ins):
                steps[0] += 1
                ins.then_inc(v_step, 1)
                dve.wait_ge(v_step, steps[0])

            dve.memset(c_wide[:], 0.0).then_inc(c_clear, 1)
            dve.memset(eps[:], EPS).then_inc(eps_set, 1)
            dve.wait_ge(params_in, 16)
            nsink_dve(dve, link)
            both = V("lb", "p (l k) -> p l k", dict(l=2))
            link(dve.tensor_tensor(lb[:, 2, :], both[:, 0, :], both[:, 1, :], ALU.max))
            for n in range(2):
                ins = dve.tensor_tensor(lb[:, n, :], both[:, n, :], lb[:, 2, :], ALU.subtract)
            ins.then_inc(lb_top, 1)
            dve.wait_ge(lb_exp, 1)
            link(dve.tensor_tensor(lb[:, 2, :], lb[:, 0, :], lb[:, 1, :], ALU.add))
            link(dve.reciprocal(lb[:, 3, :], lb[:, 2, :]))
            dve.tensor_tensor(lb[:, 0, :], lb[:, 0, :], lb[:, 3, :], ALU.mult)
            link(dve.tensor_tensor(lb[:, 1, :], lb[:, 1, :], lb[:, 3, :], ALU.mult))
            link(dve.tensor_tensor(lb[:, 2, :], lb[:, 0, :], lb[:, 1, :], ALU.add))
            link(dve.tensor_tensor(lb[:, 2, :], lb[:, 2, :], lb[:, 0, :], ALU.subtract))
            link(dve.tensor_scalar(lb[:, 3, :], lb[:, 2, :], -1.0, 1.0, ALU.mult, ALU.add))
            for k in range(AHEAD):
                split_lo(dve, k)
            dve.wait_ge(con_in, 16)
            ada_dve(dve, link, 0)
            for t in (X, C):
                phase = "qkv_" + "xc"[t]
                norm_dve(dve, link, t, t, scale(0, 0, t), shift(0, 0, t))
                rot = ("cos_ax", "sin_ax") if t == X else (None, None)
                qk_dve(dve, link, phase, 10, att_dst(t), lambda m: V("q_gain") if m < KD else V("k_gain"), *rot,
                       10 * t, 0, att_root)
                dve.wait_ge(slab_used, start[phase] + 12)
                for j in range(TT):
                    ins = dve.tensor_copy(att_v[:, TT * t + j, :], psum[(first_tile[phase] + 10 + j) % 4][:, 0:T])
                    ins.then_inc(freed_v, 1)
                for k in (10, 11):
                    split_lo(dve, start[phase] + k + AHEAD)
            ada_dve(dve, link, 1)
            dve.wait_ge(freed_v, freed[first_tile["qkv_c"] + 11][1])
            dve.memset(top4[:], 0.0).then_inc(mixer_in, 1)
            dve.wait_ge(mixer_in, 1)
            for t in (X, C):
                att_dve(dve, link, ATT[t], N_ATT * t)
                if t == X:
                    ada_dve(dve, link, 2)
                turn_dve(dve, h_hi, h_lo, KD, KD * t)
                residual_dve(dve, "attn_out_" + "xc"[t], t, branch(0, 0, t))
            for t in (X, C):
                phase = "ffn0_" + "xc"[t]
                norm_dve(dve, link, 2 + t, t, scale(0, 1, t), shift(0, 1, t))
                ffn_up(dve, ffn_up_dve, phase, t, 0)
                residual_dve(dve, phase + "_down", t, branch(0, 1, t), halves=2)
            norm_dve(dve, link, 4, C, scale(1, 0, C), shift(1, 0, C))
            hgc_dve(dve, link)
            norm_dve(dve, link, 5, X, scale(1, 0, X), shift(1, 0, X))
            hgx_dve(dve, link)
            residual_dve(dve, "hg_out", X, branch(1, 0, X))
            norm_dve(dve, link, 6, X, scale(1, 1, X), shift(1, 1, X))
            ffn_up(dve, ffn_up_dve, "ffn1", 2, 1)
            residual_dve(dve, "ffn1_down", X, branch(1, 1, X), halves=2)
            for n in range(2):
                norm_dve(dve, link, 7 + 3 * n, X, gains("ffn1_norm", n), None)
                ffn_up(dve, ffn_up_dve, f"b{n}_ffn1", 3 + 2 * n, None)
                residual_dve(dve, f"b{n}_ffn1_down", X, lambda k: 0.5, halves=2)
                norm_dve(dve, link, 8 + 3 * n, X, gains("mix_norm", n), None)
                phase = f"b{n}_swa"
                qk_dve(dve, link, phase, 5, swa_dst,
                       lambda m: V("swa_q")[:, n:n + 1] if m < 4 else V("swa_k")[:, n:n + 1], "cos_1d", "sin_1d",
                       20 + 5 * n, 10 + 5 * n, swa_root)
                dve.wait_ge(slab_used, start[phase] + 6)
                for j in range(TT):
                    dve.tensor_copy(swa_v[:, j, :], psum[(first_tile[phase] + 5 + j) % 4][:, 0:P]).then_inc(freed_v, 1)
                split_lo(dve, start[phase] + 5 + AHEAD)
                dve.wait_ge(freed_v, freed[first_tile[phase] + 6][1])
                dve.memset(top4[:], 0.0).then_inc(mixer_in, 1)
                dve.wait_ge(mixer_in, 2 + n)
                att_dve(dve, link, SWA[n], 2 * N_ATT + N_SWA * n)
                turn_dve(dve, oa_hi, oa_lo, 4, 2 * KD + 4 * n)
                gla_dve(dve, link, n)
                r_dve(dve, link, n)
                merge_dve(dve, link, n)
                residual_dve(dve, f"b{n}_out", X, lambda k: 1.0)
                norm_dve(dve, link, 9 + 3 * n, X, gains("ffn2_norm", n), None)
                ffn_up(dve, ffn_up_dve, f"b{n}_ffn2", 4 + 2 * n, None)
                residual_dve(dve, f"b{n}_ffn2_down", X, lambda k: 0.5, halves=2)


def kernel(**inputs):
    import numpy as _np
    import concourse.bacc as _bacc
    from concourse import mybir as _mybir
    from concourse.bass_utils import run_bass_kernel_spmd as _run

    nc = _bacc.Bacc("TRN2", target_bir_lowering=False, num_devices=1)
    host = arrays({k: _np.asarray(v) for k, v in inputs.items()})
    sent, dram = {}, {}
    for name, a in host.items():
        sent[f"in_{name}"] = a
        dram[name] = nc.dram_tensor(f"in_{name}", a.shape, _mybir.dt.from_np(a.dtype), kind="ExternalInput").ap()
    out = nc.dram_tensor("out", (P, KD, T), F32, kind="ExternalOutput").ap()
    build(nc, dram, out)
    r = _run(nc, [sent], core_ids=[0])
    got = r.results[0]["out"]
    return _np.ascontiguousarray(got.transpose(1, 0, 2).reshape(D, T).T)[None]
```

```python
import math
from contextlib import ExitStack

import numpy as np
import concourse.bass as bass
from concourse import mybir

F32 = mybir.dt.float32
F32R = mybir.dt.float32r
ALU = mybir.AluOpType
ACT = mybir.ActivationFunctionType
AX_X = mybir.AxisListType.X

P = 128
D = 1024
KD = D // P
T = 256
TT = T // P
FF = 2816
KF = FF // P
HALF = KF // 2
EPS = 1e-6
HD = 64
NEG = -1.0e30
SCALE = HD ** -0.5
LEVELS = [1, 2, 4, 8, 16, 32, 64]
NL = len(LEVELS) + 1
HG_HEADS = 8
GLA_HEADS = 4
GLA_TAU = 16.0
GLA_RANK = 16

X, C = 0, 1
RAW, RING = 4, 4
SLAB = HALF * P
AHEAD = RING
ADA_FIRST, ADA_QKV, ADA_ATT = 8, 24, 16

VEC = {}
_at = 0
for _name, _width in [
    ("c", 2 * KD), ("ada_b", 2 * 48), ("norm1", 2 * KD), ("norm2", 2 * KD), ("q_gain", 1), ("k_gain", 1),
    ("conv_w", 2 * KF * 3), ("conv_b", 2 * KF), ("lb", 2 * KD), ("o_gain", 1), ("ffn1_norm", 2 * KD),
    ("mix_norm", 2 * KD), ("ffn2_norm", 2 * KD), ("swa_q", 2), ("swa_k", 2), ("gla_bias", 2 * GLA_HEADS),
    ("gla_norm", 2 * KD), ("sink", 16), ("swa_sink", 2 * 8), ("gla_gate", 2 * GLA_HEADS * P),
]:
    VEC[_name] = (_at, _width)
    _at += _width
VEC_W = _at

CON = {}
_at = 0
for _name, _width in [
    ("cos_ax", T), ("sin_ax", T), ("cos_1d", T), ("sin_1d", T), ("ones", P), ("ident", P), ("head_ones", P),
    ("swap16", P), ("swap32", P), ("win0", P), ("win1", P), ("swa_cur", P), ("swa_prev", P),
    ("both", NL * P), ("causal", NL * P),
]:
    CON[_name] = (_at, _width)
    _at += _width
CON_W = _at
CON_EARLY = CON["both"][0]

PAIRS = [(j, 4 + j) for j in range(4)] + [(8 + j, 12 + j) for j in range(4)]
SWA_PAIRS = [(j, 4 + j) for j in range(4)]


def plan():
    slabs, panels, start, ada = [], [], {}, []

    def add_ada(count):
        for n in range(len(ada), len(ada) + count):
            ada.append(len(panels))
            panels.append((f"ada{n // 24}", 2 * (n % 24), 2, None, D))

    def add(phase, array, first, count, width):
        start.setdefault(phase, len(slabs))
        for n in range(0, count, 2):
            here = min(2, count - n)
            panels.append((array, first + n, here, len(slabs), width))
            for k in range(here):
                slabs.append((len(panels) - 1, k, width))
            if len(slabs) == AHEAD:
                add_ada(ADA_FIRST)
            elif AHEAD < len(slabs) <= AHEAD + 24:
                add_ada(2)
            if len(slabs) == AHEAD + 24:
                add_ada(ADA_ATT)

    def ffn(phase, up, down):
        add(phase, up, 0, 2 * KF, D)
        add(phase + "_down", down, 0, 2 * KD, SLAB)

    for t in "xc":
        add("qkv_" + t, "attn_in", 0, 12, D)
    for t in "xc":
        add("attn_out_" + t, "attn_out", 0, KD, D)
    ffn("ffn0_x", "up0", "down0")
    ffn("ffn0_c", "up0", "down0")
    add("hg_c", "hg_v", 0, 8, D)
    add("hg_c", "hg_c", 0, 2 * HG_HEADS, D)
    add("hg_x", "hg_v", 0, 8, D)
    add("hg_x", "hg_x", 0, 4 * HG_HEADS, D)
    add("hg_out", "hg_out", 0, KD, D)
    ffn("ffn1", "up1", "down1")
    for n in range(2):
        ffn(f"b{n}_ffn1", f"b_up1_{n}", f"b_down1_{n}")
        add(f"b{n}_swa", f"b_swa_{n}", 0, 6, D)
        add(f"b{n}_gla", f"b_gla_{n}", 0, 17, D)
        add(f"b{n}_r", f"b_r_{n}", 0, 8, D)
        for j in range(KD):
            add(f"b{n}_merge", f"b_ga_{n}", 2 * j, 2, D)
            add(f"b{n}_merge", f"b_gb_{n}", 2 * j, 2, D)
        add(f"b{n}_out", f"b_out_{n}", 0, KD, D)
        ffn(f"b{n}_ffn2", f"b_up2_{n}", f"b_down2_{n}")
    return slabs, panels, start, ada


def arrays(a):
    def tiles(w):
        k, n = w.shape
        return w.reshape(k // P, P, n // P, P).transpose(2, 1, 0, 3).reshape(n // P, P, k)

    def token_major(w):
        n = w.shape[1]
        return w.reshape(2, 4, P, n // 256, 256).transpose(3, 0, 2, 1, 4).reshape(2 * (n // 256), P, D)

    def down(w):
        return w.reshape(2, HALF, P, KD, P).transpose(3, 0, 2, 1, 4).reshape(2 * KD, P, SLAB)

    def pairs(first, second):
        return np.stack([first, second], 1).reshape(-1, P, first.shape[-1])

    def cat(*parts):
        return np.ascontiguousarray(np.concatenate(parts, 0))

    out = {}
    for n in range(2):
        out[f"ada{n}"] = a["ada_w"][n].reshape(4, 2, P, 12, 512).transpose(3, 0, 2, 1, 4).reshape(48, P, D)
        up = a["ffn_w_up"][n]
        out[f"up{n}"] = pairs(tiles(up[:, :FF]), tiles(up[:, FF:]))
        out[f"down{n}"] = down(a["ffn_w_down"][n])
    w = a["attn_w_in"][0]
    heads = [h for p in PAIRS for h in p]
    q = w[:, :D].reshape(D, 16, HD)[:, heads].reshape(D, D)
    out["attn_in"] = cat(tiles(q), tiles(w[:, D:D + 256]), token_major(w[:, D + 256:]))
    out["attn_out"] = tiles(a["attn_w_out"][0].reshape(16, HD, D)[heads].reshape(D, D))
    w = a["hgrn_w_in"][0]
    q, ff, fb, v, g = (tiles(w[:, n * D:(n + 1) * D]) for n in range(5))
    out["hg_v"] = token_major(w[:, 3 * D:4 * D])
    out["hg_c"] = pairs(ff, fb)
    out["hg_x"] = np.stack([ff, fb, q, g], 1).reshape(-1, P, D)
    out["hg_out"] = tiles(a["hgrn_w_out"][0])
    for n in range(2):
        for k in (1, 2):
            out[f"b_up{k}_{n}"] = pairs(tiles(a[f"ffn{k}_w_gate_2"][n]), tiles(a[f"ffn{k}_w_up_2"][n]))
            out[f"b_down{k}_{n}"] = down(a[f"ffn{k}_w_down_2"][n])
        w = a["w_in_2"][n]
        cut = np.cumsum([0, 512, 128, 128, 512, 512, 1024, 1024, GLA_RANK, 1024, 1024])
        qa, ka, va, qb, kb, vb, rb, lr, ga, gb = (w[:, i:j] for i, j in zip(cut[:-1], cut[1:]))
        heads = [h for p in SWA_PAIRS for h in p]
        qa = qa.reshape(D, 8, HD)[:, heads].reshape(D, 512)
        out[f"b_swa_{n}"] = cat(tiles(qa), tiles(ka), tiles(va))
        wide = np.zeros((D, P), w.dtype)
        wide[:, :GLA_RANK] = lr
        out[f"b_gla_{n}"] = cat(tiles(wide), tiles(qb), tiles(kb), token_major(vb))
        out[f"b_r_{n}"] = tiles(rb)
        pa = a["w_proj_a_2"][n].reshape(8, HD, D)[heads].reshape(512, D)
        short = np.zeros((KD, P, D), w.dtype)
        short[:, :, :512] = tiles(pa)
        out[f"b_ga_{n}"] = pairs(tiles(ga), short)
        out[f"b_gb_{n}"] = pairs(tiles(gb), tiles(a["w_proj_b_2"][n]))
        out[f"b_out_{n}"] = tiles(a["w_out_2"][n])
    out = {k: np.ascontiguousarray(v) for k, v in out.items()}

    vec = np.zeros((P, VEC_W), np.float32)

    def put(name, value):
        at, width = VEC[name]
        vec[:value.shape[0], at:at + width] = value.reshape(value.shape[0], -1)

    def cols(v):
        return np.moveaxis(v.reshape(*v.shape[:-1], -1, P), -1, 0)

    def twice(v):
        return np.moveaxis(np.concatenate([v, v], -1), -1, 0)

    def rows(v):
        return np.broadcast_to(v.reshape(1, -1), (P, v.size))

    put("c", np.stack([cols(a["c"][0]), cols(a["c_ctx"])], -1))
    put("ada_b", cols(a["ada_b"]))
    put("norm1", cols(a["norm1_g"]))
    put("norm2", cols(a["norm2_g"]))
    put("q_gain", twice(a["attn_q_gain"]))
    put("k_gain", twice(a["attn_k_gain"]))
    put("conv_w", cols(a["ffn_conv_w"]).transpose(0, 1, 3, 2))
    put("conv_b", cols(a["ffn_conv_b"]))
    put("lb", cols(a["hgrn_lb_logits"]))
    put("o_gain", cols(a["hgrn_o_gain"]))
    put("ffn1_norm", cols(a["ffn1_norm_2"]))
    put("mix_norm", cols(a["mix_norm_2"]))
    put("ffn2_norm", cols(a["ffn2_norm_2"]))
    put("swa_q", twice(a["swa_q_norm_2"]))
    put("swa_k", twice(a["swa_k_norm_2"]))
    put("gla_bias", cols(a["gla_gate_bias_2"]))
    put("gla_norm", cols(a["gla_out_norm_2"]))
    put("sink", rows(a["attn_sink"]))
    put("swa_sink", rows(a["swa_sinks_2"]))
    put("gla_gate", a["gla_w_gate_2"].transpose(1, 0, 2))
    out["vec"] = vec
    out["con"] = constants()
    for name in ("x", "ctx"):
        out[name] = np.ascontiguousarray(a[name][0].T.reshape(KD, P, T).transpose(1, 0, 2))
    return out


def constants():
    con = np.zeros((P, CON_W), np.float32)

    def put(name, value):
        at, width = CON[name]
        con[:, at:at + width] = value.reshape(P, width)

    tok = np.arange(T, dtype=np.float32)
    d = np.arange(P) % HD
    inv = (10000.0 ** (-(np.arange(16, dtype=np.float32) / 16))).astype(np.float32)
    place = np.where(d[:, None] < 32, (tok // 64)[None], (tok % 64)[None]).astype(np.float32)
    ang = place * inv[d % 16][:, None]
    sign = np.where(d % 32 < 16, -1.0, 1.0)[:, None]
    put("cos_ax", np.cos(ang))
    put("sin_ax", np.sin(ang) * sign)
    inv = (10000.0 ** (-(np.arange(0, HD, 2, dtype=np.float32) / HD))).astype(np.float32)
    ang = tok[None] * inv[d % 32][:, None]
    put("cos_1d", np.cos(ang))
    put("sin_1d", np.sin(ang) * np.where(d < 32, -1.0, 1.0)[:, None])
    put("ones", np.ones((P, P)))
    put("ident", np.eye(P))
    put("head_ones", np.kron(np.eye(2), np.ones((HD, HD))))
    i = np.arange(P)
    put("swap16", i[:, None] == (i ^ 16)[None])
    put("swap32", i[:, None] == (i ^ 32)[None])
    q, k = i[:, None], i[None]
    put("win0", np.where(k <= q, 0, NEG))
    put("win1", np.where(k >= q, 0, NEG))
    put("swa_cur", np.where(k <= q, 0, NEG))
    put("swa_prev", np.where(k > q, 0, NEG))
    s, t = i[:, None], i[None]
    both = [s == t] + [(s // (2 * m) == t // (2 * m)) & (s // m != t // m) for m in LEVELS]
    put("both", np.stack(both, 1))
    put("causal", np.stack([both[0]] + [b & (s < t) for b in both[1:]], 1))
    return con


CONVS = {"ffn0_x": 0, "ffn0_c": 1, "ffn1": 2}


def tile_plan(start, n_slabs):
    freed, first, count = [], {}, {"v": 0, "a": 0}

    def add(phase, who):
        first.setdefault(phase, len(freed))
        for w in who:
            count[w] += 1
            freed.append((w, count[w]))

    for phase in start:
        if phase.startswith("qkv"):
            add(phase, "v" * 12)
        elif phase == "hg_c":
            add(phase, "a" * (8 + 2 * HG_HEADS))
        elif phase == "hg_x":
            add(phase, "a" * (8 + 4 * HG_HEADS))
        elif phase.endswith("swa"):
            add(phase, "v" * 5 + "v" * 2)
        elif phase.endswith("gla"):
            add(phase, "v" * 9 + "a" * 8)
        elif phase.endswith("merge"):
            add(phase, "v" * 4 * KD)
        elif phase.endswith("_down") or "out" in phase or phase.endswith("_r"):
            add(phase, "v" * KD)
        else:
            add(phase, "v" * 2 * KF)
    return freed, first


def build(nc, dram, out):
    slabs, panels, start, ada = plan()
    freed, first_tile = tile_plan(start, len(slabs))
    with ExitStack() as ctx:
        scopes = [ctx]

        def sb(name, shape, dt=F32):
            return scopes[-1].enter_context(nc.sbuf_tensor(name, shape, dt))

        def sem(name):
            return ctx.enter_context(nc.semaphore(name))

        scopes.append(ExitStack())
        raw = [sb(f"raw{n}", [P, 2, SLAB]) for n in range(RAW)]
        scopes.pop().close()
        raw_lo = [sb(f"raw_lo{n}", [P, 2, SLAB], F32R) for n in range(RAW)]
        w_hi = [sb(f"w_hi{n}", [P, SLAB], F32R) for n in range(RING)]
        w_lo = [sb(f"w_lo{n}", [P, SLAB], F32R) for n in range(RING)]
        res = [sb("res_x", [P, KD, T]), sb("res_c", [P, KD, T])]
        h_hi = sb("h_hi", [P, KD, T], F32R)
        h_lo = sb("h_lo", [P, KD, T], F32R)
        h_fp = sb("h_fp", [P, KD, T])
        vec = sb("vec", [P, VEC_W])
        con = sb("con", [P, CON_W])
        mod = sb("mod", [P, 2, 48, 2])
        mod_g = sb("mod_g", [P, 2, 2, 2, KD])
        WIDE = 2 * ADA_QKV - 4
        c_wide = sb("c_wide", [P, KD, 2 * WIDE + 4], F32R)
        c_act = sb("c_act", [P, KD, 2])
        lb = sb("lb", [P, 4, KD])
        eps = sb("eps", [P, 1])
        warm = sb("warm", [P, 1])
        rms = sb("rms", [P, T])
        rstd = sb("rstd", [P, T])
        conv = [sb(f"conv{n}", [P, T]) for n in range(2)]
        gate = [sb(f"gate{n}", [P, T]) for n in range(2)]
        prod = [sb(f"prod{n}", [P, T]) for n in range(2)]

        def V(name, *shape):
            at, width = VEC[name]
            v = vec[:, at:at + width]
            return v if not shape else v.rearrange(shape[0], **shape[1])

        def K(name, cols=None):
            at, width = CON[name]
            return con[:, at:at + (cols or width)]

        c_in = V("c", "p (k s) -> p k s", dict(s=2))
        norm1 = V("norm1", "p (l k) -> p l k", dict(l=2))
        norm2 = V("norm2", "p (l k) -> p l k", dict(l=2))
        conv_w = V("conv_w", "p (l f w) -> p l f w", dict(l=2, w=3))
        conv_b = V("conv_b", "p (l f) -> p l f", dict(l=2))

        psum = [ctx.enter_context(nc.psum_tensor(f"bank{n}", [P, 512], F32)) for n in range(8)]
        NORM, ADA, SUMS, TURN = 4, 5, 6, 7

        params_in = sem("params_in")
        con_in = sem("con_in")
        x_in = sem("x_in")
        ctx_in = sem("ctx_in")
        raw_ready = [sem(f"raw_ready{n}") for n in range(RAW)]
        hi_ready = sem("hi_ready")
        lo_ready = sem("lo_ready")
        slab_used = sem("slab_used")
        freed_v = sem("freed_v")
        freed_a = sem("freed_a")
        v_step = sem("v_step")
        eps_set = sem("eps_set")
        c_silu = sem("c_silu")
        c_clear = sem("c_clear")
        c_hi = sem("c_hi")
        c_ready = sem("c_ready")
        ada_hi_ready = sem("ada_hi_ready")
        ada_lo_ready = sem("ada_lo_ready")
        ada_lo_pool = sem("ada_lo_pool")
        ada_used = sem("ada_used")
        ada_rows = sem("ada_rows")
        ada_turned = sem("ada_turned")
        mod_ready = sem("mod_ready")
        sq_ready = sem("sq_ready")
        norm_sum = sem("norm_sum")
        rms_ready = sem("rms_ready")
        h_fp_ready = sem("h_fp_ready")
        h_hi_ready = sem("h_hi_ready")
        sq_sum = sem("sq_sum")
        h_ready = sem("h_ready")
        h_ready_odd = sem("h_ready_odd")
        conv_1 = sem("conv_1")
        conv_2 = sem("conv_2")
        conv_3 = sem("conv_3")
        gate_ready = sem("gate_ready")
        act_hi_ready = sem("act_hi_ready")
        act_ready = sem("act_ready")
        out_done = sem("out_done")

        def freed_by(o):
            who, n = freed[o]
            return (freed_v if who == "v" else freed_a), n


        def load(sp, p):
            array, row, count, s, width = panels[p]
            if p >= RAW:
                prev = panels[p - RAW]
                if prev[3] is None:
                    sp.wait_ge(ada_used, 2 * ada.index(p - RAW) + 2)
                else:
                    sp.wait_ge(lo_ready, prev[3] + prev[2])
            src = dram[array][row:row + count]
            sp.dma_start(raw[p % RAW][:, 0:count, 0:width], src.rearrange("s p f -> p s f"))\
                .then_inc(raw_ready[p % RAW], 16)

        def split_hi(act, k, i=0):
            if k >= len(slabs):
                return
            p, place, width = slabs[k]
            if place == 0:
                act.wait_ge(raw_ready[p % RAW], 16 * (p // RAW + 1) + i * 16)
            if k >= RING:
                act.wait_ge(slab_used, k - RING + 1 + i * 8)
            act.activation(w_hi[k % RING][:, 0:width], raw[p % RAW][:, place, 0:width], ACT.Copy)\
                .then_inc(hi_ready, 1)

        def split_lo(dve, k, i=0):
            if k >= len(slabs):
                return
            p, place, width = slabs[k]
            dve.wait_ge(hi_ready, k + 1 + i * 8)
            dve.tensor_tensor(w_lo[k % RING][:, 0:width], raw[p % RAW][:, place, 0:width],
                              w_hi[k % RING][:, 0:width], ALU.subtract).then_inc(lo_ready, 1)

        def wait_h(eng, norm, k):
            eng.wait_ge(h_ready_odd if k % 2 else h_ready, KD // 2 * norm + k // 2 + 1)

        def three(pe, out_ap, a_hi, a_lo, b_hi, b_lo, start, stop):
            pe.matmul(out_ap, a_hi, b_hi, start=start, stop=False)
            pe.matmul(out_ap, a_hi, b_lo, start=False, stop=False)
            return pe.matmul(out_ap, a_lo, b_hi, start=False, stop=stop)

        def multiply(pe, k, o, hi, lo, blocks=KD, first=True, last=True, k0=0, i=0, lap=4, norm=None):
            pe.wait_ge(lo_ready, k + 1 + i * lap)
            bank = psum[o % 4][:, 0:T]
            for b in range(blocks):
                w = slice(b * P, (b + 1) * P)
                if norm is not None:
                    wait_h(pe, norm, b)
                mm = three(pe, bank, w_hi[k % RING][:, w], w_lo[k % RING][:, w], hi[:, k0 + b, :], lo[:, k0 + b, :],
                           first and b == 0, last and b == blocks - 1)
            mm.then_inc(slab_used, 1)

        def multiply_half(pe, k, o, hi, lo, half):
            if half == 0:
                pe.wait_ge(lo_ready, k + 1)
            for b in range(half * KD // 2, (half + 1) * KD // 2):
                w = slice(b * P, (b + 1) * P)
                mm = three(pe, psum[o % 4][:, 0:T], w_hi[k % RING][:, w], w_lo[k % RING][:, w], hi[:, b, :], lo[:, b, :],
                           b == 0, b == KD - 1)
            if half:
                mm.then_inc(slab_used, 1)

        def bank_free(pe, o):
            if o >= 4:
                pe.wait_ge(*freed_by(o - 4))

        def multiply_tokens(pe, k, o, part, groups=4, width=256, norm=None):
            pe.wait_ge(lo_ready, k + 1)
            for t in range(TT):
                for b in range(groups):
                    f = part * groups + b
                    w = slice(b * width, (b + 1) * width)
                    tok = slice(t * P, (t + 1) * P)
                    if norm is not None:
                        wait_h(pe, norm, f)
                    mm = three(pe, psum[(o + t) % 4][:, 0:width], h_hi[:, f, tok], h_lo[:, f, tok],
                               w_hi[k % RING][:, w], w_lo[k % RING][:, w],
                               f == 0, f == KD - 1)
            mm.then_inc(slab_used, 1)

        ADA_PARTS = [(0, ADA_FIRST), (ADA_FIRST, ADA_QKV), (ADA_FIRST + ADA_QKV, ADA_ATT)]
        ADA_BANK = [psum[ADA], psum[ADA], psum[3]]
        ADA_LATE = 2 * ADA_PARTS[1][0]
        ADA_TWO = 2 * ADA_PARTS[2][0]

        def ada_hi_of(n):
            return ada_hi[n % 4 if n < ADA_TWO else 2 + n % 2]

        def ada_act(act, n):
            p, place = ada[n // 2], n % 2
            if place == 0:
                act.wait_ge(raw_ready[p % RAW], 16 * (p // RAW + 1))
            ring = 4 if n < ADA_TWO else 2
            if n >= ring:
                act.wait_ge(ada_used, n - ring + 1)
            act.activation(ada_hi_of(n), raw[p % RAW][:, place, 0:D], ACT.Copy).then_inc(ada_hi_ready, 1)

        def ada_lo_by(n):
            if n < ADA_LATE:
                return ada_lo_ready, n + 1
            if n < ADA_TWO:
                return (ada_lo_pool, (n - ADA_LATE) // 2 + 1) if n % 2 else (ada_lo_ready, (n + ADA_LATE) // 2 + 1)
            return ada_lo_ready, (ADA_TWO + ADA_LATE) // 2 + n - ADA_TWO + 1

        def ada_lo(eng, n):
            p, place = ada[n // 2], n % 2
            eng.wait_ge(ada_hi_ready, n + 1)
            eng.tensor_tensor(raw_lo[p % RAW][:, place, 0:D], raw[p % RAW][:, place, 0:D], ada_hi_of(n), ALU.subtract)\
                .then_inc(ada_lo_by(n)[0], 1)

        def ada_pe(pe, part, n):
            at, panels_ = ADA_PARTS[part]
            total = 2 * at + n
            p, place, rows = ada[total // 2], total % 2, 2 * panels_
            pe.wait_ge(*ada_lo_by(total))
            shift_ = WIDE - 4 * (n // 4)
            for b in range(2):
                k, cols = 2 * (n % 4) + b, slice(b * 512, (b + 1) * 512)
                c = c_wide[:, k, shift_:shift_ + rows]
                pe.matmul(ADA_BANK[part][0:rows, :], c, ada_hi_of(total)[:, cols], start=n == 0 and b == 0, stop=False)
                mm = pe.matmul(ADA_BANK[part][0:rows, :], c, raw_lo[p % RAW][:, place, cols],
                               start=False, stop=n == rows - 1 and b == 1)
            mm.then_inc(ada_used, 1)

        def ada_turn_pe(pe, part):
            rows = 2 * ADA_PARTS[part][1]
            pe.wait_ge(ada_rows, part + 1)
            for q in range(4):
                mm = pe.transpose(ADA_BANK[part][:, q * rows:(q + 1) * rows],
                                  conv[q // 2][0:rows, (q % 2) * P:(q % 2 + 1) * P], K("ident")[0:rows, 0:rows])
            mm.then_inc(ada_turned, 1)

        def ada_dve(dve, link, part):
            at, panels_ = ADA_PARTS[part]
            rows, first, end = 2 * panels_, 2 * at, 2 * (at + panels_)
            dve.wait_ge(ada_used, end)
            for half in range(2):
                ins = dve.tensor_copy(conv[half][0:rows, :], ADA_BANK[part][0:rows, half * T:(half + 1) * T])
            ins.then_inc(ada_rows, 1)
            dve.wait_ge(ada_turned, part + 1)
            for half_ in range(2):
                for q in range(4):
                    sums_ = ADA_BANK[part][:, q * rows:(q + 1) * rows].rearrange("p (g c) -> p g c", c=4)
                    ada_bias = V("ada_b", "p (g q) -> p g q", dict(q=4))[:, first // 4:end // 4, q]
                    into = mod[:].rearrange("p l (g q) s -> p (l g) q s", q=4)[:, first // 4:end // 4, q, :]
                    ins = dve.tensor_tensor(into, sums_[:, :, 2 * half_:2 * half_ + 2],
                                            into if half_ else ada_bias.unsqueeze(2).to_broadcast([P, (end - first) // 4, 2]),
                                            ALU.add)
                link(ins)
            for layer in range(2):
                for n, (gains_, chunk) in enumerate(((norm1, 1), (norm2, 4))):
                    if first <= 48 * layer + 8 * chunk < end:
                        for t in (X, C):
                            ins = dve.scalar_tensor_tensor(mod_g[:, layer, n, t, :], mod[:, layer, 8 * chunk:8 * chunk + 8, t],
                                                           1.0, gains_[:, layer, :], ALU.add, ALU.mult)
            ins.then_inc(mod_ready, 1)
            dve.wait_ge(mod_ready, part + 1)

        def norm_square(act, n, t, k, base_freed=None):
            if k == 0 and n:
                wait_h(act, n - 1, KD - 2)
                wait_h(act, n - 1, KD - 1)
            if k == KD - 2 and n != 5:
                act.wait_ge(eps_set, 1)
                act.activation(warm[:], eps[:], ACT.Sqrt)
            if base_freed is None:
                act.wait_ge((x_in, ctx_in)[t], 16)
            else:
                act.wait_ge(*freed_by(base_freed + k))
            act.activation(h_fp[:, k, :], res[t][:, k, :], ACT.Square).then_inc(sq_ready, 1)

        def norm_act(act, n, shift, s_before, mod_parts=None):
            act.wait_ge(norm_sum, n + 1)
            act.activation(rms[:], psum[NORM][:, 0:T], ACT.Sqrt, bias=eps[:], scale=1.0 / D).then_inc(rms_ready, 1)
            if s_before:
                act.wait_ge(slab_used, s_before)
            if mod_parts:
                act.wait_ge(mod_ready, mod_parts)
            for k in range(KD):
                act.wait_ge(h_fp_ready, KD * n + k + 1)
                if shift is None:
                    act.activation(h_hi[:, k, :], h_fp[:, k, :], ACT.Copy).then_inc(h_hi_ready, 1)
                else:
                    act.activation(h_hi[:, k, :], h_fp[:, k, :], ACT.Identity, bias=shift(k)).then_inc(h_hi_ready, 1)

        def norm_pe(pe, n):
            pe.wait_ge(sq_sum, (KD - 2) * (n + 1))
            pe.matmul(psum[NORM][:, 0:T], K("ones"), h_fp[:, 0, :], start=True, stop=False)
            pe.wait_ge(sq_ready, KD * (n + 1))
            pe.matmul(psum[NORM][:, 0:T], K("ones"), h_fp[:, KD - 1, :], start=False, stop=True).then_inc(norm_sum, 1)

        def norm_pool(pool, n, shift):
            for k in range(1, KD - 1):
                pool.wait_ge(sq_ready, KD * n + k + 1)
                pool.tensor_tensor(h_fp[:, 0, :], h_fp[:, 0, :], h_fp[:, k, :], ALU.add).then_inc(sq_sum, 1)
                pool.wait_ge(sq_sum, (KD - 2) * n + k)
            if shift is None:
                for k in range(1, KD, 2):
                    norm_lo(pool, n, k, None).then_inc(h_ready_odd, 1)

        def norm_dve(dve, link, n, t, scale, shift):
            dve.wait_ge(rms_ready, n + 1)
            link(dve.reciprocal(rstd[:], rms[:]))
            for k in range(KD):
                dve.scalar_tensor_tensor(h_fp[:, k, :], res[t][:, k, :], scale(k), rstd[:], ALU.mult, ALU.mult)\
                    .then_inc(h_fp_ready, 1)
                if k % 2:
                    norm_lo(dve, n, k - 1, shift).then_inc(h_ready, 1)
                elif k and shift is not None:
                    norm_lo(dve, n, k - 1, shift).then_inc(h_ready_odd, 1)
            if shift is not None:
                norm_lo(dve, n, KD - 1, shift).then_inc(h_ready_odd, 1)

        def norm_lo(eng, n, k, shift):
            eng.wait_ge(h_hi_ready, KD * n + k + 1)
            if shift is None:
                return eng.tensor_tensor(h_lo[:, k, :], h_fp[:, k, :], h_hi[:, k, :], ALU.subtract)
            return eng.scalar_tensor_tensor(h_lo[:, k, :], h_fp[:, k, :], shift(k), h_hi[:, k, :], ALU.add, ALU.subtract)

        def ffn_pe(pe, phase, n_norm, n_ffn):
            s0, o0 = start[phase], first_tile[phase]
            with pe.Fori(0, 2 * KF // 4) as i:
                for j in range(4):
                    pe.wait_ge(freed_v, freed[o0 + j - 4][1] + i * 4)
                    multiply(pe, s0 + j, o0 + j, h_hi, h_lo, i=i, norm=n_norm if j == 0 else None)
            s1, o1 = start[phase + "_down"], first_tile[phase + "_down"]
            with pe.Fori(0, 2) as i:
                for j in range(8):
                    pe.wait_ge(act_ready, KF * n_ffn + HALF * (j % 2 + 1))
                    if j % 2 == 0:
                        pe.wait_ge(freed_v, freed[o1 + j // 2 - 4][1] + i * 4)
                    multiply(pe, s1 + j, o1 + j // 2, act_hi, act_lo, blocks=HALF, first=j % 2 == 0,
                             last=j % 2 == 1, k0=HALF * (j % 2), i=i, lap=8)

        def ffn_up_act(act, phase, n_ffn, conv_layer, j, f, i, i8=0):
            s, o = start[phase] + 2 * j, first_tile[phase] + 2 * j
            u = KF * n_ffn + j
            four = i8 * 4
            act.wait_ge(slab_used, s + 1 + i8 * 8)
            if conv_layer is None:
                act.wait_ge(freed_v, freed[o - 4][1] + 1 + i8 * 8)
                act.activation(gate[j % 2][:], psum[o % 4][:, 0:T], ACT.Silu).then_inc(gate_ready, 1)
                split_hi(act, s + AHEAD, i8)
            else:
                act.wait_ge(freed_v, freed[o - 4][1] + 1 + i8 * 8)
                act.activation(conv[j % 2][:], psum[o % 4][:, 0:T], ACT.Identity, scale=conv_w[:, conv_layer, f, 1:2],
                               bias=conv_b[:, conv_layer, f:f + 1] if isinstance(f, int) else
                               conv_b[:, conv_layer, bass.ds(f, 1)]).then_inc(conv_1, 1)
                split_hi(act, s + AHEAD, i8)
                nc_ = CONVS[phase]
                act.wait_ge(conv_3, KF * nc_ + j + 1 + four)
                act.activation(gate[j % 2][:], conv[j % 2][:], ACT.Silu).then_inc(gate_ready, 1)
            split_hi(act, s + 1 + AHEAD, i8)
            act.wait_ge(freed_v, freed[o][1] + 1 + i8 * 8)
            act.activation(act_hi[:, f, :], prod[j % 2][:], ACT.Copy).then_inc(act_hi_ready, 1)

        def ffn_up_dve(dve, phase, n_ffn, conv_layer, j, f, i, i8=0):
            s, o = start[phase] + 2 * j, first_tile[phase] + 2 * j
            u = KF * n_ffn + j
            four = i8 * 4
            if conv_layer is not None:
                nc_ = KF * CONVS[phase] + j
                g = psum[o % 4]
                cv = conv[j % 2]
                dve.wait_ge(conv_1, nc_ + 1 + four)
                dve.scalar_tensor_tensor(cv[:, 1:T], g[:, 0:T - 1], conv_w[:, conv_layer, f, 0:1], cv[:, 1:T],
                                         ALU.mult, ALU.add).then_inc(conv_2, 1)
                dve.wait_ge(conv_2, nc_ + 1 + four)
                dve.scalar_tensor_tensor(cv[:, 0:T - 1], g[:, 1:T], conv_w[:, conv_layer, f, 2:3], cv[:, 0:T - 1],
                                         ALU.mult, ALU.add).then_inc(conv_3, 1)
            split_lo(dve, s + AHEAD, i8)
            dve.wait_ge(slab_used, s + 2 + i8 * 8)
            dve.wait_ge(gate_ready, u + 1 + four)
            dve.tensor_tensor(prod[j % 2][:], psum[(o + 1) % 4][:, 0:T], gate[j % 2][:], ALU.mult)\
                .then_inc(freed_v, 2)
            split_lo(dve, s + 1 + AHEAD, i8)
            dve.wait_ge(act_hi_ready, u + 1 + four)
            dve.tensor_tensor(act_lo[:, f, :], prod[j % 2][:], act_hi[:, f, :], ALU.subtract)\
                .then_inc(act_ready, 1)

        def ffn_up(eng, step, phase, n_ffn, conv_layer):
            with eng.Fori(0, 5) as i:
                for j in range(4):
                    step(eng, phase, n_ffn, conv_layer, j, i * 4 + j, i, i)
            for j in range(20, KF):
                step(eng, phase, n_ffn, conv_layer, j, j, None)

        def residual_act(act, phase, halves=1, square=None, lag=1):
            for j in range(KD):
                for k in range(halves):
                    split_hi(act, start[phase] + halves * j + k + AHEAD)
                if square and j >= lag:
                    square(j - lag)
            if square and lag:
                square(KD - 1)

        def residual_dve(dve, phase, t, gain, halves=1):
            s0, o0 = start[phase], first_tile[phase]
            for j in range(KD):
                residual_tile_dve(dve, s0 + halves * j, o0 + j, res[t][:, j, :], gain(j), halves)

        def residual_tile_dve(dve, s, o, r, gain, halves=1):
            dve.wait_ge(slab_used, s + halves)
            dve.scalar_tensor_tensor(r, psum[o % 4][:, 0:T], gain, r, ALU.mult, ALU.add).then_inc(freed_v, 1)
            for k in range(halves):
                split_lo(dve, s + k + AHEAD)

        def linear_pe(pe, phase, hi, lo, ready=None):
            s0, o0 = start[phase], first_tile[phase]
            for j in range(KD):
                bank_free(pe, o0 + j)
                if ready:
                    ready(j)
                multiply(pe, s0 + j, o0 + j, hi, lo)

        def region():
            scopes.append(ExitStack())

        def close():
            scopes.pop().close()

        sums = sb("sums", [P, 4, 2])
        top = sb("top", [P, 4, 2])
        ntop = sb("ntop", [P, 4, 2])
        esink = sb("esink", [P, 4, 2])
        den = sb("den", [P, 4, 2])
        rden = sb("rden", [P, 4, 2])
        nsink = sb("nsink", [P, 32])
        region()
        act_hi = sb("act_hi", [P, KF, T], F32R)
        act_lo = sb("act_lo", [P, KF, T], F32R)
        close()
        region()
        region()
        att_o = sb("att_o", [P, 2 * TT, D])
        close()
        ada_hi_all = sb("ada_hi", [P, 4, D], F32R)
        ada_hi = [ada_hi_all[:, n, :] for n in range(4)]
        att_q = [sb("att_q_x", [P, KD, T]), sb("att_q_c", [P, KD, T])]
        att_k = sb("att_k", [P, 2, 2 * T])
        att_v = sb("att_v", [P, 2 * TT, 2 * P])
        probs = [h_fp[:, 4 + 2 * n:6 + 2 * n, :].rearrange("p a b -> p (a b)") for n in range(2)]
        att_sq = prod
        att_root = gate
        probs_t = [sb(f"probs_t{n}", [P, 4, P]) for n in range(2)]
        close()
        region()
        hg_v = sb("hg_v", [P, TT, D])
        hg_s = res[C][:].rearrange("p h (d v) -> p h d v", d=2)
        hg_sq, hg_root = conv[1], prod[1]
        hg_o_hi = sb("hg_o_hi", [P, KD, T], F32R)
        hg_o_lo = sb("hg_o_lo", [P, KD, T], F32R)
        hg_q = [sb(f"hg_q{n}", [P, T]) for n in range(2)]
        hg_g = [sb(f"hg_g{n}", [P, T]) for n in range(2)]
        hg_k = [[sb(f"hg_k{d}{n}", [P, T]) for n in range(2)] for d in range(2)]
        hg_p = [[sb(f"hg_p{d}{n}", [P, T]) for n in range(2)] for d in range(2)]
        hg_r = [sb(f"hg_r{d}", [P, T]) for d in range(2)]
        hg_u = [sb(f"hg_u{n}", [P, T]) for n in range(2)]
        hg_w = [sb(f"hg_w{n}", [P, T]) for n in range(2)]
        hg_a = [sb(f"hg_a{n}", [P, TT, P]) for n in range(2)]
        hg_kt = prod
        close()
        region()
        oa_hi = sb("oa_hi", [P, 4, T], F32R)
        oa_lo = sb("oa_lo", [P, 4, T], F32R)
        ob = res[C]
        region()
        gl_q = sb("gl_q", [P, GLA_HEADS, T])
        gl_k = sb("gl_k", [P, GLA_HEADS, T])
        region()
        swa_q = sb("swa_q", [P, 5, T])
        swa_v = sb("swa_v", [P, TT, P])
        swa_sq, swa_root = prod, gate
        swa_o = sb("swa_o", [P, TT, 4 * P])
        swa_p = [sb(f"swa_p{n}", [P, 3 * P]) for n in range(2)]
        swa_pt = [sb(f"swa_pt{n}", [P, 3, P]) for n in range(2)]
        close()
        region()
        gl_p = sb("gl_p", [P, GLA_HEADS, T])
        gl_r = sb("gl_r", [P, GLA_HEADS, T])
        gl_lr = conv[0]
        gl_v = sb("gl_v", [P, TT, D])
        gl_u = [sb(f"gl_u{n}", [P, GLA_HEADS, P]) for n in range(2)]
        gl_w = [sb(f"gl_w{n}", [P, GLA_HEADS, P]) for n in range(2)]
        gl_sq = [u[:].rearrange("p h t -> p (h t)") for u in gl_u]
        gl_a = [sb(f"gl_a{n}", [P, GLA_HEADS, P]) for n in range(2)]
        close()
        close()
        region()
        ob_hi = sb("ob_hi", [P, KD, T], F32R)
        ob_lo = sb("ob_lo", [P, KD, T], F32R)
        mg_hi = sb("mg_hi", [P, KD, T], F32R)
        mg_lo = sb("mg_lo", [P, KD, T], F32R)
        close()
        close()
        scopes[:] = [ctx]

        qk_sq = sem("qk_sq")
        qk_sum = sem("qk_sum")
        qk_rms = sem("qk_rms")
        qk_turn = sem("qk_turn")
        turn_free = sem("turn_free")
        mixer_in = sem("mixer_in")
        s_done = sem("s_done")
        top_ready = sem("top_ready")
        p_ready = sem("p_ready")
        esink_ready = sem("esink_ready")
        pt_done = sem("pt_done")
        pt_ready = sem("pt_ready")
        o_done = sem("o_done")
        o_out = sem("o_out")
        ot_done = sem("ot_done")
        ot_hi = sem("ot_hi")
        ot_ready = sem("ot_ready")
        p_set = sem("p_set")
        f_ready = sem("f_ready")
        decay_b = sem("decay_b")
        decay_f = sem("decay_f")
        kd_ready = sem("kd_ready")
        kd_ready_b = sem("kd_ready_b")
        kt_done = sem("kt_done")
        kt_ready = sem("kt_ready")
        state_done = sem("state_done")
        state_ready = sem("state_ready")
        uw_ready = sem("uw_ready")
        uw_ready_b = sem("uw_ready_b")
        a_done = sem("a_done")
        a_ready = sem("a_ready")
        pv_done = sem("pv_done")
        lin_sq = sem("lin_sq")
        lin_sum = sem("lin_sum")
        lin_rms = sem("lin_rms")
        lin_norm = sem("lin_norm")
        lin_gated = sem("lin_gated")
        lin_hi = sem("lin_hi")
        lin_ready = sem("lin_ready")
        lr_ready = sem("lr_ready")
        z_done = sem("z_done")
        z_abs = sem("z_abs")
        z_exp = sem("z_exp")
        z_ln = sem("z_ln")
        z_min = sem("z_min")
        z_sub = sem("z_sub")
        w_ready = sem("w_ready")
        r_set = sem("r_set")
        mix_sig = sem("mix_sig")
        mix_sum = sem("mix_sum")
        mix_hi = sem("mix_hi")
        mix_ready = sem("mix_ready")
        lb_top = sem("lb_top")
        lb_exp = sem("lb_exp")

        def nsink_dve(dve, link):
            link(dve.tensor_scalar(nsink[:, 0:16], V("sink"), -1.0, None, ALU.mult))
            link(dve.tensor_scalar(nsink[:, 16:32], V("swa_sink"), -1.0, None, ALU.mult))

        def qk_pe(pe, phase, tiles, dst, swap, n0, r0, sq, norm, with_ada=False):
            s0, o0 = start[phase], first_tile[phase]
            for m in range(tiles + 2):
                if m < tiles:
                    bank_free(pe, o0 + m)
                    multiply(pe, s0 + m, o0 + m, h_hi, h_lo, norm=norm if m == 0 else None)
                    if with_ada:
                        qkv_ada_pe(pe, n0 // 10 * 12 + m)
                if 1 <= m <= tiles:
                    n = n0 + m - 1
                    pe.wait_ge(qk_sq, n + 1)
                    if n:
                        pe.wait_ge(qk_rms, n)
                    pe.matmul(psum[SUMS][:, 0:T], K("head_ones"), sq[n % 2][:], start=True, stop=True)\
                        .then_inc(qk_sum, 1)
                if m >= 2 and swap:
                    pe.wait_ge(*freed_by(o0 + m - 2))
                    if r0 + m - 2:
                        pe.wait_ge(turn_free, r0 + m - 2)
                    pe.matmul(psum[TURN][:, 0:T], K(swap), dst(m - 2), start=True, stop=True).then_inc(qk_turn, 1)

        def qkv_ada_pe(pe, m, end=0):
            for n in range(2 * max(m - 2, 0), 2 * max(m - 1, 0) + end):
                ada_pe(pe, 1, n)

        def qkv_ada_act(act, m):
            if m:
                for n in range(2 * m - 2, 2 * m):
                    ada_act(act, ADA_LATE + n)

        def qkv_ada_dve(dve, m):
            if m:
                ada_lo(dve, ADA_LATE + 2 * m - 2)

        def qk_act(act, phase, tiles, n0, sq, root, with_ada=False):
            s0, o0 = start[phase], first_tile[phase]
            for m in range(tiles + 1):
                n = n0 + m
                if m < tiles:
                    if with_ada:
                        qkv_ada_act(act, n0 // 10 * 12 + m)
                    act.wait_ge(slab_used, s0 + m + 1)
                    if n >= 2:
                        act.wait_ge(qk_sum, n - 1)
                    act.activation(sq[n % 2][:], psum[(o0 + m) % 4][:, 0:T], ACT.Square).then_inc(qk_sq, 1)
                if m >= 1:
                    act.wait_ge(qk_sum, n)
                    if m >= 3:
                        act.wait_ge(*freed_by(o0 + m - 3))
                    act.activation(root[(n - 1) % 2][:], psum[SUMS][:, 0:T], ACT.Sqrt, bias=eps[:],
                                   scale=1.0 / HD).then_inc(qk_rms, 1)
                if m < tiles:
                    split_hi(act, s0 + m + AHEAD)

        def qk_dve(dve, link, phase, tiles, dst, gain, cos, sin, n0, r0, root, with_ada=False):
            s0, o0 = start[phase], first_tile[phase]
            for m in range(tiles + 2):
                if m < tiles and with_ada:
                    qkv_ada_dve(dve, n0 // 10 * 12 + m)
                if 1 <= m <= tiles:
                    n = n0 + m - 1
                    dve.wait_ge(qk_rms, n + 1)
                    if m >= 2:
                        dve.wait_ge(*freed_by(o0 + m - 2))
                    link(dve.reciprocal(rstd[:], root[n % 2][:]))
                    dve.scalar_tensor_tensor(dst(m - 1), psum[(o0 + m - 1) % 4][:, 0:T], gain(m - 1), rstd[:],
                                             ALU.mult, ALU.mult).then_inc(freed_v, 1)
                if m >= 2 and cos:
                    dve.wait_ge(*freed_by(o0 + m - 2))
                    dve.wait_ge(qk_turn, r0 + m - 1)
                    link(dve.tensor_tensor(conv[0][:], psum[TURN][:, 0:T], K(sin), ALU.mult))
                    dve.tensor_tensor(dst(m - 2), dst(m - 2), K(cos), ALU.mult).then_inc(turn_free, 1)
                    dve.wait_ge(turn_free, r0 + m - 1)
                    link(dve.tensor_tensor(dst(m - 2), dst(m - 2), conv[0][:], ALU.add))
                if m < tiles:
                    split_lo(dve, s0 + m + AHEAD)

        def width(block_):
            return block_[1].shape[-1]

        def att_pe(pe, units, u0, probs_, probs_t_, n_in, fill=lambda m: None):
            pe.wait_ge(mixer_in, n_in)
            for m in range(len(units) + 2):
                if m < len(units):
                    u = u0 + m
                    if m >= 2:
                        pe.wait_ge(p_ready, u - 1)
                    bank, at = psum[4 + m % 2], 0
                    for q, k, masks, _ in units[m][0]:
                        mm = pe.matmul(bank[:, at:at + k.shape[-1]], q, k, start=True, stop=True, skip_group_check=True)
                        for place, mask in masks:
                            mm = pe.matmul(bank[:, at + place * P:at + (place + 1) * P], K("ident"), K(mask),
                                           start=False, stop=True, skip_group_check=True)
                        at += k.shape[-1]
                    mm.then_inc(s_done, 1)
                fill(m)
                if m >= 2:
                    u = u0 + m - 2
                    pe.wait_ge(pt_ready, u + 1)
                    if m >= 3:
                        pe.wait_ge(o_out, u)
                    at = 0
                    for n, (_, _, _, v) in enumerate(units[m - 2][0]):
                        for b in range(len(v)):
                            mm = pe.matmul(psum[6][:, n * HD:(n + 1) * HD], probs_t_[m % 2][:, at + b, :], v[b],
                                           start=b == 0, stop=b == len(v) - 1)
                        at += len(v)
                    mm.then_inc(o_done, 1)
                if 1 <= m <= len(units):
                    u = u0 + m - 1
                    pe.wait_ge(p_ready, u + 1)
                    for b in range(sum(width(x) for x in units[m - 1][0]) // P):
                        mm = pe.transpose(psum[7][:, b * P:(b + 1) * P], probs_[(m - 1) % 2][:, b * P:(b + 1) * P],
                                          K("ident"))
                    mm.then_inc(pt_done, 1)

        def att_act(act, units, u0, probs_, probs_t_, fill=lambda m: None):
            for m in range(len(units) + 2):
                if len(units[0][0]) == 1:
                    fill(m)
                if m < len(units):
                    u = u0 + m
                    blocks_, at = units[m][0], 0
                    act.wait_ge(top_ready, u + 1)
                    if m >= 2:
                        act.wait_ge(pt_done, u - 1)
                    for n, x in enumerate(blocks_):
                        ins = act.activation(probs_[m % 2][:, at:at + width(x)], psum[4 + m % 2][:, at:at + width(x)],
                                             ACT.Exp, bias=ntop[:, u % 4, n:n + 1], scale=SCALE,
                                             accum_out=sums[:, u % 4, n:n + 1])
                        at += width(x)
                    ins.then_inc(p_ready, 1)
                    act.activation(esink[:, u % 4, 0:len(blocks_)], ntop[:, u % 4, 0:len(blocks_)], ACT.Exp,
                                   bias=units[m][1]).then_inc(esink_ready, 1)
                if 1 <= m <= len(units):
                    u = u0 + m - 1
                    keys = sum(width(x) for x in units[m - 1][0])
                    act.wait_ge(pt_done, u + 1)
                    if m >= 3:
                        act.wait_ge(o_done, u - 1)
                    act.activation(probs_t_[(m - 1) % 2][:, 0:keys // P, :],
                                   psum[7][:, 0:keys].rearrange("p (b q) -> p b q", q=P), ACT.Copy)\
                        .then_inc(pt_ready, 1)
                if len(units[0][0]) == 2:
                    fill(m)

        def att_dve(dve, link, units, u0, fill=lambda m: None):
            for m in range(len(units) + 2):
                if m < len(units):
                    u = u0 + m
                    blocks_, bank = units[m][0], psum[4 + m % 2]
                    dve.wait_ge(s_done, u + 1)
                    if len(blocks_) == 2 and width(blocks_[0]) == width(blocks_[1]):
                        ins = dve.reduce_max(top[:, u % 4, :], bank[:].rearrange("p (n k) -> p n k", n=2), AX_X)
                    else:
                        at = 0
                        for n, x in enumerate(blocks_):
                            ins = dve.reduce_max(top[:, u % 4, n:n + 1], bank[:, at:at + width(x)], AX_X)
                            at += width(x)
                    link(ins)
                    dve.tensor_scalar(ntop[:, u % 4, 0:len(blocks_)], top[:, u % 4, 0:len(blocks_)], -SCALE,
                                      units[m][2], ALU.mult, ALU.min).then_inc(top_ready, 1)
                if m >= 2:
                    u = u0 + m - 2
                    n = len(units[m - 2][0])
                    row = (slice(None), u % 4, slice(0, n))
                    dve.wait_ge(esink_ready, u + 1)
                    link(dve.tensor_tensor(den[row], sums[row], esink[row], ALU.add))
                    link(dve.reciprocal(rden[row], den[row]))
                    dve.wait_ge(o_done, u + 1)
                    if n == 1:
                        ins = dve.tensor_scalar(units[m - 2][3], psum[6][:, 0:HD], rden[row], None, ALU.mult)
                    else:
                        ins = dve.tensor_tensor(units[m - 2][3], psum[6][:, 0:2 * HD].rearrange("p (n d) -> p n d", n=2),
                                                rden[row].unsqueeze(2).to_broadcast([P, 2, HD]), ALU.mult)
                    ins.then_inc(o_out, 1)
                fill(m)

        def turn_pe(pe, o, tiles, u_end, n0):
            pe.wait_ge(o_out, u_end)
            for f in range(tiles):
                if n0 + f >= 2:
                    pe.wait_ge(ot_ready, n0 + f - 1)
                for t in range(TT):
                    mm = pe.transpose(psum[6 + f % 2][:, t * P:(t + 1) * P], o[:, t, f * P:(f + 1) * P], K("ident"))
                mm.then_inc(ot_done, 1)

        def turn_act(act, hi, tiles, n0):
            for f in range(tiles):
                act.wait_ge(ot_done, n0 + f + 1)
                act.activation(hi[:, f, :], psum[6 + f % 2][:, 0:T], ACT.Copy).then_inc(ot_hi, 1)

        def turn_dve(dve, hi, lo, tiles, n0):
            for f in range(tiles):
                dve.wait_ge(ot_hi, n0 + f + 1)
                dve.tensor_tensor(lo[:, f, :], psum[6 + f % 2][:, 0:T], hi[:, f, :], ALU.subtract).then_inc(ot_ready, 1)

        STEPS = [1, 2, 4, 8, 16, 32, 64, 128]
        NSTEP = len(STEPS)
        done = {"b": 0, "f": 0}

        def decay_step(eng, way, p, r, m, heads=False):
            signal = decay_f if way == "f" else decay_b
            shape = "p h (b c m) -> p (h b) c m" if heads else "p (b c m) -> p b c m"
            pv, rv = (x.rearrange(shape, c=2, m=m) for x in (p, r))
            near, far, end = (0, 1, m - 1) if way == "f" else (1, 0, 0)
            blocks = pv.shape[1]
            for x, side, other in ((rv, near, far), (pv, far, near)):
                eng.tensor_tensor(x[:, :, side, :], x[:, :, side, :],
                                  pv[:, :, other, end:end + 1].to_broadcast([P, blocks, m]), ALU.mult)\
                    .then_inc(signal, 1)
                done[way] += 1
                eng.wait_ge(signal, done[way])

        def decay_f_step(dve, p, r, m, heads=False):
            decay_step(dve, "f", p, r, m, heads)

        def decay_b_step(pool, p, r, m):
            decay_step(pool, "b", p, r, m)


        def values_pe(pe, phase, first_slab, groups, o, norm=None):
            s0 = start[phase] + first_slab
            for g in range(groups):
                bank_free(pe, o + 2 * g)
                bank_free(pe, o + 2 * g + 1)
                for part in range(2):
                    multiply_tokens(pe, s0 + 2 * g + part, o + 2 * g, part, norm=norm if g == 0 else None)

        def values_act(act, phase, first_slab, groups, o, dst):
            s0 = start[phase] + first_slab
            for g in range(groups):
                act.wait_ge(slab_used, s0 + 2 * g + 2)
                for t in range(TT):
                    act.activation(dst[:, t, g * 256:(g + 1) * 256], psum[(o + 2 * g + t) % 4][:, 0:256], ACT.Copy)\
                        .then_inc(freed_a, 1)
                for part in range(2):
                    split_hi(act, s0 + 2 * g + part + AHEAD)

        def hg_decays(d, n):
            return gate[d] if n < HG_HEADS and n % 2 else hg_r[d]

        def hg_forget_act(act, s, o, n, d):
            h, u = n % HG_HEADS, 2 * n + d
            act.wait_ge(slab_used, s + 1)
            if 2 <= n < HG_HEADS + 2:
                act.wait_ge((kd_ready, kd_ready_b)[d], n - 1)
            elif n >= 2:
                act.wait_ge(pv_done, 10 * (h - 1))
            p = hg_p[d][n % 2]
            act.activation(p[:], psum[o % 4][:, 0:T], ACT.Sigmoid).then_inc(freed_a, 1)
            act.wait_ge(*freed_by(o))
            act.activation(p[:], p[:], ACT.Identity, scale=lb[:, 3, h:h + 1], bias=lb[:, 2, h:h + 1]).then_inc(p_set, 1)
            act.wait_ge(p_set, u + 1)
            act.activation(hg_k[d][n % 2][:], p[:], ACT.Identity, scale=-1.0, bias=1.0).then_inc(f_ready, 1)

        def hgc_pe(pe):
            phase = "hg_c"
            s0, o0 = start[phase], first_tile[phase]
            values_pe(pe, phase, 0, 4, o0, norm=4)
            for h in range(HG_HEADS + 2):
                g = h - 2
                for d in range(2):
                    if h < HG_HEADS:
                        k = 8 + 2 * h + d
                        bank_free(pe, o0 + k)
                        multiply(pe, s0 + k, o0 + k, h_hi, h_lo)
                    if h >= 2 and d == 0:
                        pe.wait_ge(kd_ready, g + 1)
                        pe.wait_ge(kd_ready_b, g + 1)
                        if g:
                            pe.wait_ge(kt_ready, g)
                        for way in range(2):
                            for t in range(TT):
                                mm = pe.transpose(psum[TURN][:, (2 * way + t) * P:(2 * way + t + 1) * P],
                                                  hg_decays(way, g)[:, t * P:(t + 1) * P], K("ident"))
                        mm.then_inc(kt_done, 1)
                    if h >= 2 and d == 1:
                        pe.wait_ge(kt_ready, g + 1)
                        if g:
                            pe.wait_ge(state_ready, g)
                        for way in range(2):
                            for t in range(TT):
                                mm = pe.matmul(psum[SUMS][:, way * P:(way + 1) * P], hg_kt[way][:, t * P:(t + 1) * P],
                                               hg_v[:, t, g * P:(g + 1) * P], start=t == 0, stop=t == TT - 1)
                        mm.then_inc(state_done, 1)

        def hgc_act(act, square):
            phase = "hg_c"
            s0, o0 = start[phase], first_tile[phase]
            values_act(act, phase, 0, 4, o0, hg_v)
            for h in range(HG_HEADS + 2):
                g = h - 2
                for d in range(2):
                    if h < HG_HEADS:
                        k = 8 + 2 * h + d
                        hg_forget_act(act, s0 + k, o0 + k, h, d)
                        split_hi(act, s0 + k + AHEAD)
                    if h >= 2 and d == 0:
                        act.wait_ge(kt_done, g + 1)
                        if g:
                            act.wait_ge(state_done, g)
                        for way in range(2):
                            ins = act.activation(hg_kt[way][:], psum[TURN][:, way * T:(way + 1) * T], ACT.Copy)
                        ins.then_inc(kt_ready, 1)
                    if h >= 2 and d == 1:
                        act.wait_ge(state_done, g + 1)
                        act.activation(hg_s[:, g, :, :], psum[SUMS][:, 0:2 * P].rearrange("p (d v) -> p d v", v=P),
                                       ACT.Copy).then_inc(state_ready, 1)
                if h < KD:
                    square(h)

        def hgc_dve(dve, link):
            phase = "hg_c"
            s0, o0 = start[phase], first_tile[phase]
            for k in range(8):
                split_lo(dve, s0 + k + AHEAD)
            for h in range(HG_HEADS):
                k = 8 + 2 * h
                p, decays = hg_p[0][h % 2][:], hg_decays(0, h)[:]
                if h >= 2:
                    dve.wait_ge(kt_done, h - 1)
                dve.wait_ge(f_ready, 2 * h + 1)
                link(dve.memset(decays, 1.0))
                for m in STEPS[:4]:
                    decay_f_step(dve, p, decays, m)
                split_lo(dve, s0 + k + AHEAD)
                for m in STEPS[4:]:
                    decay_f_step(dve, p, decays, m)
                dve.tensor_tensor(decays, decays, hg_k[0][h % 2][:], ALU.mult).then_inc(kd_ready, 1)
                split_lo(dve, s0 + k + 1 + AHEAD)

        def hgc_pool(pool):
            for h in range(HG_HEADS):
                decays = hg_decays(1, h)[:]
                if h >= 2:
                    pool.wait_ge(kt_done, h - 1)
                pool.wait_ge(f_ready, 2 * h + 2)
                pool.memset(decays, 1.0).then_inc(r_set, 1)
                pool.wait_ge(r_set, h + 1)
                for m in STEPS:
                    decay_b_step(pool, hg_p[1][h % 2][:], decays, m)
                pool.tensor_tensor(decays, decays, hg_k[1][h % 2][:], ALU.mult).then_inc(kd_ready_b, 1)

        HALVES = [(0, 1), (2,), (3,), (4,), (5,), (6,), (7, 8), (9,)]
        LV = 9

        def hgx_unit_pe(pe, h, l):
            n = HG_HEADS + h
            q = hg_q[n % 2]
            if l < LV:
                a = LV * h + l
                pe.wait_ge(uw_ready, 10 * h + l + 1)
                if l:
                    pe.wait_ge(uw_ready_b, LV * h + l)
                if l >= 2 or h:
                    pe.wait_ge(a_ready, a - 1)
                for c in range(TT):
                    other = 1 - c if l == 8 else c
                    u = (q if l == 0 else hg_u[l % 2])[:, other * P:(other + 1) * P]
                    mm = pe.matmul(psum[4 + a % 2][:, c * P:(c + 1) * P], hg_w[l % 2][:, c * P:(c + 1) * P], u,
                                   start=True, stop=True)
                mm.then_inc(a_done, 1)
            if 1 <= l:
                a = LV * h + l - 1
                pe.wait_ge(a_ready, a + 1)
                if l == 1 and h:
                    pe.wait_ge(lin_norm, h)
                for c in range(TT):
                    to = 1 - c if l - 1 == 8 else c
                    mm = pe.matmul(psum[SUMS][:, to * P:(to + 1) * P], hg_v[:, c, h * P:(h + 1) * P],
                                   hg_a[a % 2][:, c, :], start=l == 1 and c == 0, stop=False, skip_group_check=True)
                mm.then_inc(pv_done, 1)
            if l == LV:
                pe.wait_ge(uw_ready, 10 * h + 10)
                pe.wait_ge(uw_ready_b, LV * h + LV)
                for d in range(2):
                    mm = pe.matmul(psum[SUMS][:, 0:T], hg_s[:, h, d, :], hg_u[d][:], start=False, stop=d == 1,
                                   skip_group_check=True)
                mm.then_inc(pv_done, 1)

        def hgx_sum_pe(pe, h):
            pe.wait_ge(lin_sq, h + 1)
            if h:
                pe.wait_ge(lin_rms, h)
            pe.matmul(psum[TURN][:, 0:T], K("ones"), hg_sq[:], start=True, stop=True).then_inc(lin_sum, 1)

        def hgx_pe(pe):
            phase = "hg_x"
            s0, o0 = start[phase], first_tile[phase]
            values_pe(pe, phase, 0, 4, o0, norm=5)
            for h in range(HG_HEADS + 1):
                for step in range(8):
                    if h < HG_HEADS:
                        k = 8 + 4 * h + step // 2
                        if step % 2 == 0:
                            bank_free(pe, o0 + k)
                        multiply_half(pe, s0 + k, o0 + k, h_hi, h_lo, step % 2)
                    if h >= 2 and step == 0:
                        hgx_sum_pe(pe, h - 2)
                    if h >= 1:
                        if h == 1 and step == 0:
                            pe.wait_ge(*freed_by(o0 + 7))
                            pe.wait_ge(state_ready, HG_HEADS)
                        for l in HALVES[step]:
                            hgx_unit_pe(pe, h - 1, l)
            hgx_sum_pe(pe, HG_HEADS - 1)

        def half(x, l, side):
            return x[:].rearrange("p (b c m) -> p b c m", c=2, m=STEPS[l - 1])[:, :, side, :]

        def hgx_unit_dve(dve, link, h, l):
            n = HG_HEADS + h
            q, kf, kb = hg_q[n % 2], hg_k[0][n % 2], hg_k[1][n % 2]
            pf, rf = hg_p[0][n % 2], hg_r[0]
            if l == 0:
                dve.wait_ge(*freed_by(first_tile["hg_x"] + 8 + 4 * h + 3))
                dve.wait_ge(f_ready, 2 * n + 2)
                if h == 0:
                    dve.wait_ge(kt_done, HG_HEADS)
                if h:
                    dve.wait_ge(pv_done, 10 * h)
                link(dve.memset(rf[:], 1.0))
                dve.tensor_tensor(hg_w[0][:], kf[:], kb[:], ALU.add).then_inc(uw_ready, 1)
            else:
                if l >= 2:
                    decay_f_step(dve, pf[:], rf[:], STEPS[l - 2])
                if l >= 2:
                    dve.wait_ge(a_done, LV * h + l - 1)
                if l == LV:
                    dve.wait_ge(a_done, LV * h + LV)
                    dve.tensor_tensor(hg_u[0][:], q[:], pf[:], ALU.mult).then_inc(uw_ready, 1)
                else:
                    u, w = hg_u[l % 2], hg_w[l % 2]
                    dve.tensor_tensor(half(u, l, 1), half(q, l, 1), half(pf, l, 1), ALU.mult)
                    dve.tensor_tensor(half(w, l, 0), half(kf, l, 0), half(rf, l, 0), ALU.mult).then_inc(uw_ready, 1)
            if l >= 1:
                a = LV * h + l - 1
                dve.wait_ge(a_done, a + 1)
                if a >= 2:
                    dve.wait_ge(pv_done, 10 * ((a - 2) // LV) + (a - 2) % LV + 1)
                at = psum[4 + a % 2][:, 0:T].rearrange("p (c t) -> p c t", t=P)
                if l - 1 == 8:
                    ins = dve.tensor_copy(hg_a[a % 2][:], at)
                else:
                    mask = K("both")[:, (l - 1) * P:l * P].unsqueeze(1).to_broadcast([P, TT, P])
                    ins = dve.tensor_tensor(hg_a[a % 2][:], at, mask, ALU.mult)
                ins.then_inc(a_ready, 1)

        def hgx_out_dve(dve, link, h):
            n = HG_HEADS + h
            dve.wait_ge(lin_rms, h + 1)
            link(dve.reciprocal(rstd[:], hg_root[:]))
            dve.scalar_tensor_tensor(conv[0][:], psum[SUMS][:, 0:T], V("o_gain"), rstd[:], ALU.mult, ALU.mult)\
                .then_inc(lin_norm, 1)
            dve.wait_ge(lin_norm, h + 1)
            dve.tensor_tensor(prod[0][:], conv[0][:], hg_g[n % 2][:], ALU.mult).then_inc(lin_gated, 1)
            dve.wait_ge(lin_hi, h + 1)
            dve.tensor_tensor(hg_o_lo[:, h, :], prod[0][:], hg_o_hi[:, h, :], ALU.subtract).then_inc(lin_ready, 1)

        def hgx_dve(dve, link):
            phase = "hg_x"
            s0, o0 = start[phase], first_tile[phase]
            dve.wait_ge(con_in, 32)
            for k in range(7):
                split_lo(dve, s0 + k + AHEAD)
            for h in range(HG_HEADS + 1):
                for step in range(8):
                    if h >= 1:
                        for l in HALVES[step]:
                            hgx_unit_dve(dve, link, h - 1, l)
                        if step == 0 and h >= 2:
                            hgx_out_dve(dve, link, h - 2)
                    if step % 2 == 0 and 4 * h + step // 2 <= 4 * HG_HEADS:
                        split_lo(dve, s0 + 7 + 4 * h + step // 2 + AHEAD)
            hgx_out_dve(dve, link, HG_HEADS - 1)

        def hgx_act(act):
            phase = "hg_x"
            s0, o0 = start[phase], first_tile[phase]
            act.wait_ge(state_done, HG_HEADS)
            values_act(act, phase, 0, 4, o0, hg_v)
            for h in range(HG_HEADS + 1):
                n = HG_HEADS + h
                if h < HG_HEADS:
                    for part in range(4):
                        k = 8 + 4 * h + part
                        if h >= 2 and part == 0:
                            hgx_out_act(act, h - 2)
                        if part < 2:
                            hg_forget_act(act, s0 + k, o0 + k, n, part)
                        else:
                            act.wait_ge(slab_used, s0 + k + 1)
                            if h >= 2:
                                act.wait_ge(pv_done, 10 * (h - 1))
                                act.wait_ge(lin_gated, h - 1)
                            dst = hg_q if part == 2 else hg_g
                            act.activation(dst[n % 2][:], psum[(o0 + k) % 4][:, 0:T], ACT.Silu).then_inc(freed_a, 1)
                        split_hi(act, s0 + k + AHEAD)
                if h == HG_HEADS:
                    hgx_out_act(act, h - 2)
                    hgx_out_act(act, h - 1)

        def hgx_out_act(act, h):
            act.wait_ge(pv_done, 10 * h + 10)
            act.activation(hg_sq[:], psum[SUMS][:, 0:T], ACT.Square).then_inc(lin_sq, 1)
            act.wait_ge(lin_sum, h + 1)
            act.activation(hg_root[:], psum[TURN][:, 0:T], ACT.Sqrt, bias=eps[:], scale=1.0 / P).then_inc(lin_rms, 1)
            act.wait_ge(lin_gated, h + 1)
            act.activation(hg_o_hi[:, h, :], prod[0][:], ACT.Copy).then_inc(lin_hi, 1)

        def hgx_pool(pool):
            for h in range(HG_HEADS):
                n = HG_HEADS + h
                q, kb, pb, rb = hg_q[n % 2], hg_k[1][n % 2], hg_p[1][n % 2], hg_r[1]
                if h == 0:
                    pool.wait_ge(kt_done, HG_HEADS)
                else:
                    pool.wait_ge(pv_done, 10 * h)
                pool.memset(rb[:], 1.0).then_inc(r_set, 1)
                pool.wait_ge(r_set, n + 1)
                pool.wait_ge(f_ready, 2 * n + 2)
                pool.wait_ge(*freed_by(first_tile["hg_x"] + 8 + 4 * h + 3))
                for l in range(1, LV + 1):
                    if l >= 2:
                        decay_b_step(pool, pb[:], rb[:], STEPS[l - 2])
                        pool.wait_ge(a_done, LV * h + l - 1)
                    if l == LV:
                        pool.wait_ge(a_done, LV * h + LV)
                        pool.tensor_tensor(hg_u[1][:], q[:], pb[:], ALU.mult).then_inc(uw_ready_b, 1)
                    else:
                        u, w = hg_u[l % 2], hg_w[l % 2]
                        pool.tensor_tensor(half(u, l, 0), half(q, l, 0), half(pb, l, 0), ALU.mult)
                        pool.tensor_tensor(half(w, l, 1), half(kb, l, 1), half(rb, l, 1), ALU.mult)\
                            .then_inc(uw_ready_b, 1)
        UG = 17
        DG = 15
        UNITS_G = [(l, c) for l in range(8) for c in range(TT)] + [(8, 0)]

        def gla_in_pe(pe, n, m):
            phase = f"b{n}_gla"
            bank_free(pe, first_tile[phase] + m)
            multiply(pe, start[phase] + m, first_tile[phase] + m, h_hi, h_lo)

        def gla_in_dve(dve, n, m):
            s, o = start[f"b{n}_gla"] + m, first_tile[f"b{n}_gla"] + m
            dve.wait_ge(slab_used, s + 1)
            bank = psum[o % 4][:, 0:T]
            if m == 0:
                ins = dve.tensor_copy(gl_lr[:], bank)
            elif m <= GLA_HEADS:
                ins = dve.tensor_scalar(gl_q[:, m - 1, :], bank, P ** -0.5, None, ALU.mult)
            else:
                ins = dve.tensor_copy(gl_k[:, m - 1 - GLA_HEADS, :], bank)
            ins.then_inc(freed_v, 1)
            split_lo(dve, s + AHEAD)

        def gla_pe(pe, n):
            phase = f"b{n}_gla"
            s0, o0 = start[phase], first_tile[phase]
            pe.wait_ge(*freed_by(o0))
            for h in range(GLA_HEADS):
                w = V("gla_gate")[0:GLA_RANK, (GLA_HEADS * n + h) * P:(GLA_HEADS * n + h + 1) * P]
                mm = pe.matmul(psum[4 + h // 2][:, (h % 2) * T:(h % 2 + 1) * T], w, gl_lr[0:GLA_RANK, :],
                               start=True, stop=True)
            mm.then_inc(z_done, 1)
            values_pe(pe, phase, 9, 4, o0 + 9)
            for o in range(o0 + 13, o0 + 17):
                pe.wait_ge(*freed_by(o))
            for j in range(UG + 1):
                if j < UG:
                    l, c = UNITS_G[j]
                    a = UG * n + j
                    to = 1 if l == 8 else c
                    if l:
                        pe.wait_ge(uw_ready, 10 * HG_HEADS + DG * n + j - 1)
                        pe.wait_ge(w_ready, DG * n + j - 1)
                    else:
                        pe.wait_ge(*freed_by(o0 + 8))
                        pe.wait_ge(z_min, GLA_HEADS * (n + 1))
                    if j >= 2:
                        pe.wait_ge(a_ready, LV * HG_HEADS + a - 1)
                    for h in range(GLA_HEADS):
                        if l == 0:
                            w, u = gl_k[:, h, c * P:(c + 1) * P], gl_q[:, h, c * P:(c + 1) * P]
                        else:
                            w, u = gl_w[j % 2][:, h, :], gl_u[j % 2][:, h, :]
                        mm = pe.matmul(psum[4 + j % 2][:, h * P:(h + 1) * P], w, u, start=True, stop=True)
                    mm.then_inc(a_done, 1)
                if j >= 1:
                    l, c = UNITS_G[j - 1]
                    a = UG * n + j - 1
                    to = 1 if l == 8 else c
                    pe.wait_ge(a_ready, LV * HG_HEADS + a + 1)
                    for f in range(2 * GLA_HEADS):
                        mm = pe.matmul(psum[f // 2][:, (f % 2) * T + to * P:(f % 2) * T + (to + 1) * P],
                                       gl_v[:, c, f * P:(f + 1) * P], gl_a[(j - 1) % 2][:, f // 2, :],
                                       start=j == 1 and f % 2 == 0, stop=j == UG, skip_group_check=True)
                    mm.then_inc(pv_done, 1)
            for h in range(GLA_HEADS):
                v = HG_HEADS + GLA_HEADS * n + h
                pe.wait_ge(lin_sq, v + 1)
                pe.wait_ge(lin_rms, v)
                for d in range(2):
                    mm = pe.matmul(psum[SUMS][:, 0:T], K("ones"), gl_sq[h % 2][:, d * T:(d + 1) * T], start=d == 0,
                                   stop=d == 1)
                mm.then_inc(lin_sum, 1)
            pe.wait_ge(lin_norm, HG_HEADS + 2 * GLA_HEADS * (n + 1))

        def gla_act(act, n):
            phase = f"b{n}_gla"
            s0, o0 = start[phase], first_tile[phase]
            act.wait_ge(z_done, n + 1)
            for h in range(GLA_HEADS):
                act.activation(gl_r[:, h, :], psum[4 + h // 2][:, (h % 2) * T:(h % 2 + 1) * T], ACT.Abs,
                               bias=V("gla_bias")[:, GLA_HEADS * n + h:GLA_HEADS * n + h + 1]).then_inc(z_abs, 1)
            act.wait_ge(z_abs, GLA_HEADS * (n + 1))
            act.activation(gl_r[:], gl_r[:], ACT.Exp, scale=-1.0).then_inc(z_exp, 1)
            act.wait_ge(z_exp, 2 * n + 1)
            act.activation(gl_r[:], gl_r[:], ACT.Ln, bias=1.0).then_inc(z_ln, 1)
            act.wait_ge(z_sub, n + 1)
            act.activation(gl_p[:], gl_p[:], ACT.Exp, scale=1.0 / GLA_TAU).then_inc(z_exp, 1)
            values_act(act, phase, 9, 4, o0 + 9, gl_v)
            for h in range(GLA_HEADS):
                v = HG_HEADS + GLA_HEADS * n + h
                act.wait_ge(pv_done, 10 * HG_HEADS + UG * (n + 1))
                if h >= 2:
                    act.wait_ge(lin_sum, v - 1)
                act.activation(gl_sq[h % 2], psum[h][:], ACT.Square).then_inc(lin_sq, 1)
                if h >= 1:
                    gla_root(act, n, h - 1)
            gla_root(act, n, GLA_HEADS - 1)

        def gla_root(act, n, h):
            v = HG_HEADS + GLA_HEADS * n + h
            act.wait_ge(lin_sum, v + 1)
            if h >= 2:
                act.wait_ge(lin_norm, HG_HEADS + 2 * GLA_HEADS * n + 2 * (h - 1))
            act.activation(gate[h % 2][:], psum[SUMS][:, 0:T], ACT.Sqrt, bias=eps[:], scale=1.0 / (2 * P))\
                .then_inc(lin_rms, 1)

        def gla_dve(dve, link, n):
            phase = f"b{n}_gla"
            s0, o0 = start[phase], first_tile[phase]
            dve.wait_ge(z_done, n + 1)
            dve.wait_ge(z_abs, GLA_HEADS * (n + 1))
            for h in range(GLA_HEADS):
                dve.tensor_scalar(gl_p[:, h, :], psum[4 + h // 2][:, (h % 2) * T:(h % 2 + 1) * T],
                                  V("gla_bias")[:, GLA_HEADS * n + h:GLA_HEADS * n + h + 1], 0.0, ALU.add, ALU.min)\
                    .then_inc(z_min, 1)
            dve.wait_ge(z_min, GLA_HEADS * (n + 1))
            dve.wait_ge(z_ln, n + 1)
            dve.tensor_tensor(gl_p[:], gl_p[:], gl_r[:], ALU.subtract).then_inc(z_sub, 1)
            for k in range(8):
                split_lo(dve, s0 + 9 + k + AHEAD)
            for j in range(UG + 1):
                if j < UG:
                    l, c = UNITS_G[j]
                    a = UG * n + j
                    if j == 0:
                        dve.wait_ge(z_exp, 2 * n + 2)
                        dve.wait_ge(freed_v, freed[o0 + 8][1])
                        link(dve.memset(gl_r[:], 1.0))
                    if l >= 2 and c == 0:
                        dve.wait_ge(w_ready, DG * n + j - 2)
                        decay_f_step(dve, gl_p, gl_r, STEPS[l - 2], heads=True)
                    if l:
                        if j >= 4:
                            dve.wait_ge(a_done, LV * HG_HEADS + a - 1)
                        to = 1 if l == 8 else c
                        dve.tensor_tensor(gl_u[j % 2][:], gl_q[:, :, to * P:(to + 1) * P],
                                          gl_p[:, :, to * P:(to + 1) * P], ALU.mult).then_inc(uw_ready, 1)
                if j >= 1:
                    l, c = UNITS_G[j - 1]
                    a = UG * n + j - 1
                    dve.wait_ge(a_done, LV * HG_HEADS + a + 1)
                    if j >= 3:
                        dve.wait_ge(pv_done, 10 * HG_HEADS + a - 1)
                    at = psum[4 + (j - 1) % 2][:].rearrange("p (h t) -> p h t", t=P)
                    if l == 8:
                        ins = dve.tensor_copy(gl_a[(j - 1) % 2][:], at)
                    else:
                        mask = K("causal")[:, l * P:(l + 1) * P].unsqueeze(1).to_broadcast([P, GLA_HEADS, P])
                        ins = dve.tensor_tensor(gl_a[(j - 1) % 2][:], at, mask, ALU.mult)
                    ins.then_inc(a_ready, 1)
            for h in range(GLA_HEADS):
                v = HG_HEADS + GLA_HEADS * n + h
                dve.wait_ge(lin_rms, v + 1)
                if h:
                    dve.wait_ge(lin_norm, HG_HEADS + 2 * GLA_HEADS * n + 2 * h)
                link(dve.reciprocal(rstd[:], gate[h % 2][:]))
                for d in range(2):
                    f = 2 * h + d
                    g = V("gla_norm")[:, KD * n + f:KD * n + f + 1]
                    dve.scalar_tensor_tensor(ob[:, f, :], psum[h][:, d * T:(d + 1) * T], g, rstd[:], ALU.mult,
                                             ALU.mult).then_inc(lin_norm, 1)

        def gla_pool(pool, n):
            for j in range(TT, UG):
                l, c = UNITS_G[j]
                a = UG * n + j
                pool.wait_ge(uw_ready, 10 * HG_HEADS + DG * n + j - 1)
                if j >= 4:
                    pool.wait_ge(a_done, LV * HG_HEADS + a - 1)
                pool.tensor_tensor(gl_w[j % 2][:], gl_k[:, :, c * P:(c + 1) * P], gl_r[:, :, c * P:(c + 1) * P],
                                   ALU.mult).then_inc(w_ready, 1)

        def r_act(act, n):
            phase = f"b{n}_r"
            s0, o0 = start[phase], first_tile[phase]
            for j in range(KD):
                act.wait_ge(slab_used, s0 + j + 1)
                act.activation(gate[j % 2][:], psum[(o0 + j) % 4][:, 0:T], ACT.Silu).then_inc(mix_sig, 1)
                split_hi(act, s0 + j + AHEAD)
                act.wait_ge(*freed_by(o0 + j))
                act.activation(ob_hi[:, j, :], prod[j % 2][:], ACT.Copy).then_inc(mix_hi, 1)

        def r_dve(dve, link, n):
            phase = f"b{n}_r"
            s0, o0 = start[phase], first_tile[phase]
            for j in range(KD):
                u = 3 * KD * n + j
                dve.wait_ge(mix_sig, u + 1)
                dve.tensor_tensor(prod[j % 2][:], ob[:, j, :], gate[j % 2][:], ALU.mult).then_inc(freed_v, 1)
                split_lo(dve, s0 + j + AHEAD)
                dve.wait_ge(mix_hi, 2 * KD * n + j + 1)
                dve.tensor_tensor(ob_lo[:, j, :], prod[j % 2][:], ob_hi[:, j, :], ALU.subtract).then_inc(mix_ready, 1)

        def merge_pe(pe, n, ot_end):
            phase = f"b{n}_merge"
            s0, o0 = start[phase], first_tile[phase]
            pe.wait_ge(ot_ready, ot_end)
            for j in range(KD):
                for m, (hi, lo, blocks) in enumerate(((h_hi, h_lo, KD), (oa_hi, oa_lo, 4), (h_hi, h_lo, KD),
                                                      (ob_hi, ob_lo, KD))):
                    k = 4 * j + m
                    if j == 0 and m == 3:
                        pe.wait_ge(mix_ready, 2 * KD * n + KD)
                    bank_free(pe, o0 + k)
                    multiply(pe, s0 + k, o0 + k, hi, lo, blocks=blocks)

        def merge_act(act, n):
            phase = f"b{n}_merge"
            s0, o0 = start[phase], first_tile[phase]
            for j in range(KD):
                for m in range(2):
                    k = 4 * j + 2 * m
                    act.wait_ge(slab_used, s0 + k + 1)
                    if k >= 4:
                        act.wait_ge(*freed_by(o0 + k - 3))
                    act.activation(gate[m][:], psum[(o0 + k) % 4][:, 0:T], ACT.Sigmoid).then_inc(mix_sig, 1)
                    split_hi(act, s0 + k + AHEAD)
                    split_hi(act, s0 + k + 1 + AHEAD)
                act.wait_ge(mix_sum, KD * n + j + 1)
                act.activation(mg_hi[:, j, :], conv[j % 2][:], ACT.Copy).then_inc(mix_hi, 1)

        def merge_dve(dve, link, n):
            phase = f"b{n}_merge"
            s0, o0 = start[phase], first_tile[phase]
            for j in range(KD):
                for m in range(2):
                    k = 4 * j + 2 * m
                    dve.wait_ge(mix_sig, 3 * KD * n + KD + 2 * j + m + 1)
                    dve.wait_ge(slab_used, s0 + k + 2)
                    dve.tensor_tensor(prod[m][:], psum[(o0 + k + 1) % 4][:, 0:T], gate[m][:], ALU.mult)\
                        .then_inc(freed_v, 2)
                    split_lo(dve, s0 + k + AHEAD)
                    split_lo(dve, s0 + k + 1 + AHEAD)
                dve.wait_ge(*freed_by(o0 + 4 * j + 3))
                dve.tensor_tensor(conv[j % 2][:], prod[0][:], prod[1][:], ALU.add).then_inc(mix_sum, 1)
                dve.wait_ge(mix_hi, 2 * KD * n + KD + j + 1)
                dve.tensor_tensor(mg_lo[:, j, :], conv[j % 2][:], mg_hi[:, j, :], ALU.subtract).then_inc(mix_ready, 1)

        def att_units(t_set):
            units = []
            for j, pair in enumerate(PAIRS):
                for part, head in enumerate(pair):
                    rows = slice(part * HD, (part + 1) * HD)
                    kv = head // 4
                    keys = slice(0, 2 * T) if t_set == X else slice(T, 2 * T)
                    v = [att_v[:, b, kv * HD:(kv + 1) * HD] for b in range(0 if t_set == X else TT, 2 * TT)]
                    blocks_ = [(att_q[t_set][rows, j, t * P:(t + 1) * P], att_k[rows, j // 4, keys],
                                [(1 - t, f"win{t}")] if t_set == X else [], v) for t in range(TT)]
                    sinks = (V("sink")[:, head:head + 1], nsink[:, head:head + 1])
                    col = slice(j * P + part * HD, j * P + (part + 1) * HD)
                    if t_set == X:
                        for t in range(TT):
                            units.append(([blocks_[t]], *sinks, att_o[:, t, col]))
                    else:
                        units.append((blocks_, *sinks, att_o[:, TT:2 * TT, col]))
            return units

        def swa_units(n):
            units = []
            for j, pair in enumerate(SWA_PAIRS):
                for part, head in enumerate(pair):
                    rows = slice(part * HD, (part + 1) * HD)
                    at = 8 * n + head
                    blocks_ = [(swa_q[rows, j, t * P:(t + 1) * P], swa_q[rows, 4, 0:(t + 1) * P],
                                [(0, "swa_cur")] if t == 0 else [(0, "swa_prev"), (1, "swa_cur")],
                                [swa_v[:, b, part * HD:(part + 1) * HD] for b in range(t + 1)]) for t in range(TT)]
                    units.append((blocks_, V("swa_sink")[:, at:at + 1], nsink[:, 16 + at:17 + at],
                                  swa_o[:, :, j * P + part * HD:j * P + (part + 1) * HD]))
            return units

        ATT = [att_units(X), att_units(C)]
        SWA = [swa_units(0), swa_units(1)]
        EARLY = 2
        U_C = len(ATT[X])
        U_SWA = [U_C + len(ATT[C]), U_C + len(ATT[C]) + len(SWA[0])]

        def att_dst(t):
            return lambda m: att_q[t][:, m, :] if m < KD else att_k[:, m - KD, t * T:(t + 1) * T]

        def swa_dst(m):
            return swa_q[:, m, :]

        def shift(layer, norm, t):
            return lambda k: mod[:, layer, 8 * (3 * norm) + k, t:t + 1]

        def scale(layer, norm, t):
            return lambda k: mod_g[:, layer, norm, t, k:k + 1]

        def branch(layer, norm, t):
            return lambda k: mod[:, layer, 8 * (3 * norm + 2) + k, t:t + 1]

        def gains(name, n):
            return lambda k: V(name)[:, KD * n + k:KD * n + k + 1]

        last = {p: first_tile[p] for p in first_tile}

        block = ctx.enter_context(nc.Block())

        @block.sync
        def _(sp):
            sp.dma_start(vec[:], dram["vec"]).then_inc(params_in, 16)
            for p in range(RAW):
                load(sp, p)
            sp.dma_start(res[X][:], dram["x"]).then_inc(x_in, 16)
            for p in range(RAW, len(panels)):
                load(sp, p)
                if p == 2 * RAW - 1:
                    sp.dma_start(con[:, 0:CON_EARLY], dram["con"][:, 0:CON_EARLY]).then_inc(con_in, 16)
                if p == 3 * RAW:
                    sp.dma_start(con[:, CON_EARLY:], dram["con"][:, CON_EARLY:]).then_inc(con_in, 16)
                    sp.dma_start(res[C][:], dram["ctx"]).then_inc(ctx_in, 16)
            for j in range(KD):
                sp.wait_ge(*freed_by(first_tile["b1_ffn2_down"] + j))
                sp.dma_start(out[:, j, :], res[X][:, j, :]).then_inc(out_done, 16)
            sp.wait_ge(out_done, 16 * KD)

        @block.gpsimd
        def _(pool):
            for t in (X, C):
                norm_pool(pool, t, shift(0, 0, t))
            for n in range(ADA_LATE + 1, ADA_TWO, 2):
                ada_lo(pool, n)
            for t in (X, C):
                norm_pool(pool, 2 + t, shift(0, 1, t))
            norm_pool(pool, 4, shift(1, 0, C))
            hgc_pool(pool)
            norm_pool(pool, 5, shift(1, 0, X))
            hgx_pool(pool)
            norm_pool(pool, 6, shift(1, 1, X))
            for n in range(2):
                norm_pool(pool, 7 + 3 * n, None)
                norm_pool(pool, 8 + 3 * n, None)
                gla_pool(pool, n)
                norm_pool(pool, 9 + 3 * n, None)

        @block.tensor
        def _(pe):
            pe.wait_ge(c_ready, 1)
            for n in range(2 * ADA_FIRST):
                ada_pe(pe, 0, n)
            pe.wait_ge(con_in, 16)
            ada_turn_pe(pe, 0)
            for t in (X, C):
                norm_pe(pe, t)
                phase = "qkv_" + "xc"[t]
                qk_pe(pe, phase, 10, att_dst(t), "swap16" if t == X else None, 10 * t, 0, att_sq, t,
                      with_ada=True)
                values_pe(pe, phase, 10, 1, first_tile[phase] + 10)
                qkv_ada_pe(pe, 12 * t + 10)
                qkv_ada_pe(pe, 12 * t + 11, 4 * t)
            ada_turn_pe(pe, 1)
            for o in range(4):
                pe.wait_ge(*freed_by(first_tile["qkv_c"] + 8 + o))
            att_pe(pe, ATT[X], 0, probs, probs_t, 1, 
                   lambda m: ada_pe(pe, 2, m - 1) if 1 <= m <= 2 * ADA_ATT else None)
            ada_turn_pe(pe, 2)
            turn_pe(pe, att_o[:, 0:TT, :], KD, U_C, 0)
            pe.wait_ge(ot_ready, KD)
            pe.wait_ge(mod_ready, 3)

            def out_tile_pe(m):
                if m % 2 and m < 2 * KD:
                    bank_free(pe, first_tile["attn_out_x"] + m // 2)
                    multiply(pe, start["attn_out_x"] + m // 2, first_tile["attn_out_x"] + m // 2, h_hi, h_lo)

            att_pe(pe, ATT[C], U_C, probs, probs_t, 1, out_tile_pe)
            turn_pe(pe, att_o[:, TT:2 * TT, :], KD, U_SWA[0], KD)
            pe.wait_ge(ot_ready, 2 * KD)
            linear_pe(pe, "attn_out_c", h_hi, h_lo)
            for t in (X, C):
                norm_pe(pe, 2 + t)
                ffn_pe(pe, "ffn0_" + "xc"[t], 2 + t, t)
            norm_pe(pe, 4)
            hgc_pe(pe)
            norm_pe(pe, 5)
            hgx_pe(pe)
            pe.wait_ge(lin_ready, HG_HEADS)
            linear_pe(pe, "hg_out", hg_o_hi, hg_o_lo)
            norm_pe(pe, 6)
            ffn_pe(pe, "ffn1", 6, 2)
            for n in range(2):
                norm_pe(pe, 7 + 3 * n)
                ffn_pe(pe, f"b{n}_ffn1", 7 + 3 * n, 3 + 2 * n)
                norm_pe(pe, 8 + 3 * n)
                phase = f"b{n}_swa"
                qk_pe(pe, phase, 5, swa_dst, "swap32", 20 + 5 * n, 10 + 5 * n, swa_sq, 8 + 3 * n)
                o = first_tile[phase] + 5
                bank_free(pe, o)
                bank_free(pe, o + 1)
                multiply_tokens(pe, start[phase] + 5, o, 0, groups=KD, width=P)
                for m in range(EARLY):
                    gla_in_pe(pe, n, m)
                att_pe(pe, SWA[n], U_SWA[n], swa_p, swa_pt, 2 + n,
                       lambda m: gla_in_pe(pe, n, m + EARLY) if m + EARLY < 9 else None)
                turn_pe(pe, swa_o, 4, U_SWA[n] + len(SWA[n]), 2 * KD + 4 * n)
                gla_pe(pe, n)
                linear_pe(pe, f"b{n}_r", h_hi, h_lo)
                merge_pe(pe, n, 2 * KD + 4 * (n + 1))
                pe.wait_ge(mix_ready, 2 * KD * (n + 1))
                linear_pe(pe, f"b{n}_out", mg_hi, mg_lo)
                norm_pe(pe, 9 + 3 * n)
                ffn_pe(pe, f"b{n}_ffn2", 9 + 3 * n, 4 + 2 * n)

        @block.scalar
        def _(act):
            act.wait_ge(params_in, 16)
            act.wait_ge(c_clear, 1)
            act.activation(c_act[:], c_in, ACT.Silu).then_inc(c_silu, 1)
            act.wait_ge(c_silu, 1)
            act.activation(c_wide[:, :, WIDE:WIDE + 2], c_act[:], ACT.Copy).then_inc(c_hi, 1)
            act.wait_ge(lb_top, 1)
            act.activation(lb[:, 0:2, :], lb[:, 0:2, :], ACT.Exp).then_inc(lb_exp, 1)
            for k in range(AHEAD):
                split_hi(act, k)
            for n in range(ADA_LATE):
                ada_act(act, n)
            def squares(n, t, base=None):
                return lambda k: norm_square(act, n, t, k, None if base is None else first_tile[base])

            def all_squares(n, t, base=None):
                for k in range(KD):
                    squares(n, t, base)(k)

            all_squares(0, X)
            for t in (X, C):
                phase = "qkv_" + "xc"[t]
                norm_act(act, t, shift(0, 0, t), start[phase], mod_parts=1)
                if t == X:
                    all_squares(1, C)
                qk_act(act, phase, 10, 10 * t, att_sq, att_root, with_ada=True)
                for k in (10, 11):
                    qkv_ada_act(act, 12 * t + k)
                    split_hi(act, start[phase] + k + AHEAD)
            qkv_ada_act(act, ADA_QKV)
            att_act(act, ATT[X], 0, probs, probs_t, lambda m: ada_act(act, ADA_TWO + m) if m < 2 * ADA_ATT else None)
            turn_act(act, h_hi, KD, 0)
            att_act(act, ATT[C], U_C, probs, probs_t,
                    lambda m: split_hi(act, start["attn_out_x"] + m // 2 + AHEAD) if m % 2 and m < 2 * KD else None)
            turn_act(act, h_hi, KD, KD)
            residual_act(act, "attn_out_c", square=squares(2, X, "attn_out_x"), lag=0)
            for t in (X, C):
                phase = "ffn0_" + "xc"[t]
                norm_act(act, 2 + t, shift(0, 1, t), start[phase])
                ffn_up(act, ffn_up_act, phase, t, 0)
                if t == X:
                    residual_act(act, phase + "_down", 2, squares(3, C, "attn_out_c"), lag=0)
                else:
                    residual_act(act, phase + "_down", 2, squares(4, C, "ffn0_c_down"))
            norm_act(act, 4, shift(1, 0, C), start["hg_c"])
            hgc_act(act, squares(5, X, "ffn0_x_down"))
            norm_act(act, 5, shift(1, 0, X), start["hg_x"])
            hgx_act(act)
            residual_act(act, "hg_out", 1, squares(6, X, "hg_out"))
            norm_act(act, 6, shift(1, 1, X), start["ffn1"])
            ffn_up(act, ffn_up_act, "ffn1", 2, 1)
            residual_act(act, "ffn1_down", 2, squares(7, X, "ffn1_down"))
            for n in range(2):
                norm_act(act, 7 + 3 * n, None, start[f"b{n}_ffn1"])
                ffn_up(act, ffn_up_act, f"b{n}_ffn1", 3 + 2 * n, None)
                residual_act(act, f"b{n}_ffn1_down", 2, squares(8 + 3 * n, X, f"b{n}_ffn1_down"))
                norm_act(act, 8 + 3 * n, None, start[f"b{n}_swa"])
                qk_act(act, f"b{n}_swa", 5, 20 + 5 * n, swa_sq, swa_root)
                split_hi(act, start[f"b{n}_swa"] + 5 + AHEAD)
                for m in range(EARLY):
                    split_hi(act, start[f"b{n}_gla"] + m + AHEAD)
                att_act(act, SWA[n], U_SWA[n], swa_p, swa_pt,
                        lambda m: split_hi(act, start[f"b{n}_gla"] + m + EARLY + AHEAD) if m + EARLY < 9 else None)
                turn_act(act, oa_hi, 4, 2 * KD + 4 * n)
                gla_act(act, n)
                r_act(act, n)
                merge_act(act, n)
                residual_act(act, f"b{n}_out", 1, squares(9 + 3 * n, X, f"b{n}_out"))
                norm_act(act, 9 + 3 * n, None, start[f"b{n}_ffn2"])
                ffn_up(act, ffn_up_act, f"b{n}_ffn2", 4 + 2 * n, None)
                residual_act(act, f"b{n}_ffn2_down", 2, squares(10, X, "b0_ffn2_down") if n == 0 else None)

        @block.vector
        def _(dve):
            steps = [0]

            def link(ins):
                steps[0] += 1
                ins.then_inc(v_step, 1)
                dve.wait_ge(v_step, steps[0])

            dve.memset(c_wide[:].bitcast(F32), 0.0).then_inc(c_clear, 1)
            dve.memset(eps[:], EPS).then_inc(eps_set, 1)
            dve.wait_ge(params_in, 16)
            dve.wait_ge(c_hi, 1)
            dve.tensor_tensor(c_wide[:, :, WIDE + 2:WIDE + 4], c_act[:], c_wide[:, :, WIDE:WIDE + 2], ALU.subtract)\
                .then_inc(c_ready, 1)
            nsink_dve(dve, link)
            both = V("lb", "p (l k) -> p l k", dict(l=2))
            link(dve.tensor_tensor(lb[:, 2, :], both[:, 0, :], both[:, 1, :], ALU.max))
            for n in range(2):
                ins = dve.tensor_tensor(lb[:, n, :], both[:, n, :], lb[:, 2, :], ALU.subtract)
            ins.then_inc(lb_top, 1)
            dve.wait_ge(lb_exp, 1)
            link(dve.tensor_tensor(lb[:, 2, :], lb[:, 0, :], lb[:, 1, :], ALU.add))
            link(dve.reciprocal(lb[:, 3, :], lb[:, 2, :]))
            dve.tensor_tensor(lb[:, 0, :], lb[:, 0, :], lb[:, 3, :], ALU.mult)
            link(dve.tensor_tensor(lb[:, 1, :], lb[:, 1, :], lb[:, 3, :], ALU.mult))
            link(dve.tensor_tensor(lb[:, 2, :], lb[:, 0, :], lb[:, 1, :], ALU.add))
            link(dve.tensor_tensor(lb[:, 2, :], lb[:, 2, :], lb[:, 0, :], ALU.subtract))
            link(dve.tensor_scalar(lb[:, 3, :], lb[:, 2, :], -1.0, 1.0, ALU.mult, ALU.add))
            for k in range(AHEAD):
                split_lo(dve, k)
            for n in range(ADA_LATE):
                ada_lo(dve, n)
            dve.wait_ge(con_in, 16)
            ada_dve(dve, link, 0)
            for t in (X, C):
                phase = "qkv_" + "xc"[t]
                norm_dve(dve, link, t, t, scale(0, 0, t), shift(0, 0, t))
                rot = ("cos_ax", "sin_ax") if t == X else (None, None)
                qk_dve(dve, link, phase, 10, att_dst(t), lambda m: V("q_gain") if m < KD else V("k_gain"), *rot,
                       10 * t, 0, att_root, with_ada=True)
                for k in (10, 11):
                    qkv_ada_dve(dve, 12 * t + k)
                dve.wait_ge(slab_used, start[phase] + 12)
                for j in range(TT):
                    ins = dve.tensor_copy(att_v[:, TT * t + j, :], psum[(first_tile[phase] + 10 + j) % 4][:, 0:T])
                    ins.then_inc(freed_v, 1)
                for k in (10, 11):
                    split_lo(dve, start[phase] + k + AHEAD)
            qkv_ada_dve(dve, ADA_QKV)
            ada_dve(dve, link, 1)
            dve.wait_ge(freed_v, freed[first_tile["qkv_c"] + 11][1])
            dve.memset(top[:], 0.0).then_inc(mixer_in, 1)
            dve.wait_ge(mixer_in, 1)
            att_dve(dve, link, ATT[X], 0, lambda m: ada_lo(dve, ADA_TWO + m) if m < 2 * ADA_ATT else None)
            ada_dve(dve, link, 2)
            turn_dve(dve, h_hi, h_lo, KD, 0)

            def out_tile_dve(m):
                if m % 2 and m < 2 * KD:
                    j = m // 2
                    residual_tile_dve(dve, start["attn_out_x"] + j, first_tile["attn_out_x"] + j, res[X][:, j, :],
                                      branch(0, 0, X)(j))

            att_dve(dve, link, ATT[C], U_C, out_tile_dve)
            turn_dve(dve, h_hi, h_lo, KD, KD)
            residual_dve(dve, "attn_out_c", C, branch(0, 0, C))
            for t in (X, C):
                phase = "ffn0_" + "xc"[t]
                norm_dve(dve, link, 2 + t, t, scale(0, 1, t), shift(0, 1, t))
                ffn_up(dve, ffn_up_dve, phase, t, 0)
                residual_dve(dve, phase + "_down", t, branch(0, 1, t), halves=2)
            norm_dve(dve, link, 4, C, scale(1, 0, C), shift(1, 0, C))
            hgc_dve(dve, link)
            norm_dve(dve, link, 5, X, scale(1, 0, X), shift(1, 0, X))
            hgx_dve(dve, link)
            residual_dve(dve, "hg_out", X, branch(1, 0, X))
            norm_dve(dve, link, 6, X, scale(1, 1, X), shift(1, 1, X))
            ffn_up(dve, ffn_up_dve, "ffn1", 2, 1)
            residual_dve(dve, "ffn1_down", X, branch(1, 1, X), halves=2)
            for n in range(2):
                norm_dve(dve, link, 7 + 3 * n, X, gains("ffn1_norm", n), None)
                ffn_up(dve, ffn_up_dve, f"b{n}_ffn1", 3 + 2 * n, None)
                residual_dve(dve, f"b{n}_ffn1_down", X, lambda k: 0.5, halves=2)
                norm_dve(dve, link, 8 + 3 * n, X, gains("mix_norm", n), None)
                phase = f"b{n}_swa"
                qk_dve(dve, link, phase, 5, swa_dst,
                       lambda m: V("swa_q")[:, n:n + 1] if m < 4 else V("swa_k")[:, n:n + 1], "cos_1d", "sin_1d",
                       20 + 5 * n, 10 + 5 * n, swa_root)
                dve.wait_ge(slab_used, start[phase] + 6)
                for j in range(TT):
                    dve.tensor_copy(swa_v[:, j, :], psum[(first_tile[phase] + 5 + j) % 4][:, 0:P]).then_inc(freed_v, 1)
                split_lo(dve, start[phase] + 5 + AHEAD)
                dve.wait_ge(freed_v, freed[first_tile[phase] + 6][1])
                dve.memset(top[:], 0.0).then_inc(mixer_in, 1)
                dve.wait_ge(mixer_in, 2 + n)
                for m in range(EARLY):
                    gla_in_dve(dve, n, m)
                att_dve(dve, link, SWA[n], U_SWA[n], lambda m: gla_in_dve(dve, n, m + EARLY) if m + EARLY < 9 else None)
                turn_dve(dve, oa_hi, oa_lo, 4, 2 * KD + 4 * n)
                gla_dve(dve, link, n)
                r_dve(dve, link, n)
                merge_dve(dve, link, n)
                residual_dve(dve, f"b{n}_out", X, lambda k: 1.0)
                norm_dve(dve, link, 9 + 3 * n, X, gains("ffn2_norm", n), None)
                ffn_up(dve, ffn_up_dve, f"b{n}_ffn2", 4 + 2 * n, None)
                residual_dve(dve, f"b{n}_ffn2_down", X, lambda k: 0.5, halves=2)


def kernel(**inputs):
    import numpy as _np
    import concourse.bacc as _bacc
    from concourse import mybir as _mybir
    from concourse.bass_utils import run_bass_kernel_spmd as _run

    nc = _bacc.Bacc("TRN2", target_bir_lowering=False, num_devices=1)
    host = arrays({k: _np.asarray(v) for k, v in inputs.items()})
    sent, dram = {}, {}
    for name, a in host.items():
        sent[f"in_{name}"] = a
        dram[name] = nc.dram_tensor(f"in_{name}", a.shape, _mybir.dt.from_np(a.dtype), kind="ExternalInput").ap()
    out = nc.dram_tensor("out", (P, KD, T), F32, kind="ExternalOutput").ap()
    build(nc, dram, out)
    r = _run(nc, [sent], core_ids=[0])
    got = r.results[0]["out"]
    return _np.ascontiguousarray(got.transpose(1, 0, 2).reshape(D, T).T)[None]
```
